# Optimizing a Trainium2 kernel written in Bass

```python
import math
import jax, jax.numpy as jnp
from jax import lax
import numpy as np

D_MODEL = 1024
BATCH = 1
SEQ = 256
DEPTH = 2

CHUNK = 64
N_MEM = 256
EPS = 1e-6
MASK_VALUE = -1e30
D_MIX = D_MODEL
HG_HEADS = 4
HG_DIM = D_MIX // 4 // HG_HEADS
D_A = HG_HEADS * HG_DIM
D_B = D_MIX // 4
CONV_W = 3
CONV_GROUPS = 4
D_C = D_MIX - D_A - D_B
MLA_HEADS = 8
MLA_V = D_C // MLA_HEADS
MLA_NOPE = 64
MLA_ROPE = 32
Q_LORA = D_MODEL // 4
KV_LORA = D_MODEL // 8
ROPE_THETA = 10000.0
Q_BLOCK = 128
SPLIT_SIZES = (D_A, D_A, D_A, D_A, D_B, D_B, D_B, Q_LORA, KV_LORA, MLA_ROPE)
D_IN = 4 * D_A + 3 * D_B + Q_LORA + KV_LORA + MLA_ROPE
XA_HEADS = 4
XA_DIM = D_MODEL // XA_HEADS
N_GROUPS = 4
EXPERTS_PER_GROUP = 8
N_EXPERTS = N_GROUPS * EXPERTS_PER_GROUP
TOP_K = 2
D_EXPERT = D_MODEL // 4

kernel_name = 'hybrid_chunk_causal_block'

def rms_norm(x, g):
    xf = x.astype(jnp.float32)
    y = xf * lax.rsqrt(jnp.mean(xf * xf, axis=-1, keepdims=True) + EPS)
    return (y * g.astype(jnp.float32)).astype(x.dtype)

def group_rms_norm(x, g, groups):
    shp = x.shape
    xg = x.reshape(*shp[:-1], groups, shp[-1] // groups)
    return rms_norm(xg, g.reshape(groups, shp[-1] // groups)).reshape(shp)

def rope_tables(positions):
    half = MLA_ROPE // 2
    inv_freq = ROPE_THETA ** (-jnp.arange(half, dtype=jnp.float32) * 2.0 / MLA_ROPE)
    ang = positions.astype(jnp.float32)[..., None] * inv_freq
    return jnp.cos(ang), jnp.sin(ang)

def rotary(x, cos, sin):
    if x.ndim == 4:
        cos, sin = cos[:, :, None, :], sin[:, :, None, :]
    half = MLA_ROPE // 2
    xf = x.astype(jnp.float32)
    x1, x2 = xf[..., :half], xf[..., half:]
    return jnp.concatenate([x1 * cos - x2 * sin, x2 * cos + x1 * sin], axis=-1).astype(x.dtype)

def hgrn2_mixer(q, f_raw, i, g, lb, norm_g):
    B_, S_, _ = q.shape
    n = S_ // CHUNK
    lbf = lb.astype(jnp.float32)
    f = lbf + (1.0 - lbf) * jax.nn.sigmoid(f_raw.astype(jnp.float32))
    f = jnp.clip(f, 1e-6, 1.0)
    log_f = jnp.log(f)
    k = 1.0 - f
    q_act = jax.nn.silu(q.astype(jnp.float32))

    def heads(t):
        return t.astype(jnp.float32).reshape(B_, n, CHUNK, HG_HEADS, HG_DIM).transpose(1, 0, 3, 2, 4)

    qc, kc, vc = heads(q_act), heads(k), heads(i)
    bc = jnp.cumsum(heads(log_f), axis=3)
    causal = jnp.tril(jnp.ones((CHUNK, CHUNK), dtype=bool))[:, :, None]

    def step(state, xs):
        qb, kb, vb, bb = xs
        o_inter = jnp.einsum('bhld,bhdv->bhlv', qb * jnp.exp(bb), state)
        diff = bb[:, :, :, None, :] - bb[:, :, None, :, :]
        decay = jnp.where(causal, jnp.exp(jnp.minimum(diff, 0.0)), 0.0)
        scores = jnp.einsum('bhtd,bhsd,bhtsd->bhts', qb, kb, decay)
        o = o_inter + jnp.einsum('bhts,bhsv->bhtv', scores, vb)
        b_last = bb[:, :, -1:, :]
        state = jnp.exp(b_last[:, :, 0, :])[..., None] * state + jnp.einsum(
            'bhsd,bhsv->bhdv', kb * jnp.exp(b_last - bb), vb)
        return state, o

    s0 = jnp.zeros((B_, HG_HEADS, HG_DIM, HG_DIM), jnp.float32)
    _, o = lax.scan(step, s0, (qc, kc, vc, bc))
    o = o.transpose(1, 0, 3, 2, 4).reshape(B_, S_, HG_HEADS, HG_DIM)
    gate = jax.nn.silu(g.astype(jnp.float32)).reshape(B_, S_, HG_HEADS, HG_DIM)
    o = rms_norm(o, norm_g) * gate
    return o.reshape(B_, S_, D_A).astype(q.dtype)

def short_conv_mixer(b_gate, c_gate, h, w_conv, norm_g):
    u = c_gate * h
    y = lax.conv_general_dilated(u, w_conv[:, None, :].astype(u.dtype), window_strides=(1,),
                                 padding=[(CONV_W - 1, 0)], dimension_numbers=('NWC', 'WIO', 'NWC'),
                                 feature_group_count=D_B)
    return group_rms_norm(b_gate * y, norm_g, CONV_GROUPS)

def mla_mixer(c_q, c_kv, k_pe, cos, sin, q_norm, w_uq, kv_norm, w_ukv, out_norm):
    B_, S_, _ = c_q.shape
    q = (rms_norm(c_q, q_norm) @ w_uq).reshape(B_, S_, MLA_HEADS, MLA_NOPE + MLA_ROPE)
    q_nope, q_pe = q[..., :MLA_NOPE], rotary(q[..., MLA_NOPE:], cos, sin)
    kv = (rms_norm(c_kv, kv_norm) @ w_ukv).reshape(B_, S_, MLA_HEADS, MLA_NOPE + MLA_V)
    k_nope, v = kv[..., :MLA_NOPE], kv[..., MLA_NOPE:]
    k_rot = rotary(k_pe, cos, sin)
    scale = (MLA_NOPE + MLA_ROPE) ** -0.5
    key_chunk = jnp.arange(S_) // CHUNK
    nb = S_ // Q_BLOCK
    qn_b = q_nope.reshape(B_, nb, Q_BLOCK, MLA_HEADS, MLA_NOPE).transpose(1, 0, 2, 3, 4)
    qp_b = q_pe.reshape(B_, nb, Q_BLOCK, MLA_HEADS, MLA_ROPE).transpose(1, 0, 2, 3, 4)

    def block(args):
        qn, qp, blk = args
        s = (jnp.einsum('bqhd,bkhd->bhqk', qn, k_nope)
             + jnp.einsum('bqhr,bkr->bhqk', qp, k_rot)).astype(jnp.float32) * scale
        q_chunk = (blk * Q_BLOCK + jnp.arange(Q_BLOCK)) // CHUNK
        mask = key_chunk[None, :] <= q_chunk[:, None]
        s = jnp.where(mask, s, MASK_VALUE)
        p = jax.nn.softmax(s, axis=-1).astype(v.dtype)
        return jnp.einsum('bhqk,bkhv->bqhv', p, v)

    o = lax.map(block, (qn_b, qp_b, jnp.arange(nb)))
    o = o.transpose(1, 0, 2, 3, 4).reshape(B_, S_, D_C)
    return group_rms_norm(o, out_norm, MLA_HEADS)

def cross_attention(h, m, wq, wk, wv, wo):
    B_, S_, _ = h.shape
    q = (h @ wq).reshape(B_, S_, XA_HEADS, XA_DIM)
    k = (m @ wk).reshape(B_, m.shape[1], XA_HEADS, XA_DIM)
    v = (m @ wv).reshape(B_, m.shape[1], XA_HEADS, XA_DIM)
    s = jnp.einsum('bqhd,bkhd->bhqk', q, k).astype(jnp.float32) * (XA_DIM ** -0.5)
    p = jax.nn.softmax(s, axis=-1).astype(v.dtype)
    o = jnp.einsum('bhqk,bkhd->bqhd', p, v).reshape(B_, S_, D_MODEL)
    return o @ wo

def hier_moe(h, wg, bg, we, be, w_gate, w_up, w_down):
    B_, S_, D = h.shape
    t = h.reshape(B_ * S_, D)
    grp_prob = jax.nn.softmax((t @ wg).astype(jnp.float32) + bg.astype(jnp.float32), axis=-1)
    p_g, g_idx = lax.top_k(grp_prob, 1)
    exp_logits = jnp.einsum('td,gde->tge', t, we).astype(jnp.float32) + be.astype(jnp.float32)
    sel_logits = jnp.einsum('tg,tge->te', jax.nn.one_hot(g_idx[:, 0], N_GROUPS, dtype=jnp.float32), exp_logits)
    w_top, e_top = lax.top_k(jax.nn.softmax(sel_logits, axis=-1), TOP_K)
    w_top = w_top / jnp.sum(w_top, axis=-1, keepdims=True) * p_g
    expert_ids = g_idx * EXPERTS_PER_GROUP + e_top
    combine = jnp.einsum('tk,tke->te', w_top, jax.nn.one_hot(expert_ids, N_EXPERTS, dtype=jnp.float32))
    y = jnp.zeros((B_ * S_, D), jnp.float32)
    for e in range(N_EXPERTS):
        hid = jax.nn.silu(t @ w_gate[e]) * (t @ w_up[e])
        y = y + combine[:, e:e + 1] * (hid @ w_down[e]).astype(jnp.float32)
    return y.reshape(B_, S_, D).astype(h.dtype)

def setup_inputs(seed: int = 0) -> dict:
    key = jax.random.key(seed)
    ks = jax.random.split(key, 32)

    def nrm(k, shape, scale):
        return jax.random.normal(k, shape, jnp.float32) * scale

    def gain(k, shape):
        return 1.0 + 0.02 * jax.random.normal(k, shape, jnp.float32)

    L, D = DEPTH, D_MODEL
    positions = (jnp.arange(SEQ, dtype=jnp.int32)[None, :]
                 + jax.random.randint(ks[2], (BATCH, 1), 0, 64, dtype=jnp.int32) * CHUNK)
    return {
        'x': nrm(ks[0], (BATCH, SEQ, D), 1.0),
        'mem': nrm(ks[1], (BATCH, N_MEM, D), 1.0),
        'positions': positions,
        'norm_mix': gain(ks[3], (L, D)),
        'w_in': nrm(ks[4], (L, D, D_IN), D ** -0.5),
        'hgrn_lower_bounds': nrm(ks[5], (L, D_A), 1.0),
        'hgrn_norm': gain(ks[6], (L, HG_DIM)),
        'conv_w': nrm(ks[7], (L, CONV_W, D_B), CONV_W ** -0.5),
        'conv_norm': gain(ks[8], (L, D_B)),
        'mla_q_norm': gain(ks[9], (L, Q_LORA)),
        'mla_w_uq': nrm(ks[10], (L, Q_LORA, MLA_HEADS * (MLA_NOPE + MLA_ROPE)), Q_LORA ** -0.5),
        'mla_kv_norm': gain(ks[11], (L, KV_LORA)),
        'mla_w_ukv': nrm(ks[12], (L, KV_LORA, MLA_HEADS * (MLA_NOPE + MLA_V)), KV_LORA ** -0.5),
        'mla_out_norm': gain(ks[13], (L, D_C)),
        'w_out': nrm(ks[14], (L, D_MIX, D), D_MIX ** -0.5),
        'norm_cross': gain(ks[15], (L, D)),
        'norm_mem': gain(ks[16], (L, D)),
        'xa_wq': nrm(ks[17], (L, D, D), D ** -0.5),
        'xa_wk': nrm(ks[18], (L, D, D), D ** -0.5),
        'xa_wv': nrm(ks[19], (L, D, D), D ** -0.5),
        'xa_wo': nrm(ks[20], (L, D, D), D ** -0.5),
        'norm_ffn': gain(ks[21], (L, D)),
        'router_group_w': nrm(ks[22], (L, D, N_GROUPS), D ** -0.5),
        'router_group_b': nrm(ks[23], (L, N_GROUPS), 0.01),
        'router_expert_w': nrm(ks[24], (L, N_GROUPS, D, EXPERTS_PER_GROUP), D ** -0.5),
        'router_expert_b': nrm(ks[25], (L, N_GROUPS, EXPERTS_PER_GROUP), 0.01),
        'expert_w_gate': nrm(ks[26], (L, N_EXPERTS, D, D_EXPERT), D ** -0.5),
        'expert_w_up': nrm(ks[27], (L, N_EXPERTS, D, D_EXPERT), D ** -0.5),
        'expert_w_down': nrm(ks[28], (L, N_EXPERTS, D_EXPERT, D), D_EXPERT ** -0.5),
        'final_norm': gain(ks[29], (D,)),
    }

def reference(x, mem, positions, norm_mix, w_in, hgrn_lower_bounds, hgrn_norm, conv_w, conv_norm,
              mla_q_norm, mla_w_uq, mla_kv_norm, mla_w_ukv, mla_out_norm, w_out,
              norm_cross, norm_mem, xa_wq, xa_wk, xa_wv, xa_wo,
              norm_ffn, router_group_w, router_group_b, router_expert_w, router_expert_b,
              expert_w_gate, expert_w_up, expert_w_down, final_norm):
    lb_soft = jax.nn.softmax(hgrn_lower_bounds.astype(jnp.float32), axis=0)
    lbs = jnp.cumsum(lb_soft, axis=0) - lb_soft[0]
    cos, sin = rope_tables(positions)
    split_at = [int(s) for s in np.cumsum(SPLIT_SIZES)[:-1]]
    h = x
    for l in range(DEPTH):
        u = rms_norm(h, norm_mix[l])
        proj = u @ w_in[l]
        q_a, f_a, i_a, g_a, b_b, c_b, h_b, c_q, c_kv, k_pe = jnp.split(proj, split_at, axis=-1)
        o_a = hgrn2_mixer(q_a, f_a, i_a, g_a, lbs[l], hgrn_norm[l])
        o_b = short_conv_mixer(b_b, c_b, h_b, conv_w[l], conv_norm[l])
        o_c = mla_mixer(c_q, c_kv, k_pe, cos, sin, mla_q_norm[l], mla_w_uq[l],
                        mla_kv_norm[l], mla_w_ukv[l], mla_out_norm[l])
        mixed = jnp.concatenate([o_a.astype(u.dtype), o_b.astype(u.dtype), o_c.astype(u.dtype)], axis=-1)
        h = h + mixed @ w_out[l]
        h = h + cross_attention(rms_norm(h, norm_cross[l]), rms_norm(mem, norm_mem[l]),
                                xa_wq[l], xa_wk[l], xa_wv[l], xa_wo[l])
        h = h + hier_moe(rms_norm(h, norm_ffn[l]), router_group_w[l], router_group_b[l],
                         router_expert_w[l], router_expert_b[l],
                         expert_w_gate[l], expert_w_up[l], expert_w_down[l])
    return rms_norm(h, final_norm)


_drawn_inputs = setup_inputs


def setup_inputs(seed=0):
    import zlib

    import numpy as np

    out = dict(_drawn_inputs(seed))
    spreads = {}
    factors = {'hgrn_norm': 2.736,
     'norm_cross': 8.0,
     'norm_mem': 5.24,
     'router_expert_b': 2.713,
     'final_norm': 8.51,
     'router_group_b': 4.59}
    for name, (base, spread) in spreads.items():
        noise = np.random.default_rng([zlib.crc32(name.encode()), seed]).standard_normal(out[name].shape)
        drawn = base * np.exp(spread * noise) if base else spread * noise
        out[name] = __import__('jax').numpy.asarray(drawn.astype(out[name].dtype))
    for name, factor in factors.items():
        out[name] = (out[name] * factor).astype(out[name].dtype)
    return out
```

```python
from contextlib import ExitStack

import numpy as np

import concourse.bass as bass
from concourse import mybir

F32 = mybir.dt.float32
I32 = mybir.dt.int32
U8 = mybir.dt.uint8
ALU = mybir.AluOpType
ACT = mybir.ActivationFunctionType
AX = mybir.AxisListType

P = 128
L = 2
S = 256
D = 1024
T = S // P
KC = D // P
CHUNK = 64
EPS = 1e-6
DIN = 2208
HH, HD = 4, 64
MH, NOPE, ROPE, MV = 8, 64, 32, 64
QK = NOPE + ROPE
XH, XD = 4, 256
NG, EG = 4, 8
NE = NG * EG
FE = 256
SLOTS = 32
QUAD = 4
RING = 8
UNIT = 4096
LEVELS = 5
UNIT_DMAS = 2
LOADED = 16 * UNIT_DMAS
MIX_UNITS, CROSS_UNITS = 8, 8
FIXED_UNITS = MIX_UNITS + CROSS_UNITS
QUADS_PER_STEP = 4
UNITS_PER_QUAD = 6
STEP_UNITS = QUADS_PER_STEP * UNITS_PER_QUAD
MOE_STEPS = NE // QUAD // QUADS_PER_STEP

TABLES = {}
_at = 0
for _name, _w in [("ident", P), ("ones", P), ("blk64", P), ("before", P), ("restart", S),
                  ("iota32", SLOTS), ("iota8", 8), ("thresholds", 8), ("chunkmask", 1), ("invfreq", 1),
                  ("sinsign", 1), ("eps", 1)]:
    TABLES[_name] = (_at, _w)
    _at += _w
TABLE_W = _at


def shape_tables():
    t = np.zeros((P, TABLE_W), np.float32)
    i = np.arange(P)

    def put(name, value):
        a, w = TABLES[name]
        t[:, a:a + w] = value

    put("ident", np.eye(P))
    put("ones", 1.0)
    put("blk64", (i[:, None] // 64 == i[None] // 64))
    put("before", i[:, None] < i[None])
    put("restart", (np.arange(S) % CHUNK != 0)[None])
    put("iota32", np.arange(SLOTS)[None])
    put("iota8", np.arange(8)[None])
    put("thresholds", SLOTS * np.arange(8)[None])
    put("chunkmask", np.where(i < CHUNK, -1e30, 0.0)[:, None])
    half = ROPE // 2
    freq = np.float32(10000.0) ** (-np.arange(half, dtype=np.float32) * np.float32(2.0) / np.float32(ROPE))
    put("invfreq", freq[i % half][:, None])
    put("sinsign", np.where(i % ROPE < half, -1.0, 1.0)[:, None])
    put("eps", EPS)
    m = np.zeros((P, LEVELS, P), np.float32)
    s, q = i[:, None], i[None]
    m[:, 0] = (s // 4 == q // 4) & (s <= q)
    for lv in range(1, LEVELS):
        b = 4 << lv
        m[:, lv] = (s // b == q // b) & (s % b < b // 2) & (q % b >= b // 2)
    return t, m.reshape(P, LEVELS * P)


JOBS = []
for _n in range(4):
    JOBS.append((f"mix_xt{_n}", "A"))
JOBS += [("f", "A"), ("q", "V"), ("i", "A"), ("g", "V"), ("lv0e", "V"), ("lv0o", "V"),
         ("b", "A"), ("c", "A"), ("lv1e", "V"), ("lv1o", "V"), ("hc", "V"), ("lv2e", "V"), ("lv2o", "V"),
         ("cq", "A"), ("lv3e", "V"), ("lv3o", "V"), ("kv", "A"), ("kvs", "V"), ("lv4e", "V"), ("lv4o", "V"),
         ("latss", "A"), ("ktok", "A"), ("u0", "V"), ("u1", "V"), ("convss", "A"),
         ("o_in", "A"), ("o_st", "V"), ("hgss", "A")]
JOBS += [(f"mq{n}", "A") for n in range(4)] + [(f"mqs{n}", "V") for n in range(4)]
JOBS += [(f"mk{n}", "A") for n in range(4)] + [("mv0", "A"), ("mv1", "A")]
JOBS += [(f"ms{n}", "V") for n in range(6)] + [(f"mt{n}", "A") for n in range(6)]
JOBS += [("mo0", "A"), ("mo1", "A"), ("mss0", "A"), ("mss1", "A")] + [(f"out{n}", "V") for n in range(4)]
JOBS += [(f"cross_xt{n}", "A") for n in range(4)] + [(f"xq{n}", "A") for n in range(4)]
JOBS += [(f"mem_xt{n}", "A") for n in range(4)] + [(f"xk{n}", "A") for n in range(4)]
JOBS += [(f"xv{n}", "V") for n in range(4)] + [(f"xs{n}", "A") for n in range(4)]
JOBS += [(f"xt{n}", "A") for n in range(4)] + [(f"xo{n}", "V") for n in range(4)]
JOBS += [(f"xout{n}", "V") for n in range(4)]
JOBS += [(f"ffn_xt{n}", "A") for n in range(4)] + [("router", "V"), ("places", "V")]
INDEX = {name: n for n, (name, _) in enumerate(JOBS)}


def emptied(name):
    n = INDEX[name]
    return sum(c == JOBS[n][1] for _, c in JOBS[:n + 1])


def hybrid_trunk(nc, tables, level_masks, a, out):
    with ExitStack() as ctx:
        def sb(name, shape, dt=F32, stack=ctx):
            return stack.enter_context(nc.sbuf_tensor(name, shape, dt))

        def sem(name):
            return ctx.enter_context(nc.semaphore(name))

        ring = [sb(f"ring{n}", [P, UNIT]) for n in range(RING)]
        h = sb("h", [P, T, D])
        uT = sb("uT", [P, KC, S])
        tab = sb("tab", [P, TABLE_W])
        lvmask = sb("lvmask", [P, LEVELS, P], U8)
        states = sb("states", [P, 3, 2, P])
        gains = sb("gains", [P, 4, KC])
        g_hgrn = sb("g_hgrn", [P, 1])
        w_conv = sb("w_conv", [P, 3, 2])
        g_conv = sb("g_conv", [P, 2])
        g_lat = sb("g_lat", [P, 3])
        g_out = sb("g_out", [P, 4])
        lb_raw = sb("lb_raw", [P, L, 2])
        lb_tab = sb("lb_tab", [P, 2, L, 2])
        lb = sb("lb", [P, 2, 2])
        lb_tmp = sb("lb_tmp", [P, 4, 2])
        w_rout = sb("w_rout", [P, KC, NG + NE])
        b_rout = sb("b_rout", [P, NG + NE])
        ss = sb("ss", [P, 2])
        ms = sb("ms", [P, 2])
        rs0 = sb("rs0", [P, 2])
        rs = sb("rs", [P, 2])
        nt = sb("nt", [P, 2])
        rounds_f = sb("rounds_f", [P, 1])
        rounds_i = sb("rounds_i", [P, 1], I32)

        def tb(name):
            x, w = TABLES[name]
            return tab[:, x:x + w]

        with ExitStack() as st:
            mqT = sb("mqT", [P, MH, S], F32, st)
            mkT = sb("mkT", [P, MH, S], F32, st)
            mV = sb("mV", [P, T, MH * MV], F32, st)
            hg2 = sb("hg2", [P, 4, S], F32, st)
            qh, bcum = hg2[:, 0:2], hg2[:, 2:4]
            mpt0 = hg2.rearrange("p a (b s) -> p (a b) s", b=2)
            kh = sb("kh", [P, 2, S], F32, st)
            ih = sb("ih", [P, T, S], F32, st)
            gate = sb("gate", [P, 2, S], F32, st)
            cosT = sb("cosT", [P, S], F32, st)
            sinT = sb("sinT", [P, S], F32, st)
            small = sb("small", [P, 64], F32, st)
            with ExitStack() as s1:
                lat = sb("lat", [P, 3, S], F32, s1)
                w_uqs = sb("w_uqs", [P, 2, MH, ROPE], F32, s1)
                w_kps = sb("w_kps", [P, KC, ROPE], F32, s1)
                cb = sb("cb", [P, 2, S], F32, s1)
                cu = sb("cu", [P, 2, S], F32, s1)
                cy = sb("cy", [P, 2, S], F32, s1)
                dl = sb("dl", [P, 2, S], F32, s1)
                ql = sb("ql", [P, 2, S], F32, s1)
                kl = sb("kl", [P, 2, S], F32, s1)
                sacc = sb("sacc", [P, 2, T, 2, P], F32, s1)
            ktok = mqT[:, 4:6].rearrange("p t (c s) -> p t c s", c=2)
            with ExitStack() as s1:
                mp0 = sb("mp0", [P, MH, P], F32, s1)
                mp1 = sb("mp1", [P, MH, S], F32, s1)
                mpt1 = sb("mpt1", [P, 2, MH, P], F32, s1)
        with ExitStack() as st:
            qT = sb("qT", [P, KC, S], F32, st)
            kT = sb("kT", [P, KC, S], F32, st)
            vv = sb("vv", [P, T, D], F32, st)
            pr = sb("pr", [P, T, XH, S], F32, st)
            pT = sb("pT", [P, T, XH, S], F32, st)
            oT = sb("oT", [P, KC, S], F32, st)
            xsm = sb("xsm", [P, 64], F32, st)
        with ExitStack() as st:
            hn = sb("hn", [P, T, KC, P], F32, st)
            sel = sb("sel", [P, T, QUADS_PER_STEP * QUAD, SLOTS], F32, st)
            comb = sb("comb", [P, T, QUADS_PER_STEP * QUAD, SLOTS], F32, st)
            xT = sb("xT", [P, KC, P], F32, st)
            cT = sb("cT", [P, T, P], F32, st)
            sg = sb("sg", [P, FE], F32, st)
            hid = sb("hid", [P, FE], F32, st)
            hidT = sb("hidT", [P, 2, P], F32, st)
            yy = sb("yy", [P, D], F32, st)
            lg = sb("lg", [P, T, NG + NE], F32, st)
            combine = sb("combine", [P, T, NE], F32, st)
            chosen = sb("chosen", [P, T, NE], F32, st)
            place = sb("place", [P, T, NE], F32, st)
            rt = sb("rt", [P, 256], F32, st)
            frow = sb("frow", [P, D], F32, st)
        bank = [ctx.enter_context(nc.psum_tensor(f"bank{n}", [P, 512], F32)) for n in range(8)]

        per_layer = ["params", "pe_job", "act_emptied", "dve_emptied", "act_step", "dve_step", "sumsq", "meansq",
                     "rstd0", "normed", "sig_q", "sig_f", "sig_g", "fgate", "logf", "bcum_ready", "diff",
                     "expdiff", "levels_ready", "qk_state", "ktok_scaled", "state_ready", "scores_done",
                     "o_sum", "hg_sq", "hg_rstd",
                     "conv_yb", "conv_sq", "conv_rstd", "lat_sq", "lat_rstd", "lat_ready", "swapped",
                     "mixed", "mla_k", "mla_q", "mla_neg", "mla_exp", "mla_p", "mla_osq", "mla_rstd",
                     "mem_in", "x_max", "x_exp", "x_p", "angles", "rotary", "r_exp", "r_exp_e", "r_chosen",
                     "rounds", "slots", "places_moved", "m_gather", "m_up", "m_down", "m_scatter", "xt_ready", "ct_ready",
                     "silu", "hid_ready", "hidT_ready", "ya_ready", "yv_ready", "added", "sel_written", "arrived"]
        M = {n: sem(n) for n in per_layer}
        nums = [M[n].num for n in per_layer]
        assert nums == list(range(nums[0], nums[0] + len(nums)))
        per_layer_range = range(nums[0], nums[-1] + 1)
        released = sem("released")
        unit_in = [sem(f"unit_in{n}") for n in range(RING)]
        unit_free = sem("unit_free")
        start_in = sem("start_in")
        rope_ang = sem("rope_ang")
        rope_sin = sem("rope_sin")
        lb_e = sem("lb_e")
        lb_x = sem("lb_x")
        setup_done = sem("setup_done")
        sp_rounds = sem("sp_rounds")
        sp_took = sem("sp_took")
        sp_saw = sem("sp_saw")
        pool_saw = sem("pool_saw")
        stored = sem("stored")

        def cols(w, n0, n1, rows="(p c)"):
            return w[:, :, n0:n1].rearrange(f"l {rows} n -> l p c n", p=P)

        gate_w = a["expert_w_gate"].rearrange("l e (p c) f -> (l e) p (c f)", p=P)
        up_w = a["expert_w_up"].rearrange("l e (p c) f -> (l e) p (c f)", p=P)
        down_w = a["expert_w_down"].rearrange("l e (c p) n -> (l e) p c n", p=P)

        block = ctx.enter_context(nc.Block())

        @block.sync
        def _(sp):
            issued = sp.alloc_register("issued")
            sp.reg_mov(issued, 0)
            sp.sem_inc(sp_took, 1)

            def unit(base, n, slot, first, second):
                sp.wait_ge(unit_free, base + (n + 1))
                for dst, src in (first, second):
                    sp.dma_start(dst, src).then_inc(unit_in[slot], 16)

            def column_unit(base, n, w, lay, n0, n1, rows="(p c)"):
                slot = n % RING
                v = ring[slot][:, 0:KC * (n1 - n0)].rearrange("p (c n) -> p c n", c=KC)
                src = cols(w, n0, n1, rows)
                hc = KC // 2
                unit(base, n, slot,
                     (v[:, 0:hc], src[bass.ds(lay, 1), :, 0:hc].rearrange("l p c n -> p (l c) n")),
                     (v[:, hc:KC], src[bass.ds(lay, 1), :, hc:KC].rearrange("l p c n -> p (l c) n")))

            def step_units(base, lay, j):
                for g in range(QUADS_PER_STEP):
                    e0 = lay * NE + (j * QUADS_PER_STEP + g) * QUAD
                    for n in range(UNITS_PER_QUAD):
                        u = g * UNITS_PER_QUAD + n
                        slot = u % RING
                        if n < 4:
                            v = ring[slot].rearrange("p (e w x) -> p e w x", e=QUAD, w=2)
                            x = 2 * FE
                            unit(base, u, slot,
                                 (v[:, :, 0], gate_w[bass.ds(e0, QUAD), :, n * x:(n + 1) * x].rearrange("e p x -> p e x")),
                                 (v[:, :, 1], up_w[bass.ds(e0, QUAD), :, n * x:(n + 1) * x].rearrange("e p x -> p e x")))
                        else:
                            v = ring[slot].rearrange("p (e c x) -> p e c x", e=QUAD, c=2)
                            x = 512
                            k = (n - 4) * x
                            dn = down_w[bass.ds(e0, QUAD), :, :, k:k + x].rearrange("e p c x -> p e c x")
                            unit(base, u, slot, (v[:, 0:2], dn[:, 0:2]), (v[:, 2:4], dn[:, 2:4]))

            with sp.Fori(0, L) as lay:
                base = sp.snap(issued)
                for n in range(5):
                    column_unit(base, n, a["w_in"], lay, 512 * n, min(512 * n + 512, DIN))
                sp.wait_ge(unit_free, base + 6)
                sp.dma_start(ring[5][:, 0:1536].rearrange("p (c n) -> p c n", c=2),
                             a["mla_w_uq"][bass.ds(lay, 1)].rearrange("l (c p) n -> p (l c) n", p=P)).then_inc(unit_in[5], 16)
                sp.dma_start(ring[5][:, 1536:2560],
                             a["mla_w_ukv"][bass.ds(lay, 1)].rearrange("l p n -> p (l n)")).then_inc(unit_in[5], 16)
                for n in range(2):
                    column_unit(base, 6 + n, a["w_out"], lay, 512 * n, 512 * n + 512, "(c p)")
                for k, (w, rows) in enumerate([("xa_wq", "(p c)"), ("xa_wk", "(p c)"), ("xa_wv", "(p c)"), ("xa_wo", "(c p)")]):
                    for n in range(2):
                        column_unit(base, 8 + 2 * k + n, a[w], lay, 512 * n, 512 * n + 512, rows)
                sp.reg_add(issued, issued, FIXED_UNITS)
                with sp.Fori(0, MOE_STEPS) as j:
                    base_j = sp.snap(issued)
                    step_units(base_j, lay, j)
                    sp.reg_add(issued, issued, STEP_UNITS)
                sp.wait_ge(sp_rounds, lay + 1)
                sp.sem_inc(sp_saw, 1)
                r = sp.value_load(rounds_i[0:1, 0:1], min_val=1, max_val=8)
                sp.sem_inc(sp_took, 1)
                with sp.If(r > 1):
                    with sp.Fori(1, r):
                        with sp.Fori(0, MOE_STEPS) as j2:
                            base_j = sp.snap(issued)
                            step_units(base_j, lay, j2)
                            sp.reg_add(issued, issued, STEP_UNITS)
            sp.wait_ge(stored, 32)

        @block.tensor
        def _(pe):
            ring_base = pe.alloc_register("ring_base")
            pe.reg_mov(ring_base, 0)
            pe.sem_inc(unit_free, RING)
            pe.wait_ge(start_in, 16 * 3)
            ident = tb("ident")

            def begin(name):
                n = INDEX[name]
                if n >= 8:
                    before, who = JOBS[n - 8]
                    pe.wait_ge(M["act_emptied"] if who == "A" else M["dve_emptied"], emptied(before))
                return bank[n % 8]

            def after(name):
                pe.wait_ge(M["act_emptied"] if JOBS[INDEX[name]][1] == "A" else M["dve_emptied"], emptied(name))

            def wait_unit(base, n):
                pe.wait_ge(unit_in[n % RING], base + LOADED * (n // RING + 1))

            def transposes(prefix, src, k):
                pe.wait_ge(M["normed"], k)
                for n in range(4):
                    o = begin(f"{prefix}_xt{n}")
                    for c in range(2):
                        for t in range(T):
                            mm = pe.transpose(o[:, c * S + t * P:c * S + t * P + P], src[:, t, 2 * n + c], ident)
                    mm.then_inc(M["pe_job"], 1)

            def channel_tile(o, w, c0, m, rhs, chunks=KC, row0=0):
                for c in range(chunks):
                    mm = pe.matmul(o[row0:row0 + m], w[:, c, c0:c0 + m], rhs[:, c], start=(c == 0), stop=(c == chunks - 1))
                return mm

            def two_tiles(name, w, c0, rhs):
                o = begin(name)
                for k in range(2):
                    mm = channel_tile(o[:, k * S:(k + 1) * S], w, c0 + k * P, P, rhs)
                mm.then_inc(M["pe_job"], 1)

            def unit_view(slot, n):
                return ring[slot][:, 0:KC * n].rearrange("p (c n) -> p c n", c=KC)

            def level(lv):
                pe.wait_ge(M["levels_ready"], lv + 1)
                for odd in range(2):
                    o = begin(f"lv{lv}{'eo'[odd]}")
                    lo = CHUNK * odd
                    for t in range(T):
                        for pair in range(2):
                            x = (t * 2 + pair) * P
                            mm = pe.matmul(o[:, x:x + P], kl[lo:lo + HD, pair, t * P:t * P + P],
                                           ql[lo:lo + HD, pair, t * P:t * P + P], start=True, stop=True)
                    mm.then_inc(M["pe_job"], 1)

            def block_sums(name, blk, sq, ready, count):
                pe.wait_ge(ready, count)
                pe.matmul(begin(name)[:, :], blk, sq.rearrange("p c s -> p (c s)"), start=True, stop=True).then_inc(M["pe_job"], 1)

            def add_to_rows(prefix, lhs, base, first):
                for n in range(2):
                    wait_unit(base, first + n)
                    w = unit_view((first + n) % RING, 512)
                    for t in range(T):
                        o = begin(f"{prefix}{2 * n + t}")
                        for c in range(KC):
                            mm = pe.matmul(o[:, :], lhs[:, c, t * P:t * P + P], w[:, c], start=(c == 0), stop=(c == KC - 1))
                        mm.then_inc(M["pe_job"], 1)
                    pe.wait_ge(M["pe_job"], INDEX[f"{prefix}{2 * n + 1}"] + 1)
                    pe.sem_inc(unit_free, 1)

            def free_unit(name):
                pe.wait_ge(M["pe_job"], INDEX[name] + 1)
                pe.sem_inc(unit_free, 1)

            def quad(step, g, base):
                q = step * QUADS_PER_STEP + g
                t0, t1, gu, d0, d1, s0, s1 = bank[0], bank[1], bank[2 + g % 2], bank[4], bank[5], bank[6], bank[7]
                x = slice(g * QUAD, (g + 1) * QUAD)
                for half, o in enumerate((t0, t1)):
                    for c in range(4):
                        for t in range(T):
                            mm = pe.matmul(o[:, c * P:c * P + P], hn[:, t, half * 4 + c],
                                           sel[:, t, x].rearrange("p e s -> p (e s)"), start=(t == 0), stop=(t == T - 1))
                    mm.then_inc(M["m_gather"], 1)
                pe.wait_ge(M["xt_ready"], q * 2 + 1)
                for t in range(T):
                    mm = pe.transpose(t0[:, t * P:t * P + P], comb[:, t, x].rearrange("p e s -> p (e s)"), ident)
                mm.then_inc(M["m_gather"], 1)
                pe.wait_ge(M["xt_ready"], q * 2 + 2)
                for n in range(4):
                    u = g * UNITS_PER_QUAD + n
                    wait_unit(base, u)
                    w = ring[u % RING].rearrange("p (e w c f) -> p e w c f", e=QUAD, w=2, c=2)
                    for c in range(2):
                        for e in range(QUAD):
                            first, last = n == 0 and c == 0, n == 3 and c == 1
                            mm = pe.matmul(gu[32 * e:32 * e + 32, :], xT[:, 2 * n + c, 32 * e:32 * e + 32],
                                           w[:, e, :, c], start=first, stop=last, tile_position=(0, 32 * e))
                    mm.then_inc(M["m_up"], 1)
                    pe.wait_ge(M["m_up"], q * 4 + (n + 1))
                    pe.sem_inc(unit_free, 1)
                pe.wait_ge(M["hid_ready"], q + 1)
                for c in range(2):
                    mm = pe.transpose(t1[:, c * P:c * P + P], hid[:, c * P:c * P + P], ident)
                mm.then_inc(M["m_gather"], 1)
                pe.wait_ge(M["hidT_ready"], q + 1)
                for n, o in enumerate((d0, d1)):
                    u = g * UNITS_PER_QUAD + 4 + n
                    wait_unit(base, u)
                    w = ring[u % RING].rearrange("p (e c x) -> p e c x", e=QUAD, c=2)
                    for c in range(2):
                        for e in range(QUAD):
                            mm = pe.matmul(o[32 * e:32 * e + 32, :], hidT[:, c, 32 * e:32 * e + 32], w[:, e, c],
                                           start=(c == 0), stop=(c == 1), tile_position=(0, 32 * e))
                    mm.then_inc(M["m_down"], 1)
                    pe.wait_ge(M["m_down"], q * 2 + (n + 1))
                    pe.sem_inc(unit_free, 1)
                pe.wait_ge(M["ct_ready"], q + 1)
                for t in range(T):
                    pe.wait_ge(M["added"], q * 4 + (2 * t + 1))
                    for n, o in enumerate((s0, s1)):
                        if t == 0:
                            pe.wait_ge(M["ya_ready"] if n == 0 else M["yv_ready"], q + 1)
                        pe.matmul(o[:, :], cT[:, t], yy[:, n * 512:n * 512 + 512], start=True, stop=True).then_inc(M["m_scatter"], 1)

            with pe.Fori(0, L) as lay:
                base = pe.snap(ring_base)
                pe.reg_add(ring_base, ring_base, LOADED * FIXED_UNITS // RING)
                transposes("mix", mqT.rearrange("p a s -> p (a s)").rearrange("p (t c k) -> p t c k", t=T, c=KC), 1)
                after("mix_xt3")
                wait_unit(base, 0)
                w = unit_view(0, 512)
                two_tiles("f", w, 256, uT)
                two_tiles("q", w, 0, uT)
                free_unit("q")
                wait_unit(base, 1)
                w = unit_view(1, 512)
                o = begin("i")
                for t in range(T):
                    for c in range(KC):
                        mm = pe.matmul(o[:, t * S:(t + 1) * S], uT[:, c, t * P:t * P + P], w[:, c, 0:256], start=(c == 0), stop=(c == KC - 1))
                mm.then_inc(M["pe_job"], 1)
                two_tiles("g", w, 256, uT)
                free_unit("g")
                level(0)
                wait_unit(base, 2)
                w = unit_view(2, 512)
                two_tiles("b", w, 0, uT)
                two_tiles("c", w, 256, uT)
                free_unit("c")
                level(1)
                wait_unit(base, 3)
                w = unit_view(3, 512)
                two_tiles("hc", w, 0, uT)
                level(2)
                two_tiles("cq", w, 256, uT)
                free_unit("cq")
                level(3)
                wait_unit(base, 4)
                w = unit_view(4, DIN - 2048)
                o = begin("kv")
                channel_tile(o[:, 0:S], w, 0, P, uT)
                channel_tile(o[:, S:2 * S], w, 64, 96, uT).then_inc(M["pe_job"], 1)
                o = begin("kvs")
                pe.wait_ge(M["swapped"], 1)
                channel_tile(o[:, 0:S], w_kps, 0, ROPE, uT, row0=64).then_inc(M["pe_job"], 1)
                free_unit("kvs")
                level(4)
                pe.wait_ge(M["lat_sq"], 1)
                o = begin("latss")
                sq = mqT.rearrange("p a s -> p (a s)")
                pe.matmul(o[:, 0:S], tb("ones"), sq[:, 0:S], start=True, stop=False)
                pe.matmul(o[:, 0:S], tb("ones"), sq[:, S:2 * S], start=False, stop=True)
                pe.matmul(o[:, S:2 * S], tb("ones"), sq[:, 2 * S:3 * S], start=True, stop=True).then_inc(M["pe_job"], 1)
                pe.wait_ge(M["ktok_scaled"], 1)
                o = begin("ktok")
                for t in range(T):
                    for pair in range(2):
                        mm = pe.transpose(o[:, (t * 2 + pair) * P:(t * 2 + pair + 1) * P], kl[:, pair, t * P:t * P + P], ident)
                mm.then_inc(M["pe_job"], 1)
                after("ktok")
                o = begin("u0")
                for k, ch in enumerate((0, 2)):
                    for pair in range(2):
                        mm = pe.matmul(o[:, (2 * k + pair) * P:(2 * k + pair + 1) * P], ktok[0:64, ch // 2, pair],
                                       ih[0:64, ch // 2, pair * P:pair * P + P], start=True, stop=True)
                mm.then_inc(M["pe_job"], 1)
                o = begin("u1")
                for pair in range(2):
                    mm = pe.matmul(o[:, pair * P:pair * P + P], ktok[64:128, 0, pair],
                                   ih[64:128, 0, pair * P:pair * P + P], start=True, stop=True)
                mm.then_inc(M["pe_job"], 1)
                block_sums("convss", tb("blk64"), cu, M["conv_sq"], 1)
                pe.wait_ge(M["scores_done"], 1)
                o = begin("o_in")
                for pair in range(2):
                    for t in range(T):
                        for odd in range(2):
                            hx = (2 * pair + odd) * HD
                            mm = pe.matmul(o[64 * odd:64 * odd + 64, pair * S + t * P:pair * S + t * P + P],
                                           ih[:, t, hx:hx + HD], sacc[:, odd, t, pair], start=True, stop=True)
                mm.then_inc(M["pe_job"], 1)
                pe.wait_ge(M["state_ready"], 1)
                o = begin("o_st")
                for pair in range(2):
                    for ch in range(1, 4):
                        mm = pe.matmul(o[:, pair * S + ch * CHUNK:pair * S + (ch + 1) * CHUNK], states[:, ch - 1, pair],
                                       ql[:, pair, ch * CHUNK:(ch + 1) * CHUNK], start=True, stop=True)
                mm.then_inc(M["pe_job"], 1)
                block_sums("hgss", tb("blk64"), kl, M["hg_sq"], 1)
                wait_unit(base, 5)
                wq = ring[5][:, 0:1536].rearrange("p (c n) -> p c n", c=2)
                wkv = ring[5][:, 1536:2560]
                pe.wait_ge(M["lat_ready"], 1)
                for n in range(4):
                    o = begin(f"mq{n}")
                    for k in range(2):
                        mm = channel_tile(o[:, k * S:(k + 1) * S], wq, (2 * n + k) * QK, QK, lat, chunks=2)
                    mm.then_inc(M["pe_job"], 1)
                pe.wait_ge(M["swapped"], 2)
                for n in range(4):
                    o = begin(f"mqs{n}")
                    for k in range(2):
                        mm = channel_tile(o[:, k * S:(k + 1) * S], w_uqs.rearrange("p c h r -> p c (h r)"),
                                          (2 * n + k) * ROPE, ROPE, lat, chunks=2, row0=64)
                    mm.then_inc(M["pe_job"], 1)
                for n in range(4):
                    o = begin(f"mk{n}")
                    for k in range(2):
                        hx = (2 * n + k) * (NOPE + MV)
                        mm = pe.matmul(o[0:NOPE, k * S:(k + 1) * S], wkv[:, hx:hx + NOPE], lat[:, 2], start=True, stop=True)
                    mm.then_inc(M["pe_job"], 1)
                for t in range(T):
                    pe.matmul(begin(f"mv{t}")[:, :], lat[:, 2, t * P:t * P + P],
                              wkv.rearrange("p (h n) -> p h n", h=MH)[:, :, NOPE:NOPE + MV], start=True, stop=True).then_inc(M["pe_job"], 1)
                free_unit("mv1")
                after("mv1")
                pe.wait_ge(M["mla_k"], 1)
                pe.wait_ge(M["mla_q"], 1)
                for n in range(2):
                    o = begin(f"ms{n}")
                    for k in range(4):
                        mm = pe.matmul(o[:, k * P:(k + 1) * P], mqT[0:QK, 4 * n + k, 0:P], mkT[0:QK, 4 * n + k, 0:P], start=True, stop=True)
                    mm.then_inc(M["pe_job"], 1)
                for n in range(4):
                    o = begin(f"ms{2 + n}")
                    for k in range(2):
                        mm = pe.matmul(o[:, k * S:(k + 1) * S], mqT[0:QK, 2 * n + k, P:S], mkT[0:QK, 2 * n + k], start=True, stop=True)
                    mm.then_inc(M["pe_job"], 1)
                pe.wait_ge(M["mla_p"], 1)
                for n in range(2):
                    o = begin(f"mt{n}")
                    for k in range(4):
                        mm = pe.transpose(o[:, k * P:(k + 1) * P], mp0[:, 4 * n + k], ident)
                    mm.then_inc(M["pe_job"], 1)
                pe.wait_ge(M["mla_p"], 2)
                for n in range(4):
                    o = begin(f"mt{2 + n}")
                    for k in range(4):
                        mm = pe.transpose(o[:, k * P:(k + 1) * P], mp1[:, 4 * (n % 2) + k, (n // 2) * P:(n // 2 + 1) * P], ident)
                    mm.then_inc(M["pe_job"], 1)
                after("mt5")
                for n in range(2):
                    o = begin(f"mo{n}")
                    for t in range(T):
                        for k in range(4):
                            hx = 4 * n + k
                            dst = o[64 * (k % 2):64 * (k % 2) + 64, (k // 2) * S + t * P:(k // 2) * S + (t + 1) * P]
                            for kt in range(t + 1):
                                mm = pe.matmul(dst, mV[:, kt, hx * MV:(hx + 1) * MV], mpt1[:, kt, hx] if t else mpt0[:, hx],
                                               start=(kt == 0), stop=(kt == t))
                    mm.then_inc(M["pe_job"], 1)
                for n in range(2):
                    block_sums(f"mss{n}", tb("blk64"), mqT[:, 4 + 2 * n:6 + 2 * n], M["mla_osq"], n + 1)
                pe.wait_ge(M["mixed"], 3)
                add_to_rows("out", uT, base, 6)

                transposes("cross", qT.rearrange("p a s -> p (a s)").rearrange("p (t c k) -> p t c k", t=T, c=KC), 2)
                after("cross_xt3")
                for n in range(2):
                    wait_unit(base, 8 + n)
                    w = unit_view((8 + n) % RING, 512)
                    two_tiles(f"xq{2 * n}", w, 0, uT)
                    two_tiles(f"xq{2 * n + 1}", w, 256, uT)
                    free_unit(f"xq{2 * n + 1}")
                transposes("mem", pr.rearrange("p t h s -> p (t h s)").rearrange("p (t c k) -> p t c k", t=T, c=KC), 3)
                after("mem_xt3")
                mT = pT.rearrange("p t h s -> p (t h) s")
                for n in range(2):
                    wait_unit(base, 10 + n)
                    w = unit_view((10 + n) % RING, 512)
                    two_tiles(f"xk{2 * n}", w, 0, mT)
                    two_tiles(f"xk{2 * n + 1}", w, 256, mT)
                    free_unit(f"xk{2 * n + 1}")
                add_to_rows("xv", mT, base, 12)
                after("xk3")
                for t in range(T):
                    for n in range(2):
                        o = begin(f"xs{2 * t + n}")
                        for k in range(2):
                            hx = 2 * n + k
                            for c in range(2):
                                mm = pe.matmul(o[:, k * S:(k + 1) * S], qT[:, 2 * hx + c, t * P:t * P + P], kT[:, 2 * hx + c],
                                               start=(c == 0), stop=(c == 1))
                        mm.then_inc(M["pe_job"], 1)
                for t in range(T):
                    pe.wait_ge(M["x_p"], t + 1)
                    for kt in range(T):
                        o = begin(f"xt{2 * t + kt}")
                        for hx in range(XH):
                            mm = pe.transpose(o[:, hx * P:(hx + 1) * P], pr[:, t, hx, kt * P:(kt + 1) * P], ident)
                        mm.then_inc(M["pe_job"], 1)
                after("xv3")
                after("xt3")
                for n in range(4):
                    o = begin(f"xo{n}")
                    for k in range(2):
                        for kt in range(T):
                            mm = pe.matmul(o[:, k * S:(k + 1) * S], vv[:, kt, (2 * n + k) * P:(2 * n + k + 1) * P], pT[:, kt, n],
                                           start=(kt == 0), stop=(kt == 1))
                    mm.then_inc(M["pe_job"], 1)
                after("xo3")
                add_to_rows("xout", oT, base, 14)

                transposes("ffn", hn, 4)
                after("ffn_xt3")
                o = begin("router")
                for t in range(T):
                    for c in range(KC):
                        mm = pe.matmul(o[:, t * 64:t * 64 + NG + NE], uT[:, c, t * P:t * P + P], w_rout[:, c], start=(c == 0), stop=(c == KC - 1))
                mm.then_inc(M["pe_job"], 1)
                pe.wait_ge(M["r_chosen"], 1)
                o = begin("places")
                pe.matmul(o[:, 0:NE], tb("before"), chosen[:, 0], start=True, stop=True)
                pe.matmul(o[:, NE:2 * NE], tb("before"), chosen[:, 1], start=True, stop=False)
                pe.matmul(o[:, NE:2 * NE], tb("ones"), chosen[:, 0], start=False, stop=True)
                pe.matmul(o[:, 2 * NE:3 * NE], tb("ones"), chosen[:, 0], start=True, stop=False)
                pe.matmul(o[:, 2 * NE:3 * NE], tb("ones"), chosen[:, 1], start=False, stop=True).then_inc(M["pe_job"], 1)

                pe.wait_ge(M["rounds"], 1)
                after("places")
                r = pe.value_load(rounds_i[0:1, 0:1], min_val=1, max_val=8)
                with pe.Fori(0, r) as rnd:
                    with pe.Fori(0, MOE_STEPS) as j:
                        step = rnd * MOE_STEPS + j
                        base_j = pe.snap(ring_base)
                        pe.reg_add(ring_base, ring_base, LOADED * STEP_UNITS // RING)
                        pe.wait_ge(M["slots"], step + 1)
                        for g in range(QUADS_PER_STEP):
                            quad(step, g, base_j)
                pe.sem_inc(M["arrived"], 1)
                pe.wait_ge(released, lay + 1)

        @block.scalar
        def _(act):
            steps = [0]

            def tick():
                steps[0] += 1
                return 1

            def settle():
                act.wait_ge(M["act_step"], steps[0])

            def job(name):
                act.wait_ge(M["pe_job"], INDEX[name] + 1)
                return bank[INDEX[name] % 8]

            def sum_squares(src, junk):
                for t in range(T):
                    act.activation(junk[:, t], src[:, t], ACT.Square, accum_out=ss[:, t:t + 1]).then_inc(M["sumsq"], 1)

            def first_rstd(k):
                act.wait_ge(M["meansq"], k)
                act.activation(nt[:, :], ms[:, :], ACT.Ln).then_inc(M["act_step"], tick())
                settle()
                act.activation(rs0[:, :], nt[:, :], ACT.Exp, scale=-0.5).then_inc(M["rstd0"], 1)

            def empty_transposes(prefix, dst, gain):
                for n in range(4):
                    o = job(f"{prefix}_xt{n}")
                    for c in range(2):
                        i = act.activation(dst[:, 2 * n + c], o[:, c * S:(c + 1) * S], ACT.Identity, scale=gains[:, gain, 2 * n + c:2 * n + c + 1])
                    i.then_inc(M["act_emptied"], 1)

            def copy_out(name, dst, src=None):
                o = job(name)
                act.activation(dst, o[:, :] if src is None else src(o), ACT.Copy).then_inc(M["act_emptied"], 1)

            def group_rstd(name, dst, n, done):
                o = job(name)
                act.activation(dst, o[:, :], ACT.Ln, bias=tb("eps"), scale=1.0 / n).then_inc(M["act_step"], tick())
                settle()
                act.activation(dst, dst, ACT.Exp, scale=-0.5).then_inc(done, 1)

            flat = lambda x: x.rearrange("p c s -> p (c s)")
            act.dma_start(tab[:, :], tables[:, :]).then_inc(start_in, 16)
            act.dma_start(uT.rearrange("p c s -> p (c s)")[:, 0:LEVELS * P], level_masks[:, :]).then_inc(start_in, 16)
            act.dma_start(h[:, :, :], a["x"].rearrange("b (t p) d -> p (b t) d", p=P)).then_inc(start_in, 16)
            for l in range(L):
                for ct in range(2):
                    act.dma_start(lb_raw[:, l, ct:ct + 1], a["hgrn_lower_bounds"][l:l + 1, ct * P:(ct + 1) * P].rearrange("l p -> p l")).then_inc(lb_e, 16)
            act.wait_ge(start_in, 16 * 3)
            act.wait_ge(lb_x, 1)
            act.activation(lb_tmp[:, 0:L], lb_tmp[:, 0:L], ACT.Exp).then_inc(lb_x, 1)
            with act.Fori(0, L) as lay:
                steps[0] = 0
                row = bass.ds(lay, 1)
                def param(dst, src):
                    act.dma_start(dst, src).then_inc(M["params"], 16)
                for k, name in enumerate(["norm_mix", "norm_cross", "norm_mem", "norm_ffn"]):
                    param(gains[:, k], a[name][row].rearrange("l (p c) -> p (l c)", p=P))
                for k in range(2):
                    param(g_hgrn[64 * k:64 * k + 64], a["hgrn_norm"][row].rearrange("l p -> p l"))
                    param(g_conv[:, k:k + 1], a["conv_norm"][row, k * P:(k + 1) * P].rearrange("l p -> p l"))
                    param(g_lat[:, k:k + 1], a["mla_q_norm"][row, k * P:(k + 1) * P].rearrange("l p -> p l"))
                    for t in range(3):
                        param(w_conv[:, t, k:k + 1], a["conv_w"][row, t, k * P:(k + 1) * P].rearrange("l p -> p l"))
                for k in range(4):
                    param(g_out[:, k:k + 1], a["mla_out_norm"][row, k * P:(k + 1) * P].rearrange("l p -> p l"))
                param(g_lat[:, 2:3], a["mla_kv_norm"][row].rearrange("l p -> p l"))
                param(mkT[64:96, 0, :].bitcast(I32), a["positions"].broadcast_to([ROPE, S]))
                param(w_rout[:, :, 0:NG], a["router_group_w"][row].rearrange("l (p c) g -> p (l c) g", p=P))
                for g in range(NG):
                    param(w_rout[:, :, NG + g * EG:NG + (g + 1) * EG], a["router_expert_w"][row, g].rearrange("l (p c) e -> p (l c) e", p=P))
                param(b_rout[:, 0:NG], a["router_group_b"][row].broadcast_to([P, NG]))
                param(b_rout[:, NG:NG + NE], a["router_expert_b"][row].rearrange("l g e -> l (g e)").broadcast_to([P, NE]))

                nrow = mqT.rearrange("p a s -> p (a s)").rearrange("p (t c) -> p t c", t=T)
                sum_squares(h, nrow)
                first_rstd(1)
                act.wait_ge(M["params"], 16 * N_PARAMS)
                act.wait_ge(M["angles"], 1)
                act.activation(sinT[64:96], sinT[64:96], ACT.Sin).then_inc(M["act_step"], tick())
                act.activation(cosT[64:96], cosT[64:96], ACT.Sin).then_inc(M["rotary"], 1)
                empty_transposes("mix", uT, 0)
                act.activation(flat(dl), job("f")[:, :], ACT.Sigmoid).then_inc(M["act_emptied"], 1)
                act.activation(flat(ql), job("q")[:, :], ACT.Sigmoid).then_inc(M["sig_q"], 1)
                copy_out("i", ih.rearrange("p t s -> p (t s)"))
                act.activation(flat(kl), job("g")[:, :], ACT.Sigmoid).then_inc(M["sig_g"], 1)
                act.wait_ge(M["fgate"], 1)
                act.activation(flat(dl), flat(dl), ACT.Ln).then_inc(M["logf"], 1)

                def exp_level(lv):
                    act.wait_ge(M["diff"], lv + 1)
                    if lv == 0:
                        act.activation(flat(ql), flat(dl), ACT.Exp).then_inc(M["act_step"], tick())
                        act.activation(flat(kl), flat(dl), ACT.Exp, scale=-1.0).then_inc(M["expdiff"], 1)
                    else:
                        act.activation(flat(kl), flat(dl), ACT.Exp).then_inc(M["expdiff"], 1)
                exp_level(0)
                copy_out("b", flat(cb))
                copy_out("c", flat(cu))
                exp_level(1)
                exp_level(2)
                copy_out("cq", flat(lat[:, 0:2]))
                exp_level(3)
                o = job("kv")
                act.activation(lat[:, 2], o[:, 0:S], ACT.Copy).then_inc(M["act_step"], tick())
                act.activation(mkT[64:96, 0], o[64:96, S:2 * S], ACT.Copy).then_inc(M["act_emptied"], 1)
                settle()
                act.wait_ge(M["act_emptied"], emptied("kv"))
                act.activation(mqT.rearrange("p a s -> p (a s)")[:, 0:3 * S], flat(lat), ACT.Square).then_inc(M["lat_sq"], 1)
                exp_level(4)
                o = job("latss")
                rl = mkT[:, 4:6]
                act.activation(rl[:, 0], o[:, 0:S], ACT.Ln, bias=tb("eps"), scale=1.0 / 256).then_inc(M["act_step"], tick())
                act.activation(rl[:, 1], o[:, S:2 * S], ACT.Ln, bias=tb("eps"), scale=1.0 / 128).then_inc(M["act_emptied"], 1)
                settle()
                act.wait_ge(M["act_emptied"], emptied("latss"))
                act.activation(flat(rl), flat(rl), ACT.Exp, scale=-0.5).then_inc(M["lat_rstd"], 1)
                act.wait_ge(M["qk_state"], 1)
                act.activation(flat(ql), flat(bcum), ACT.Exp).then_inc(M["act_step"], tick())
                act.activation(flat(kl), flat(dl), ACT.Exp).then_inc(M["expdiff"], 1)
                copy_out("ktok", ktok.rearrange("p t c s -> p (t c s)"))
                act.wait_ge(M["conv_yb"], 1)
                act.activation(flat(cu), flat(cy), ACT.Square).then_inc(M["conv_sq"], 1)
                group_rstd_done(act, job, "convss", flat(cb), 64, M, tick, settle, tb, M["conv_rstd"])
                copy_out("o_in", flat(dl))
                act.wait_ge(M["o_sum"], 1)
                act.activation(flat(kl), flat(dl), ACT.Square).then_inc(M["hg_sq"], 1)
                group_rstd_done(act, job, "hgss", flat(ql), 64, M, tick, settle, tb, M["hg_rstd"])
                for n in range(4):
                    copy_out(f"mq{n}", mqT[0:QK, 2 * n:2 * n + 2].rearrange("p c s -> p (c s)"), lambda o: o[0:QK, :])
                for n in range(4):
                    copy_out(f"mk{n}", mkT[0:NOPE, 2 * n:2 * n + 2].rearrange("p c s -> p (c s)"), lambda o: o[0:NOPE, :])
                for t in range(T):
                    copy_out(f"mv{t}", mV[:, t])
                for t, mp in enumerate((mp0, mp1)):
                    act.wait_ge(M["mla_neg"], t + 1)
                    for k in range(MH):
                        x = 8 * t + k
                        act.activation(mp[:, k], mp[:, k], ACT.Exp, bias=small[:, x:x + 1],
                                       accum_out=small[:, 16 + x:17 + x]).then_inc(M["mla_exp"], 1)
                for n in range(2):
                    copy_out(f"mt{n}", mpt0[:, 4 * n:4 * n + 4].rearrange("p c s -> p (c s)"))
                for n in range(4):
                    copy_out(f"mt{2 + n}", mpt1[:, n // 2, 4 * (n % 2):4 * (n % 2) + 4].rearrange("p c s -> p (c s)"))
                for n in range(2):
                    copy_out(f"mo{n}", mqT[:, 2 * n:2 * n + 2].rearrange("p c s -> p (c s)"))
                for n in range(2):
                    act.wait_ge(M["act_emptied"], emptied(f"mo{n}"))
                    act.activation(mqT[:, 4 + 2 * n:6 + 2 * n], mqT[:, 2 * n:2 * n + 2], ACT.Square).then_inc(M["mla_osq"], 1)
                for n in range(2):
                    group_rstd_done(act, job, f"mss{n}", mkT[:, 2 * n:2 * n + 2].rearrange("p c s -> p (c s)"), 64, M, tick, settle, tb, M["mla_rstd"])

                act.wait_ge(M["dve_emptied"], emptied("out3"))
                act.dma_start(pr.rearrange("p t h s -> p t (h s)"), a["mem"].rearrange("b (t p) d -> p (b t) d", p=P)).then_inc(M["mem_in"], 16)
                sum_squares(h, qT.rearrange("p a s -> p (a s)").rearrange("p (t c) -> p t c", t=T))
                first_rstd(2)
                empty_transposes("cross", uT, 1)
                act.wait_ge(M["mem_in"], 16)
                sum_squares(pr.rearrange("p t h s -> p t (h s)"), oT.rearrange("p a s -> p (a s)").rearrange("p (t c) -> p t c", t=T))
                for n in range(4):
                    copy_out(f"xq{n}", qT[:, 2 * n:2 * n + 2].rearrange("p c s -> p (c s)"))
                first_rstd(3)
                empty_transposes("mem", pT.rearrange("p t h s -> p (t h) s"), 2)
                for n in range(4):
                    copy_out(f"xk{n}", kT[:, 2 * n:2 * n + 2].rearrange("p c s -> p (c s)"))
                for n in range(4):
                    act.wait_ge(M["x_max"], n + 1)
                    o = job(f"xs{n}")
                    for k in range(2):
                        x = 2 * n + k
                        i = act.activation(pr[:, n // 2, 2 * (n % 2) + k], o[:, k * S:(k + 1) * S], ACT.Exp, bias=xsm[:, x:x + 1],
                                           scale=XD ** -0.5, accum_out=xsm[:, 8 + x:9 + x])
                        i.then_inc(M["x_exp"], 1)
                    act.wait_ge(M["x_exp"], 2 * n + 2)
                    act.sem_inc(M["act_emptied"], 1)
                for n in range(4):
                    t, kt = n // 2, n % 2
                    o = job(f"xt{n}")
                    act.activation(pT[:, kt, :, t * P:(t + 1) * P], o[:, :].rearrange("p (h s) -> p h s", h=XH), ACT.Copy).then_inc(M["act_emptied"], 1)

                act.wait_ge(M["dve_emptied"], emptied("xout3"))
                sum_squares(h, hn.rearrange("p t c k -> p t (c k)"))
                first_rstd(4)
                empty_transposes("ffn", uT, 3)
                act.wait_ge(M["r_exp"], 1)
                act.activation(rt[:, 8:16], rt[:, 8:16], ACT.Exp).then_inc(M["r_exp_e"], 1)
                act.wait_ge(M["r_exp"], 2)
                act.activation(rt[:, 128:130], rt[:, 128:130], ACT.Exp).then_inc(M["r_exp_e"], 1)
                act.wait_ge(M["rounds"], 1)
                r = act.value_load(rounds_i[0:1, 0:1], min_val=1, max_val=8)
                with act.Fori(0, r) as rnd:
                    with act.Fori(0, MOE_STEPS) as j:
                        step = rnd * MOE_STEPS + j
                        for g in range(QUADS_PER_STEP):
                            q = step * QUADS_PER_STEP + g
                            act.wait_ge(M["m_gather"], q * 4 + 3)
                            act.activation(cT.rearrange("p t s -> p (t s)"), bank[0][:, 0:S], ACT.Copy).then_inc(M["ct_ready"], 1)
                            act.wait_ge(M["m_up"], q * 4 + 4)
                            act.activation(sg[:, :], bank[2 + g % 2][:, 0:FE], ACT.Silu).then_inc(M["silu"], 1)
                            act.wait_ge(M["m_gather"], q * 4 + 4)
                            act.activation(hidT.rearrange("p c s -> p (c s)"), bank[1][:, 0:S], ACT.Copy).then_inc(M["hidT_ready"], 1)
                            act.wait_ge(M["m_down"], q * 2 + 1)
                            act.activation(yy[:, 0:512], bank[4][:, :], ACT.Copy).then_inc(M["ya_ready"], 1)
                act.sem_inc(M["arrived"], 1)
                act.wait_ge(released, lay + 1)
            act.dma_start(frow[:, :], a["final_norm"].rearrange("(l d) -> l d", l=1).broadcast_to([P, D])).then_inc(M["params"], 16)
            steps[0] = 0
            sum_squares(h, hn.rearrange("p t c k -> p t (c k)"))
            first_rstd(1)
            for t in range(T):
                act.wait_ge(M["normed"], t + 1)
                act.dma_start(out.rearrange("b (t p) d -> p (b t) d", p=P)[:, t], h[:, t]).then_inc(stored, 16)

        @block.vector
        def _(dve):
            steps = [0]

            def tick():
                steps[0] += 1
                return 1

            def settle():
                dve.wait_ge(M["dve_step"], steps[0])

            def st(i):
                i.then_inc(M["dve_step"], tick())

            def job(name):
                dve.wait_ge(M["pe_job"], INDEX[name] + 1)
                return bank[INDEX[name] % 8]

            def gone(i):
                i.then_inc(M["dve_emptied"], 1)

            flat = lambda x: x.rearrange("p c s -> p (c s)")

            def mean_square(k):
                dve.wait_ge(M["sumsq"], 2 * k)
                dve.tensor_scalar(ms[:, :], ss[:, :], 1.0 / D, EPS, ALU.mult, ALU.add).then_inc(M["meansq"], 1)

            def refine(k):
                dve.wait_ge(M["rstd0"], k)
                st(dve.tensor_tensor(nt[:, :], rs0[:, :], rs0[:, :], ALU.mult))
                settle()
                st(dve.tensor_tensor(nt[:, :], nt[:, :], ms[:, :], ALU.mult))
                settle()
                st(dve.tensor_scalar(nt[:, :], nt[:, :], -0.5, 1.5, ALU.mult, ALU.add))
                settle()
                st(dve.tensor_tensor(rs[:, :], rs0[:, :], nt[:, :], ALU.mult))
                settle()

            def norm_rows(dst, src, k):
                mean_square(k)
                refine(k)
                for t in range(T):
                    i = dve.tensor_scalar(dst[:, t].rearrange("p (c k) -> p c k", c=KC),
                                          src[:, t].rearrange("p (k c) -> p c k", c=KC), rs[:, t:t + 1], None, ALU.mult)
                    if t == 0:
                        st(i)
                settle()
                i.then_inc(M["normed"], 1)

            def norm_rows_in_place(tmp, x, k):
                mean_square(k)
                refine(k)
                for t in range(T):
                    st(dve.tensor_scalar(tmp[:, t], x[:, t], rs[:, t:t + 1], None, ALU.mult))
                settle()
                for t in range(T):
                    i = dve.tensor_copy(x[:, t].rearrange("p (c k) -> p c k", c=KC), tmp[:, t].rearrange("p (k c) -> p c k", c=KC))
                    if t == 0:
                        st(i)
                settle()
                i.then_inc(M["normed"], 1)

            dve.wait_ge(start_in, 16 * 3)
            dve.tensor_copy(lvmask.rearrange("p l s -> p (l s)"), uT.rearrange("p c s -> p (c s)")[:, 0:LEVELS * P])
            dve.wait_ge(lb_e, 16 * 2 * L)
            dve.tensor_tensor(lb_tmp[:, 2], lb_raw[:, 0], lb_raw[:, 1], ALU.max).then_inc(setup_done, 1)
            dve.wait_ge(setup_done, 1)
            for l in range(L):
                i = dve.tensor_tensor(lb_tmp[:, l], lb_raw[:, l], lb_tmp[:, 2], ALU.subtract)
                i.then_inc(setup_done, 1)
            dve.wait_ge(setup_done, 3)
            dve.sem_inc(lb_x, 1)
            dve.wait_ge(lb_x, 2)
            dve.tensor_tensor(lb_tmp[:, 2], lb_tmp[:, 0], lb_tmp[:, 1], ALU.add).then_inc(setup_done, 1)
            dve.wait_ge(setup_done, 4)
            dve.reciprocal(lb_tmp[:, 3], lb_tmp[:, 2]).then_inc(setup_done, 1)
            dve.wait_ge(setup_done, 5)
            for l in range(L):
                dve.tensor_tensor(lb_tmp[:, l], lb_tmp[:, l], lb_tmp[:, 3], ALU.mult).then_inc(setup_done, 1)
            dve.wait_ge(setup_done, 7)
            dve.tensor_tensor(lb_tab[:, 0, 0], lb_tmp[:, 0], lb_tmp[:, 0], ALU.subtract).then_inc(setup_done, 1)
            dve.tensor_tensor(lb_tmp[:, 2], lb_tmp[:, 0], lb_tmp[:, 1], ALU.add).then_inc(setup_done, 1)
            dve.wait_ge(setup_done, 9)
            dve.tensor_tensor(lb_tab[:, 0, 1], lb_tmp[:, 2], lb_tmp[:, 0], ALU.subtract).then_inc(setup_done, 1)
            dve.memset(states[:, :, :, :], 0.0).then_inc(setup_done, 1)
            dve.wait_ge(setup_done, 11)
            dve.tensor_scalar(lb_tab[:, 1], lb_tab[:, 0], -1.0, 1.0, ALU.mult, ALU.add).then_inc(setup_done, 1)
            dve.wait_ge(setup_done, 12)

            with dve.Fori(0, L) as lay:
                steps[0] = 0
                st(dve.tensor_copy(lb[:, :, :], lb_tab[:, :, bass.ds(lay, 1), :].rearrange("p w l c -> p w (l c)")))
                settle()
                nrow = mqT.rearrange("p a s -> p (a s)").rearrange("p (t c) -> p t c", t=T)
                norm_rows(nrow, h, 1)
                dve.wait_ge(M["params"], 16 * N_PARAMS)
                R = slice(64, 96)
                ang, kk = mkT[R, 1], mkT[R, 2]
                st(dve.tensor_copy(ang, mkT[R, 0].bitcast(I32)))
                settle()
                st(dve.tensor_scalar(ang, ang, tb("invfreq")[R], None, ALU.mult))
                settle()
                TWO_PI = (6.28125, 0.0019340515136718750, 2 * np.pi - 6.28125 - 0.0019340515136718750)
                for dst, quarter in ((sinT[R], 0.0), (cosT[R], 0.25)):
                    st(dve.tensor_scalar(kk, ang, 1.0 / (2 * np.pi), quarter, ALU.mult, ALU.add))
                    settle()
                    st(dve.tensor_scalar(kk, kk, 12582912.0, None, ALU.add))
                    settle()
                    st(dve.tensor_scalar(kk, kk, 12582912.0, None, ALU.subtract))
                    settle()
                    src = ang
                    for part in TWO_PI:
                        st(dve.scalar_tensor_tensor(dst, kk, -float(part), src, ALU.mult, ALU.add))
                        settle()
                        src = dst
                    st(dve.tensor_scalar(dst, dst, float(np.pi / 2) if quarter else 0.0, 3.1415925, ALU.add, ALU.min))
                    settle()
                    st(dve.tensor_scalar(dst, dst, -3.1415925, None, ALU.max))
                    settle()
                dve.sem_inc(M["angles"], 1)
                dve.wait_ge(M["act_emptied"], emptied("f"))
                for ct in range(2):
                    st(dve.tensor_scalar(dl[:, ct], dl[:, ct], lb[:, 1, ct:ct + 1], lb[:, 0, ct:ct + 1], ALU.mult, ALU.add))
                settle()
                st(dve.tensor_scalar(flat(dl), flat(dl), 1e-6, 1.0, ALU.max, ALU.min))
                settle()
                dve.tensor_scalar(flat(kh), flat(dl), -1.0, 1.0, ALU.mult, ALU.add).then_inc(M["fgate"], 1)
                dve.wait_ge(M["sig_q"], 1)
                gone(dve.tensor_tensor(flat(qh), flat(ql), job("q")[:, :], ALU.mult))
                dve.wait_ge(M["logf"], 1)
                for ct in range(2):
                    st(dve.tensor_tensor_scan(bcum[:, ct], tb("restart"), dl[:, ct], 0.0, ALU.mult, ALU.add))
                dve.wait_ge(M["sig_g"], 1)
                gone(dve.tensor_tensor(flat(gate), flat(kl), job("g")[:, :], ALU.mult))
                settle()

                def differences(lv):
                    blk = 4 << lv
                    b4 = flat(bcum).rearrange("p (n k) -> p n k", k=blk)
                    d4 = flat(dl).rearrange("p (n k) -> p n k", k=blk)
                    ref = (blk - 1) if lv == 0 else blk // 2 - 1
                    r4 = b4[:, :, ref:ref + 1].broadcast_to([P, 2 * S // blk, blk])
                    if lv == 0:
                        dve.tensor_tensor(d4, b4, r4, ALU.subtract).then_inc(M["diff"], 1)
                    else:
                        st(dve.tensor_tensor(d4, b4, r4, ALU.subtract))
                        settle()
                        dve.scalar_tensor_tensor(flat(dl), flat(dl), -1.0, flat(dl), ALU.mult, ALU.min).then_inc(M["diff"], 1)

                def scale_level(lv):
                    dve.wait_ge(M["expdiff"], lv + 1)
                    if lv:
                        st(dve.tensor_tensor(flat(ql), flat(qh), flat(kl), ALU.mult))
                    else:
                        dve.wait_ge(M["act_step"], 3)
                        st(dve.tensor_tensor(flat(ql), flat(qh), flat(ql), ALU.mult))
                    settle()
                    dve.tensor_tensor(flat(kl), flat(kh), flat(kl), ALU.mult).then_inc(M["levels_ready"], 1)

                def keep_level(lv):
                    for odd in range(2):
                        o = job(f"lv{lv}{'eo'[odd]}")
                        gone(dve.copy_predicated(sacc[:, odd].rearrange("p t c s -> p (t c) s"),
                                                 lvmask[:, lv:lv + 1].broadcast_to([P, 4, P]),
                                                 o[:, :].rearrange("p (n s) -> p n s", n=4)))

                dve.wait_ge(M["dve_emptied"], emptied("g"))
                st(dve.memset(sacc[:, :, :, :, :], 0.0))
                differences(0)
                scale_level(0)
                keep_level(0)
                differences(1)
                scale_level(1)
                keep_level(1)
                differences(2)
                dve.wait_ge(M["act_emptied"], emptied("c"))
                gone(dve.tensor_tensor(flat(cu), flat(cu), job("hc")[:, :], ALU.mult))
                scale_level(2)
                keep_level(2)
                differences(3)
                dve.wait_ge(M["dve_emptied"], emptied("hc"))
                for ct in range(2):
                    st(dve.tensor_scalar(cy[:, ct], cu[:, ct], w_conv[:, 2, ct:ct + 1], None, ALU.mult))
                settle()
                for k in (1, 2):
                    for ct in range(2):
                        st(dve.scalar_tensor_tensor(cy[:, ct, k:], cu[:, ct, 0:S - k], w_conv[:, 2 - k, ct:ct + 1], cy[:, ct, k:], ALU.mult, ALU.add))
                    settle()
                dve.tensor_tensor(flat(cy), flat(cy), flat(cb), ALU.mult).then_inc(M["conv_yb"], 1)
                scale_level(3)
                keep_level(3)
                differences(4)
                scale_level(4)
                o = job("kvs")
                dve.wait_ge(M["rotary"], 1)
                dve.wait_ge(M["act_emptied"], emptied("kv"))
                st(dve.tensor_scalar(sinT[R], sinT[R], tb("sinsign")[R], None, ALU.mult))
                st(dve.tensor_tensor(mkT[R, 0], mkT[R, 0], cosT[R], ALU.mult))
                settle()
                gone(dve.tensor_tensor(mkT[R, 1], o[R, 0:S], sinT[R], ALU.mult))
                dve.wait_ge(M["dve_emptied"], emptied("kvs"))
                st(dve.tensor_tensor(mkT[R, 2], mkT[R, 0], mkT[R, 1], ALU.add))
                keep_level(4)
                dve.wait_ge(M["dve_emptied"], emptied("lv4o"))
                dve.sem_inc(M["scores_done"], 1)
                b4 = flat(bcum).rearrange("p (n k) -> p n k", k=CHUNK)
                st(dve.tensor_tensor(flat(dl).rearrange("p (n k) -> p n k", k=CHUNK),
                                     b4[:, :, CHUNK - 1:CHUNK].broadcast_to([P, 2 * S // CHUNK, CHUNK]), b4, ALU.subtract))
                settle()
                dve.sem_inc(M["qk_state"], 1)
                dve.wait_ge(M["lat_rstd"], 1)
                for c in range(3):
                    i = dve.scalar_tensor_tensor(lat[:, c], lat[:, c], g_lat[:, c:c + 1], mkT[:, 4 if c < 2 else 5], ALU.mult, ALU.mult)
                    st(i)
                settle()
                dve.sem_inc(M["lat_ready"], 1)
                for k in (0, 1):
                    st(dve.tensor_copy(mkT[R, k], mkT[R, 2]))
                st(dve.tensor_copy(mkT[R, 3:8], mkT[R, 2:3].broadcast_to([ROPE, 5, S])))
                settle()
                dve.sem_inc(M["mla_k"], 1)
                dve.wait_ge(M["expdiff"], 6)
                st(dve.tensor_copy(small[:, 48:56].rearrange("p (c n) -> p c n", c=2), ql[:, :, CHUNK - 1::CHUNK]))
                settle()
                st(dve.tensor_tensor(flat(kl), flat(kh), flat(kl), ALU.mult))
                settle()
                dve.sem_inc(M["ktok_scaled"], 1)
                st(dve.tensor_tensor(flat(ql), flat(qh), flat(ql), ALU.mult))
                o0, o1 = job("u0"), job("u1")

                def diag(x, pair, odd):
                    return x[64 * odd:64 * odd + 64, pair * P + 64 * odd:pair * P + 64 * odd + 64]

                for odd in range(2):
                    for pair in range(2):
                        lo = slice(64 * odd, 64 * odd + 64)
                        st(dve.tensor_copy(states[lo, 0, pair, lo], diag(o0, pair, odd)))
                for ch, (o, off) in ((1, (o1, 0)), (2, (o0, 2))):
                    settle()
                    for odd in range(2):
                        for pair in range(2):
                            lo = slice(64 * odd, 64 * odd + 64)
                            st(dve.scalar_tensor_tensor(states[lo, ch, pair, lo], states[lo, ch - 1, pair, lo],
                                                        small[lo, 48 + 4 * pair + ch:49 + 4 * pair + ch], diag(o, pair + off, odd), ALU.mult, ALU.add))
                settle()
                dve.sem_inc(M["dve_emptied"], 2)
                dve.sem_inc(M["state_ready"], 1)
                dve.wait_ge(M["pe_job"], INDEX["kvs"] + 1)
                dve.wait_ge(M["conv_rstd"], 1)
                for ct in range(2):
                    st(dve.scalar_tensor_tensor(uT[:, 2 + ct], cy[:, ct], g_conv[:, ct:ct + 1], cb[:, ct], ALU.mult, ALU.mult))
                settle()
                dve.sem_inc(M["mixed"], 1)
                dve.wait_ge(M["act_emptied"], emptied("o_in"))
                o = job("o_st")
                dv = dl[:, :, CHUNK:S]
                gone(dve.tensor_tensor(dv, dv, o[:, :].rearrange("p (c s) -> p c s", c=2)[:, :, CHUNK:S], ALU.add))
                dve.wait_ge(M["dve_emptied"], emptied("o_st"))
                dve.sem_inc(M["o_sum"], 1)
                st(dve.scalar_tensor_tensor(flat(gate), flat(gate), g_hgrn[:, 0:1], flat(dl), ALU.mult, ALU.mult))
                settle()
                dve.wait_ge(M["hg_rstd"], 1)
                st(dve.tensor_tensor(flat(uT[:, 0:2]), flat(gate), flat(ql), ALU.mult))
                settle()
                dve.sem_inc(M["mixed"], 1)
                for n in range(4):
                    dve.wait_ge(M["act_emptied"], emptied(f"mq{n}"))
                    o = job(f"mqs{n}")
                    q = mqT[R, 2 * n:2 * n + 2]
                    tmp = dl[R]
                    st(dve.tensor_tensor(q, q, cosT[R].unsqueeze(1).broadcast_to([ROPE, 2, S]), ALU.mult))
                    gone(dve.tensor_tensor(tmp, o[R, :].rearrange("p (c s) -> p c s", c=2), sinT[R].unsqueeze(1).broadcast_to([ROPE, 2, S]), ALU.mult))
                    settle()
                    dve.wait_ge(M["dve_emptied"], emptied(f"mqs{n}"))
                    st(dve.tensor_tensor(q, q, tmp, ALU.add))
                    settle()
                dve.sem_inc(M["mla_q"], 1)
                for t, mp in enumerate((mp0, mp1)):
                    keys = P * (t + 1)
                    per = 4 if t == 0 else 2
                    for n in range(2 if t == 0 else 4):
                        o = job(f"ms{n if t == 0 else 2 + n}")[:, :].rearrange("p (k s) -> p k s", k=per)
                        dst = mp[:, n * per:(n + 1) * per]
                        st(dve.tensor_scalar(dst[:, :, 0:keys - 64], o[:, :, 0:keys - 64], QK ** -0.5, None, ALU.mult))
                        dve.wait_ge(M["dve_step"], steps[0])
                        gone(dve.tensor_scalar(dst[:, :, keys - 64:keys], o[:, :, keys - 64:keys], QK ** -0.5, tb("chunkmask"), ALU.mult, ALU.add))
                    dve.wait_ge(M["dve_emptied"], emptied(f"ms{1 if t == 0 else 5}"))
                    st(dve.tensor_reduce(small[:, 8 * t:8 * t + 8], mp[:, :, :], AX.X, ALU.max))
                    settle()
                    dve.tensor_scalar(small[:, 8 * t:8 * t + 8], small[:, 8 * t:8 * t + 8], -1.0, None, ALU.mult).then_inc(M["mla_neg"], 1)
                for t, mp in enumerate((mp0, mp1)):
                    dve.wait_ge(M["mla_exp"], 8 * (t + 1))
                    st(dve.reciprocal(small[:, 32 + 8 * t:40 + 8 * t], small[:, 16 + 8 * t:24 + 8 * t]))
                    settle()
                    dve.tensor_tensor(mp[:, :, :], mp[:, :, :], small[:, 32 + 8 * t:40 + 8 * t].unsqueeze(2).broadcast_to([P, MH, P * (t + 1)]),
                                      ALU.mult).then_inc(M["mla_p"], 1)
                dve.wait_ge(M["mla_rstd"], 2)
                for ct in range(4):
                    st(dve.scalar_tensor_tensor(uT[:, 4 + ct], mqT[:, ct], g_out[:, ct:ct + 1], mkT[:, ct], ALU.mult, ALU.mult))
                settle()
                dve.sem_inc(M["mixed"], 1)
                add_rows(dve, job, gone, "out", h, M)

                norm_rows(qT.rearrange("p a s -> p (a s)").rearrange("p (t c) -> p t c", t=T), h, 2)
                norm_rows_in_place(oT.rearrange("p a s -> p (a s)").rearrange("p (t c) -> p t c", t=T),
                                   pr.rearrange("p t h s -> p t (h s)"), 3)
                for n in range(2):
                    for t in range(T):
                        gone(dve.tensor_copy(vv[:, t, 512 * n:512 * n + 512], job(f"xv{2 * n + t}")[:, :]))
                for n in range(4):
                    o = job(f"xs{n}")
                    st(dve.tensor_reduce(xsm[:, 2 * n:2 * n + 2], o[:, :].rearrange("p (k s) -> p k s", k=2), AX.X, ALU.max))
                    settle()
                    dve.tensor_scalar(xsm[:, 2 * n:2 * n + 2], xsm[:, 2 * n:2 * n + 2], -XD ** -0.5, None, ALU.mult).then_inc(M["x_max"], 1)
                for t in range(T):
                    dve.wait_ge(M["x_exp"], 4 * (t + 1))
                    st(dve.reciprocal(xsm[:, 16 + 4 * t:20 + 4 * t], xsm[:, 8 + 4 * t:12 + 4 * t]))
                    settle()
                    dve.tensor_tensor(pr[:, t], pr[:, t], xsm[:, 16 + 4 * t:20 + 4 * t].unsqueeze(2).broadcast_to([P, XH, S]), ALU.mult).then_inc(M["x_p"], 1)
                for n in range(4):
                    gone(dve.tensor_copy(oT[:, 2 * n:2 * n + 2].rearrange("p c s -> p (c s)"), job(f"xo{n}")[:, :]))
                add_rows(dve, job, gone, "xout", h, M)

                norm_rows(hn.rearrange("p t c k -> p t (c k)"), h, 4)
                o = job("router")
                gone(dve.tensor_tensor(lg[:, :, :], o[:, 0:128].rearrange("p (t n) -> p t n", t=T)[:, :, 0:NG + NE],
                                       b_rout[:, :].unsqueeze(1).broadcast_to([P, T, NG + NE]), ALU.add))
                dve.wait_ge(M["dve_emptied"], emptied("router"))

                def seg(x, *shape):
                    n = int(np.prod(shape))
                    v = rt[:, x:x + n]
                    return v if len(shape) == 1 else v.rearrange("p (a b) -> p a b", a=shape[0])

                def one_hot(dst, x, top, n, tmp, low):
                    st(dve.tensor_reduce(top, x, AX.X, ALU.max))
                    settle()
                    bt = top.unsqueeze(2).broadcast_to([P, T, n])
                    st(dve.tensor_tensor(tmp, x, bt, ALU.is_equal))
                    st(dve.tensor_scalar(dst, tb("iota8")[:, 0:n].unsqueeze(1).broadcast_to([P, T, n]), -8.0, None, ALU.add))
                    settle()
                    st(dve.tensor_tensor(tmp, tmp, dst, ALU.mult))
                    settle()
                    st(dve.tensor_reduce(low, tmp, AX.X, ALU.min))
                    settle()
                    st(dve.tensor_tensor(dst, dst, low.unsqueeze(2).broadcast_to([P, T, n]), ALU.is_equal))
                    settle()

                oh_g, tmp4, top_g, low = seg(0, T, NG), seg(16, T, NG), seg(24, T), seg(26, T)
                gl = lg[:, :, 0:NG]
                one_hot(oh_g, gl, top_g, NG, tmp4, low)
                st(dve.tensor_tensor(seg(8, T, NG), gl, top_g.unsqueeze(2).broadcast_to([P, T, NG]), ALU.subtract))
                settle()
                dve.sem_inc(M["r_exp"], 1)
                picked = seg(160, T * NG, EG)
                for t in range(T):
                    st(dve.tensor_tensor(picked[:, t * NG:(t + 1) * NG], lg[:, t, NG:].rearrange("p (g e) -> p g e", g=NG),
                                         oh_g[:, t].unsqueeze(2).broadcast_to([P, NG, EG]), ALU.mult))
                settle()
                own = seg(32, T, EG)
                st(dve.tensor_reduce(own, picked.rearrange("p (t g) e -> p t e g", t=T), AX.X, ALU.add))
                settle()
                oh1, oh2, tmp8, top1, top2 = seg(48, T, EG), seg(64, T, EG), seg(80, T, EG), seg(28, T), seg(30, T)
                one_hot(oh1, own, top1, EG, tmp8, low)
                rest = seg(96, T, EG)
                st(dve.scalar_tensor_tensor(rest, oh1, -1e30, own, ALU.mult, ALU.add))
                settle()
                one_hot(oh2, rest, top2, EG, tmp8, low)
                st(dve.tensor_tensor(rt[:, 128:130], top2, top1, ALU.subtract))
                settle()
                dve.sem_inc(M["r_exp"], 1)
                dve.wait_ge(M["r_exp_e"], 1)
                st(dve.tensor_reduce(rt[:, 130:132], seg(8, T, NG), AX.X, ALU.add))
                dve.wait_ge(M["r_exp_e"], 2)
                st(dve.tensor_scalar(rt[:, 132:134], rt[:, 128:130], 1.0, None, ALU.add))
                settle()
                st(dve.tensor_tensor(rt[:, 134:136], rt[:, 130:132], rt[:, 132:134], ALU.mult))
                settle()
                w1, w2 = rt[:, 136:138], rt[:, 138:140]
                st(dve.reciprocal(w1, rt[:, 134:136]))
                settle()
                st(dve.tensor_tensor(w2, w1, rt[:, 128:130], ALU.mult))
                settle()
                both, cw = seg(96, T, EG), seg(112, T, EG)
                st(dve.tensor_tensor(both, oh1, oh2, ALU.add))
                st(dve.tensor_tensor(cw, oh1, w1.unsqueeze(2).broadcast_to([P, T, EG]), ALU.mult))
                st(dve.tensor_tensor(tmp8, oh2, w2.unsqueeze(2).broadcast_to([P, T, EG]), ALU.mult))
                settle()
                st(dve.tensor_tensor(cw, cw, tmp8, ALU.add))
                settle()
                for t in range(T):
                    ohb = oh_g[:, t].unsqueeze(2).broadcast_to([P, NG, EG])
                    for dst, src in ((chosen, both), (combine, cw)):
                        st(dve.tensor_tensor(dst[:, t].rearrange("p (g e) -> p g e", g=NG), ohb,
                                             src[:, t:t + 1].broadcast_to([P, NG, EG]), ALU.mult))
                settle()
                dve.sem_inc(M["r_chosen"], 1)
                o = job("places")
                st(dve.scalar_tensor_tensor(place.rearrange("p t e -> p (t e)"), o[:, 0:2 * NE], 1e6, chosen.rearrange("p t e -> p (t e)"), ALU.add, ALU.mult))
                gone(dve.tensor_reduce(rounds_f[:, :], o[:, 2 * NE:3 * NE], AX.X, ALU.max))
                settle()
                st(dve.tensor_scalar(place[:, :, :], place[:, :, :], 1e6, None, ALU.subtract))
                dve.wait_ge(M["dve_emptied"], emptied("places"))
                st(dve.tensor_tensor(rt[:, 0:8], rounds_f[:, 0:1].broadcast_to([P, 8]), tb("thresholds"), ALU.is_gt))
                settle()
                st(dve.tensor_reduce(rounds_f[:, :], rt[:, 0:8], AX.X, ALU.add))
                settle()
                dve.wait_ge(sp_took, lay + 1)
                dve.tensor_copy(rounds_i[:, :], rounds_f[:, :]).then_inc(M["rounds"], 1)
                dve.wait_ge(M["rounds"], 1)
                dve.sem_inc(sp_rounds, 1)
                dve.sem_inc(M["added"], 1)
                r = dve.value_load(rounds_i[0:1, 0:1], min_val=1, max_val=8)
                with dve.Fori(0, r) as rnd:
                    with dve.Fori(0, MOE_STEPS) as j:
                        step = rnd * MOE_STEPS + j
                        ne = QUADS_PER_STEP * QUAD
                        for t in range(T):
                            dve.tensor_tensor(sel[:, t], place[:, t, bass.ds(j * ne, ne)].unsqueeze(2).broadcast_to([P, ne, SLOTS]),
                                              tb("iota32").unsqueeze(1).broadcast_to([P, ne, SLOTS]), ALU.is_equal).then_inc(M["sel_written"], 1)
                        dve.wait_ge(M["sel_written"], step * 2 + 2)
                        for t in range(T):
                            i = dve.tensor_tensor(comb[:, t], sel[:, t], combine[:, t, bass.ds(j * ne, ne)].unsqueeze(2).broadcast_to([P, ne, SLOTS]), ALU.mult)
                            if t == T - 1:
                                i.then_inc(M["slots"], 1)
                        for g in range(QUADS_PER_STEP):
                            q = step * QUADS_PER_STEP + g
                            for half in range(2):
                                dve.wait_ge(M["m_gather"], q * 4 + (half + 1))
                                dve.tensor_tensor(xT[:, 4 * half:4 * half + 4], bank[half][:, :].rearrange("p (c s) -> p c s", c=4),
                                                  gains[:, 3, 4 * half:4 * half + 4].unsqueeze(2).broadcast_to([P, 4, P]), ALU.mult).then_inc(M["xt_ready"], 1)
                            dve.wait_ge(M["silu"], q + 1)
                            dve.wait_ge(M["m_up"], q * 4 + 4)
                            dve.tensor_tensor(hid[:, :], sg[:, :], bank[2 + g % 2][:, FE:2 * FE], ALU.mult).then_inc(M["hid_ready"], 1)
                            dve.wait_ge(M["m_down"], q * 2 + 2)
                            dve.tensor_copy(yy[:, 512:1024], bank[5][:, :]).then_inc(M["yv_ready"], 1)
                            for t in range(T):
                                for n in range(2):
                                    k = 2 * t + n
                                    dve.wait_ge(M["m_scatter"], q * 4 + (k + 1))
                                    dve.wait_ge(M["added"], q * 4 + (k + 1))
                                    hx = h[:, t, 512 * n:512 * n + 512]
                                    dve.tensor_tensor(hx, hx, bank[6 + n][:, :], ALU.add).then_inc(M["added"], 1)
                    dve.tensor_scalar(place[:, :, :], place[:, :, :], float(SLOTS), None, ALU.subtract).then_inc(M["places_moved"], 1)
                    dve.wait_ge(M["places_moved"], rnd + 1)
                dve.wait_ge(M["arrived"], 3)
                dve.sem_clear(per_layer_range)
                dve.sem_inc(released, 1)
            steps[0] = 0
            mean_square(1)
            refine(1)
            dve.wait_ge(M["params"], 16)
            for t in range(T):
                dve.scalar_tensor_tensor(h[:, t], h[:, t], rs[:, t:t + 1], frow[:, :], ALU.mult, ALU.mult).then_inc(M["normed"], 1)

        @block.gpsimd
        def _(pool):
            ring_at = pool.alloc_register("ring_at")
            pool.reg_mov(ring_at, 0)
            half = ROPE // 2
            with pool.Fori(0, L) as lay:
                pool.wait_ge(M["act_emptied"], emptied("mix_xt0"))
                base = pool.snap(ring_at)
                for n in (4, 5):
                    pool.wait_ge(unit_in[n], base + LOADED)
                    pool.sem_inc(pool_saw, 1)
                    if n == 4:
                        src = ring[4][:, 0:KC * 160].rearrange("p (c n) -> p c n", c=KC)[:, :, 128:160]
                        for k in range(2):
                            i = pool.tensor_copy(w_kps[:, :, k * half:(k + 1) * half], src[:, :, (1 - k) * half:(2 - k) * half])
                    else:
                        src = ring[5][:, 0:1536].rearrange("p (c h n) -> p c h n", c=2, h=MH)
                        for c in range(2):
                            for k in range(2):
                                i = pool.tensor_copy(w_uqs[:, c, :, k * half:(k + 1) * half], src[:, c, :, NOPE + (1 - k) * half:NOPE + (2 - k) * half])
                    i.then_inc(M["swapped"], 1)
                pool.wait_ge(M["rounds"], 1)
                r = pool.value_load(rounds_i[0:1, 0:1], min_val=1, max_val=8)
                pool.reg_add(ring_at, ring_at, LOADED * FIXED_UNITS // RING)
                with pool.Fori(0, r):
                    pool.reg_add(ring_at, ring_at, MOE_STEPS * LOADED * STEP_UNITS // RING)
                pool.sem_inc(M["arrived"], 1)
                pool.wait_ge(released, lay + 1)


def group_rstd_done(act, job, name, dst, n, M, tick, settle, tb, done):
    o = job(name)
    act.activation(dst, o[:, :], ACT.Ln, bias=tb("eps"), scale=1.0 / n).then_inc(M["act_emptied"], 1)
    act.wait_ge(M["act_emptied"], emptied(name))
    act.activation(dst, dst, ACT.Exp, scale=-0.5).then_inc(done, 1)


def add_rows(dve, job, gone, prefix, h, M):
    for n in range(2):
        for t in range(T):
            hx = h[:, t, 512 * n:512 * n + 512]
            gone(dve.tensor_tensor(hx, hx, job(f"{prefix}{2 * n + t}")[:, :], ALU.add))
    dve.wait_ge(M["dve_emptied"], emptied(f"{prefix}3"))


N_PARAMS = 4 + 2 * 6 + 4 + 1 + 1 + 1 + NG + 2

_INS = ["x", "mem", "positions", "norm_mix", "w_in", "hgrn_lower_bounds", "hgrn_norm", "conv_w", "conv_norm",
        "mla_q_norm", "mla_w_uq", "mla_kv_norm", "mla_w_ukv", "mla_out_norm", "w_out", "norm_cross", "norm_mem",
        "xa_wq", "xa_wk", "xa_wv", "xa_wo", "norm_ffn", "router_group_w", "router_group_b", "router_expert_w",
        "router_expert_b", "expert_w_gate", "expert_w_up", "expert_w_down", "final_norm"]


def kernel(**inputs):
    import numpy as _np
    import concourse.bacc as _bacc
    from concourse import mybir as _mybir
    from concourse.bass_utils import run_bass_kernel_spmd as _run

    nc = _bacc.Bacc("TRN2", target_bir_lowering=False, num_devices=1)
    arrays, aps = {}, {}
    tables, level_masks = shape_tables()
    given = {n: inputs[n] for n in _INS}
    given["tables"], given["level_masks"] = tables, level_masks
    for name, x in given.items():
        x = _np.ascontiguousarray(x)
        arrays[f"in_{name}"] = x
        aps[name] = nc.dram_tensor(f"in_{name}", x.shape, _mybir.dt.from_np(x.dtype), kind="ExternalInput").ap()
    out = nc.dram_tensor("out_rows", (1, S, D), _mybir.dt.float32, kind="ExternalOutput").ap()
    hybrid_trunk(nc, aps.pop("tables"), aps.pop("level_masks"), aps, out)
    r = _run(nc, [arrays], core_ids=[0])
    return r.results[0]["out_rows"]
```

```python
from contextlib import ExitStack

import numpy as np

import concourse.bass as bass
from concourse import mybir

F32 = mybir.dt.float32
I32 = mybir.dt.int32
U8 = mybir.dt.uint8
ALU = mybir.AluOpType
ACT = mybir.ActivationFunctionType
AX = mybir.AxisListType

P = 128
L = 2
S = 256
D = 1024
T = S // P
KC = D // P
CHUNK = 64
EPS = 1e-6
DIN = 2208
HH, HD = 4, 64
MH, NOPE, ROPE, MV = 8, 64, 32, 64
QK = NOPE + ROPE
XH, XD = 4, 256
NG, EG = 4, 8
NE = NG * EG
FE = 256
SLOTS = 32
QUAD = 4
RING = 6
UNIT = 4096
LEVELS = 5
UNIT_DMAS = 2
LOADED = 16 * UNIT_DMAS
UNITS = [("xk0", "xa_wk", 0, 512, "(p c)"), ("in_fq", "w_in", 0, 512, "(p c)"), ("in_ig", "w_in", 512, 1024, "(p c)"),
         ("xk2", "xa_wk", 512, 768, "(p c)"), ("in_bc", "w_in", 1024, 1536, "(p c)"),
         ("in_hq", "w_in", 1536, 2048, "(p c)"), ("in_kv", "w_in", 2048, DIN, "(p c)"),
         ("xk3", "xa_wk", 768, 1024, "(p c)"), ("uq", "mla_w_uq", 0, 768, None), ("ukv", "mla_w_ukv", 0, 1024, None),
         ("xv0", "xa_wv", 0, 512, "(p c)"), ("xv1", "xa_wv", 512, 1024, "(p c)"),
         ("out0", "w_out", 0, 512, "(c p)"), ("out1", "w_out", 512, 1024, "(c p)"),
         ("xq0", "xa_wq", 0, 512, "(p c)"), ("xq1", "xa_wq", 512, 1024, "(p c)"),
         ("xout0", "xa_wo", 0, 512, "(c p)"), ("xout1", "xa_wo", 512, 1024, "(c p)")]
UNIT_NUMBER = {unit[0]: n for n, unit in enumerate(UNITS)}
FIXED_UNITS = len(UNITS)
assert FIXED_UNITS % RING == 0
QUADS_PER_STEP = 4
UNITS_PER_QUAD = 6
STEP_UNITS = QUADS_PER_STEP * UNITS_PER_QUAD
assert STEP_UNITS % RING == 0
MOE_STEPS = NE // QUAD // QUADS_PER_STEP

TABLES = {}
_at = 0
for _name, _w in [("ident", P), ("ones", P), ("blk64", P), ("before", P), ("restart", S),
                  ("iota32", SLOTS), ("iota8", 8), ("thresholds", 8), ("chunkmask", 1), ("invfreq", 1),
                  ("sinsign", 1), ("eps", 1)]:
    TABLES[_name] = (_at, _w)
    _at += _w
TABLE_W = _at

PARAMS = {}
_at = 0
for _name, _w in [("gains", 4 * KC), ("g_hgrn", 1), ("g_conv", 2), ("g_lat", 3), ("g_out", 4), ("w_conv", 6), ("lb_raw", 2)]:
    PARAMS[_name] = (_at, _w)
    _at += _w
PARAM_W = _at
LN_EXP_TABLES, SILU_TABLES = 6, 18


def shape_tables():
    t = np.zeros((P, TABLE_W), np.float32)
    i = np.arange(P)

    def put(name, value):
        a, w = TABLES[name]
        t[:, a:a + w] = value

    put("ident", np.eye(P))
    put("ones", 1.0)
    put("blk64", (i[:, None] // 64 == i[None] // 64))
    put("before", i[:, None] < i[None])
    put("restart", (np.arange(S) % CHUNK != 0)[None])
    put("iota32", np.arange(SLOTS)[None])
    put("iota8", np.arange(8)[None])
    put("thresholds", SLOTS * np.arange(8)[None])
    put("chunkmask", np.where(i < CHUNK, -1e30, 0.0)[:, None])
    half = ROPE // 2
    freq = np.float32(10000.0) ** (-np.arange(half, dtype=np.float32) * np.float32(2.0) / np.float32(ROPE))
    put("invfreq", freq[i % half][:, None])
    put("sinsign", np.where(i % ROPE < half, -1.0, 1.0)[:, None])
    put("eps", EPS)
    m = np.zeros((P, LEVELS, P), np.float32)
    s, q = i[:, None], i[None]
    m[:, 0] = (s // 4 == q // 4) & (s <= q)
    for lv in range(1, LEVELS):
        b = 4 << lv
        m[:, lv] = (s // b == q // b) & (s % b < b // 2) & (q % b >= b // 2)
    return t, m.reshape(P, LEVELS * P)


JOBS = [("xk0", "A"), ("xk1", "A")] + [(f"mix_xt{n}", "A") for n in range(4)]
JOBS += [("f", "A"), ("q", "V"), ("i", "A"), ("g", "V"), ("xk2", "A"), ("lv0e", "V"), ("lv0o", "V"),
         ("b", "A"), ("lv1e", "V"), ("lv1o", "V"), ("c", "A"), ("lv2e", "V"), ("lv2o", "V"),
         ("hc", "V"), ("lv3e", "V"), ("lv3o", "V"), ("cq", "A"), ("lv4e", "V"), ("lv4o", "V"),
         ("kv", "A"), ("kvs", "V"), ("xk3", "A"), ("latss", "A"), ("ktok", "A"), ("u0", "V"), ("u1", "V"), ("convss", "A"),
         ("o_in", "A"), ("o_st", "V"), ("hgss", "A")]
JOBS += [(f"mq{n}", "A") for n in range(4)] + [(f"mqs{n}", "V") for n in range(4)]
JOBS += [(f"mk{n}", "A") for n in range(4)] + [("mv0", "A"), ("mv1", "A"), ("xv0", "A")]
JOBS += [(f"ms{n}", "V") for n in range(6)] + [("xv1", "A"), ("mt0", "A"), ("mt1", "A"), ("xv2", "A")]
JOBS += [(f"mt{n}", "A") for n in range(2, 6)]
JOBS += [("mo0", "A"), ("mo1", "A"), ("mss0", "A"), ("mss1", "A"), ("xv3", "A")] + [(f"out{n}", "V") for n in range(4)]
JOBS += [(f"cross_xt{n}", "A") for n in range(4)] + [(f"xq{n}", "A") for n in range(4)]
JOBS += [(f"xs{n}", "A") for n in range(4)]
JOBS += [(f"xt{n}", "A") for n in range(4)] + [(f"xo{n}", "V") for n in range(4)]
JOBS += [(f"xout{n}", "V") for n in range(4)]
JOBS += [(f"ffn_xt{n}", "A") for n in range(4)] + [("router", "V"), ("places", "V")]
INDEX = {name: n for n, (name, _) in enumerate(JOBS)}


def emptied(name):
    n = INDEX[name]
    return sum(c == JOBS[n][1] for _, c in JOBS[:n + 1])


def hybrid_trunk(nc, tables, level_masks, a, out):
    with ExitStack() as ctx:
        def sb(name, shape, dt=F32, stack=ctx):
            return stack.enter_context(nc.sbuf_tensor(name, shape, dt))

        def sem(name):
            return ctx.enter_context(nc.semaphore(name))

        ring = [sb(f"ring{n}", [P, UNIT]) for n in range(RING)]
        h = sb("h", [P, T, D])
        uT = sb("uT", [P, KC, S])
        tab = sb("tab", [P, TABLE_W])
        lvmask = sb("lvmask", [P, LEVELS, P], U8)
        states = sb("states", [P, 3, 2, P])
        memN = sb("memN", [P, KC, S])
        mT = sb("mT", [P, KC, S])
        kT = sb("kT", [P, KC, S])
        vv = sb("vv", [P, T, D])
        ptab = sb("ptab", [P, L, PARAM_W])
        par = sb("par", [P, PARAM_W])
        w_rout = sb("w_rout", [P, KC, NG + NE])
        b_rout = sb("b_rout", [P, NG + NE])
        cosT = sb("cosT", [P, S])
        sinT = sb("sinT", [P, S])

        def pm(name):
            x, w = PARAMS[name]
            return par[:, x:x + w]

        gains = pm("gains").rearrange("p (g c) -> p g c", g=4)
        g_hgrn, g_conv, g_lat, g_out = pm("g_hgrn"), pm("g_conv"), pm("g_lat"), pm("g_out")
        w_conv = pm("w_conv").rearrange("p (t c) -> p t c", t=3)
        lb_raw = ptab[:, :, PARAMS["lb_raw"][0]:PARAM_W]
        lb_tab = sb("lb_tab", [P, 2, L, 2])
        lb = sb("lb", [P, 2, 2])
        lb_tmp = sb("lb_tmp", [P, 4, 2])
        ss = sb("ss", [P, 2])
        ms = sb("ms", [P, 2])
        rs0 = sb("rs0", [P, 2])
        rs = sb("rs", [P, 2])
        nt = sb("nt", [P, 2])
        rounds_f = sb("rounds_f", [P, 1])
        rounds_i = sb("rounds_i", [P, 1], I32)

        def tb(name):
            x, w = TABLES[name]
            return tab[:, x:x + w]

        with ExitStack() as st:
            mqT = sb("mqT", [P, MH, S], F32, st)
            mkT = sb("mkT", [P, MH, S], F32, st)
            mV = sb("mV", [P, T, MH * MV], F32, st)
            hg2 = sb("hg2", [P, 4, S], F32, st)
            qh, bcum = hg2[:, 0:2], hg2[:, 2:4]
            mpt0 = hg2.rearrange("p a (b s) -> p (a b) s", b=2)
            kh = sb("kh", [P, 2, S], F32, st)
            ih = sb("ih", [P, T, S], F32, st)
            gate = sb("gate", [P, 2, S], F32, st)
            small = sb("small", [P, 64], F32, st)
            with ExitStack() as s1:
                lat = sb("lat", [P, 3, S], F32, s1)
                w_uqs = sb("w_uqs", [P, 2, MH, ROPE], F32, s1)
                w_kps = sb("w_kps", [P, KC, ROPE], F32, s1)
                cb = sb("cb", [P, 2, S], F32, s1)
                cu = sb("cu", [P, 2, S], F32, s1)
                cy = sb("cy", [P, 2, S], F32, s1)
                dl = sb("dl", [P, 2, S], F32, s1)
                ql = sb("ql", [P, 2, S], F32, s1)
                kl = sb("kl", [P, 2, S], F32, s1)
                sacc = sb("sacc", [P, 2, T, 2, P], F32, s1)
            ktok = mqT[:, 4:6].rearrange("p t (c s) -> p t c s", c=2)
            with ExitStack() as s1:
                mp0 = sb("mp0", [P, MH, P], F32, s1)
                mp1 = sb("mp1", [P, MH, S], F32, s1)
                mpt1 = sb("mpt1", [P, 2, MH, P], F32, s1)
        with ExitStack() as st:
            qT = sb("qT", [P, KC, S], F32, st)
            pr = sb("pr", [P, T, XH, S], F32, st)
            pT = sb("pT", [P, T, XH, S], F32, st)
            oT = sb("oT", [P, KC, S], F32, st)
            xsm = sb("xsm", [P, 64], F32, st)
        with ExitStack() as st:
            hn = sb("hn", [P, T, KC, P], F32, st)
            sel = sb("sel", [P, T, QUADS_PER_STEP * QUAD, SLOTS], F32, st)
            comb = sb("comb", [P, T, QUADS_PER_STEP * QUAD, SLOTS], F32, st)
            xT = sb("xT", [P, KC, P], F32, st)
            cT = sb("cT", [P, T, P], F32, st)
            sg = sb("sg", [P, FE], F32, st)
            hid = sb("hid", [P, FE], F32, st)
            hidT = sb("hidT", [P, 2, P], F32, st)
            yy = sb("yy", [P, D], F32, st)
            lg = sb("lg", [P, T, NG + NE], F32, st)
            combine = sb("combine", [P, T, NE], F32, st)
            chosen = sb("chosen", [P, T, NE], F32, st)
            place = sb("place", [P, T, NE], F32, st)
            rt = sb("rt", [P, 256], F32, st)
            frow = sb("frow", [P, D], F32, st)
        bank = [ctx.enter_context(nc.psum_tensor(f"bank{n}", [P, 512], F32)) for n in range(8)]

        per_layer = ["params", "pe_job", "act_emptied", "dve_emptied", "act_step", "dve_step", "sumsq", "meansq",
                     "rstd0", "normed", "par_ready", "sig_q", "sig_g", "fgate", "logf", "bcum_ready", "diff",
                     "expdiff", "levels_ready", "qk_state", "ktok_scaled", "state_ready", "scores_done",
                     "o_sum", "hg_sq", "hg_rstd",
                     "conv_yb", "conv_sq", "conv_rstd", "lat_sq", "lat_rstd", "lat_ready", "swapped",
                     "mixed", "mla_k", "mla_q", "mla_neg", "mla_exp", "mla_p", "mla_osq", "mla_rstd",
                     "gained", "x_max", "x_exp", "x_p", "r_exp", "r_exp_e", "r_chosen",
                     "rounds", "slots", "places_moved", "m_gather", "m_up", "m_down", "m_scatter", "xt_ready", "ct_ready",
                     "silu", "hid_ready", "hidT_ready", "ya_ready", "yv_ready", "added", "sel_written", "arrived"]
        M = {n: sem(n) for n in per_layer}
        nums = [M[n].num for n in per_layer]
        assert nums == list(range(nums[0], nums[0] + len(nums)))
        per_layer_range = range(nums[0], nums[-1] + 1)
        released = sem("released")
        unit_in = [sem(f"unit_in{n}") for n in range(RING)]
        unit_free = sem("unit_free")
        mem_in = sem("mem_in")
        x_in = sem("x_in")
        tables_in = sem("tables_in")
        params_in = sem("params_in")
        masks_in = sem("masks_in")
        positions_in = sem("positions_in")
        mem_sumsq = sem("mem_sumsq")
        mem_meansq = sem("mem_meansq")
        mem_step = sem("mem_step")
        mem_rstd = sem("mem_rstd")
        mem_normed = sem("mem_normed")
        mem_turned = sem("mem_turned")
        mem_kept = sem("mem_kept")
        rope_step = sem("rope_step")
        angles = sem("angles")
        rotary = sem("rotary")
        rotary_ready = sem("rotary_ready")
        lb_x = sem("lb_x")
        setup_done = sem("setup_done")
        sp_rounds = sem("sp_rounds")
        sp_took = sem("sp_took")
        sp_saw = sem("sp_saw")
        pool_saw = sem("pool_saw")
        stored = sem("stored")

        def cols(w, n0, n1, rows="(p c)"):
            return w[:, :, n0:n1].rearrange(f"l {rows} n -> l p c n", p=P)

        gate_w = a["expert_w_gate"].rearrange("l e (p c) f -> (l e) p (c f)", p=P)
        up_w = a["expert_w_up"].rearrange("l e (p c) f -> (l e) p (c f)", p=P)
        down_w = a["expert_w_down"].rearrange("l e (c p) n -> (l e) p c n", p=P)

        block = ctx.enter_context(nc.Block())

        @block.sync
        def _(sp):
            issued = sp.alloc_register("issued")
            sp.reg_mov(issued, 0)
            sp.dma_start(kT.rearrange("p c s -> p (c s)").rearrange("p (t d) -> p t d", t=T),
                         a["mem"].rearrange("b (t p) d -> p (b t) d", p=P)).then_inc(mem_in, 16)
            sp.dma_start(tab[:, :], tables[:, :]).then_inc(tables_in, 16)
            sp.dma_start(h[:, :, :], a["x"].rearrange("b (t p) d -> p (b t) d", p=P)).then_inc(x_in, 16)
            sp.sem_inc(sp_took, 1)

            def unit(base, n, slot, first, second):
                sp.wait_ge(unit_free, base + (n + 1))
                for dst, src in (first, second):
                    sp.dma_start(dst, src).then_inc(unit_in[slot], 16)

            def column_unit(base, n, w, lay, n0, n1, rows="(p c)"):
                slot = n % RING
                v = ring[slot][:, 0:KC * (n1 - n0)].rearrange("p (c n) -> p c n", c=KC)
                src = cols(w, n0, n1, rows)
                hc = KC // 2
                unit(base, n, slot,
                     (v[:, 0:hc], src[bass.ds(lay, 1), :, 0:hc].rearrange("l p c n -> p (l c) n")),
                     (v[:, hc:KC], src[bass.ds(lay, 1), :, hc:KC].rearrange("l p c n -> p (l c) n")))

            def step_units(base, lay, j):
                for g in range(QUADS_PER_STEP):
                    e0 = lay * NE + (j * QUADS_PER_STEP + g) * QUAD
                    for n in range(UNITS_PER_QUAD):
                        u = g * UNITS_PER_QUAD + n
                        slot = u % RING
                        if n < 4:
                            v = ring[slot].rearrange("p (e w x) -> p e w x", e=QUAD, w=2)
                            x = 2 * FE
                            unit(base, u, slot,
                                 (v[:, :, 0], gate_w[bass.ds(e0, QUAD), :, n * x:(n + 1) * x].rearrange("e p x -> p e x")),
                                 (v[:, :, 1], up_w[bass.ds(e0, QUAD), :, n * x:(n + 1) * x].rearrange("e p x -> p e x")))
                        else:
                            v = ring[slot].rearrange("p (e c x) -> p e c x", e=QUAD, c=2)
                            x = 512
                            k = (n - 4) * x
                            dn = down_w[bass.ds(e0, QUAD), :, :, k:k + x].rearrange("e p c x -> p e c x")
                            unit(base, u, slot, (v[:, 0:2], dn[:, 0:2]), (v[:, 2:4], dn[:, 2:4]))

            with sp.Fori(0, L) as lay:
                base = sp.snap(issued)
                for n, (name, w, n0, n1, rows) in enumerate(UNITS):
                    if rows:
                        column_unit(base, n, a[w], lay, n0, n1, rows)
                    else:
                        chunks = a[w].shape[1] // P
                        v = ring[n % RING][:, 0:chunks * n1].rearrange("p (c n) -> p c n", c=chunks)
                        src = a[w].rearrange("l (c p) n -> l p c n", p=P)
                        half = n1 // 2
                        unit(base, n, n % RING,
                             (v[:, :, 0:half], src[bass.ds(lay, 1), :, :, 0:half].rearrange("l p c n -> p (l c) n")),
                             (v[:, :, half:n1], src[bass.ds(lay, 1), :, :, half:n1].rearrange("l p c n -> p (l c) n")))
                sp.reg_add(issued, issued, FIXED_UNITS)
                with sp.Fori(0, MOE_STEPS) as j:
                    base_j = sp.snap(issued)
                    step_units(base_j, lay, j)
                    sp.reg_add(issued, issued, STEP_UNITS)
                sp.wait_ge(sp_rounds, lay + 1)
                sp.sem_inc(sp_saw, 1)
                r = sp.value_load(rounds_i[0:1, 0:1], min_val=1, max_val=8)
                sp.sem_inc(sp_took, 1)
                with sp.If(r > 1):
                    with sp.Fori(1, r):
                        with sp.Fori(0, MOE_STEPS) as j2:
                            base_j = sp.snap(issued)
                            step_units(base_j, lay, j2)
                            sp.reg_add(issued, issued, STEP_UNITS)
            sp.wait_ge(stored, 32)

        @block.tensor
        def _(pe):
            ring_base = pe.alloc_register("ring_base")
            pe.reg_mov(ring_base, 0)
            pe.sem_inc(unit_free, RING)
            ident = tb("ident")

            def begin(name):
                n = INDEX[name]
                if n >= 8:
                    before, who = JOBS[n - 8]
                    pe.wait_ge(M["act_emptied"] if who == "A" else M["dve_emptied"], emptied(before))
                return bank[n % 8]

            def after(name):
                pe.wait_ge(M["act_emptied"] if JOBS[INDEX[name]][1] == "A" else M["dve_emptied"], emptied(name))

            def wait_unit(base, n):
                n = UNIT_NUMBER.get(n, n)
                pe.wait_ge(unit_in[n % RING], base + LOADED * (n // RING + 1))

            def transposes(prefix, src, k):
                pe.wait_ge(M["normed"], k)
                for n in range(4):
                    o = begin(f"{prefix}_xt{n}")
                    for c in range(2):
                        for t in range(T):
                            mm = pe.transpose(o[:, c * S + t * P:c * S + t * P + P], src[:, t, 2 * n + c], ident)
                    mm.then_inc(M["pe_job"], 1)

            def channel_tile(o, w, c0, m, rhs, chunks=KC, row0=0):
                for c in range(chunks):
                    mm = pe.matmul(o[row0:row0 + m], w[:, c, c0:c0 + m], rhs[:, c], start=(c == 0), stop=(c == chunks - 1))
                return mm

            def two_tiles(name, w, c0, rhs):
                o = begin(name)
                for k in range(2):
                    mm = channel_tile(o[:, k * S:(k + 1) * S], w, c0 + k * P, P, rhs)
                mm.then_inc(M["pe_job"], 1)

            def unit_view(slot, n):
                return ring[slot][:, 0:KC * n].rearrange("p (c n) -> p c n", c=KC)

            def level(lv):
                pe.wait_ge(M["levels_ready"], lv + 1)
                for odd in range(2):
                    o = begin(f"lv{lv}{'eo'[odd]}")
                    lo = CHUNK * odd
                    for t in range(T):
                        for pair in range(2):
                            x = (t * 2 + pair) * P
                            mm = pe.matmul(o[:, x:x + P], kl[lo:lo + HD, pair, t * P:t * P + P],
                                           ql[lo:lo + HD, pair, t * P:t * P + P], start=True, stop=True)
                    mm.then_inc(M["pe_job"], 1)

            def block_sums(name, blk, sq, ready, count):
                pe.wait_ge(ready, count)
                pe.matmul(begin(name)[:, :], blk, sq.rearrange("p c s -> p (c s)"), start=True, stop=True).then_inc(M["pe_job"], 1)

            def slot_view(name):
                n = UNIT_NUMBER[name]
                return unit_view(n % RING, UNITS[n][3] - UNITS[n][2])

            def fill_values(n, base):
                unit = f"xv{n // 2}"
                if n % 2 == 0:
                    wait_unit(base, unit)
                o = begin(f"xv{n}")
                w, t = slot_view(unit), n % 2
                for c in range(KC):
                    mm = pe.matmul(o[:, :], mT[:, c, t * P:t * P + P], w[:, c], start=(c == 0), stop=(c == KC - 1))
                mm.then_inc(M["pe_job"], 1)
                if n % 2 == 1:
                    free_unit(f"xv{n}")

            def add_to_rows(prefix, lhs, base):
                for n in range(2):
                    wait_unit(base, f"{prefix}{n}")
                    w = slot_view(f"{prefix}{n}")
                    for t in range(T):
                        o = begin(f"{prefix}{2 * n + t}")
                        for c in range(KC):
                            mm = pe.matmul(o[:, :], lhs[:, c, t * P:t * P + P], w[:, c], start=(c == 0), stop=(c == KC - 1))
                        mm.then_inc(M["pe_job"], 1)
                    pe.wait_ge(M["pe_job"], INDEX[f"{prefix}{2 * n + 1}"] + 1)
                    pe.sem_inc(unit_free, 1)

            def free_unit(name):
                pe.wait_ge(M["pe_job"], INDEX[name] + 1)
                pe.sem_inc(unit_free, 1)

            def quad(step, g, base):
                q = step * QUADS_PER_STEP + g
                t0, t1, gu, d0, d1, s0, s1 = bank[0], bank[1], bank[2 + g % 2], bank[4], bank[5], bank[6], bank[7]
                x = slice(g * QUAD, (g + 1) * QUAD)
                for half, o in enumerate((t0, t1)):
                    for c in range(4):
                        for t in range(T):
                            mm = pe.matmul(o[:, c * P:c * P + P], hn[:, t, half * 4 + c],
                                           sel[:, t, x].rearrange("p e s -> p (e s)"), start=(t == 0), stop=(t == T - 1))
                    mm.then_inc(M["m_gather"], 1)
                pe.wait_ge(M["xt_ready"], q * 2 + 1)
                for t in range(T):
                    mm = pe.transpose(t0[:, t * P:t * P + P], comb[:, t, x].rearrange("p e s -> p (e s)"), ident)
                mm.then_inc(M["m_gather"], 1)
                pe.wait_ge(M["xt_ready"], q * 2 + 2)
                for n in range(4):
                    u = g * UNITS_PER_QUAD + n
                    wait_unit(base, u)
                    w = ring[u % RING].rearrange("p (e w c f) -> p e w c f", e=QUAD, w=2, c=2)
                    for c in range(2):
                        for e in range(QUAD):
                            first, last = n == 0 and c == 0, n == 3 and c == 1
                            mm = pe.matmul(gu[32 * e:32 * e + 32, :], xT[:, 2 * n + c, 32 * e:32 * e + 32],
                                           w[:, e, :, c], start=first, stop=last, tile_position=(0, 32 * e))
                    mm.then_inc(M["m_up"], 1)
                    pe.wait_ge(M["m_up"], q * 4 + (n + 1))
                    pe.sem_inc(unit_free, 1)
                pe.wait_ge(M["hid_ready"], q + 1)
                for c in range(2):
                    mm = pe.transpose(t1[:, c * P:c * P + P], hid[:, c * P:c * P + P], ident)
                mm.then_inc(M["m_gather"], 1)
                pe.wait_ge(M["hidT_ready"], q + 1)
                for n, o in enumerate((d0, d1)):
                    u = g * UNITS_PER_QUAD + 4 + n
                    wait_unit(base, u)
                    w = ring[u % RING].rearrange("p (e c x) -> p e c x", e=QUAD, c=2)
                    for c in range(2):
                        for e in range(QUAD):
                            mm = pe.matmul(o[32 * e:32 * e + 32, :], hidT[:, c, 32 * e:32 * e + 32], w[:, e, c],
                                           start=(c == 0), stop=(c == 1), tile_position=(0, 32 * e))
                    mm.then_inc(M["m_down"], 1)
                    pe.wait_ge(M["m_down"], q * 2 + (n + 1))
                    pe.sem_inc(unit_free, 1)
                pe.wait_ge(M["ct_ready"], q + 1)
                for t in range(T):
                    pe.wait_ge(M["added"], q * 4 + (2 * t + 1))
                    for n, o in enumerate((s0, s1)):
                        if t == 0:
                            pe.wait_ge(M["ya_ready"] if n == 0 else M["yv_ready"], q + 1)
                        pe.matmul(o[:, :], cT[:, t], yy[:, n * 512:n * 512 + 512], start=True, stop=True).then_inc(M["m_scatter"], 1)

            pe.wait_ge(tables_in, 16)
            pe.wait_ge(mem_normed, 1)
            rows = mqT.rearrange("p a s -> p (a s)").rearrange("p (t c k) -> p t c k", t=T, c=KC)
            for n in range(4):
                for c in range(2):
                    for t in range(T):
                        mm = pe.transpose(bank[n][:, c * S + t * P:c * S + t * P + P], rows[:, t, 2 * n + c], ident)
                mm.then_inc(mem_turned, 1)

            with pe.Fori(0, L) as lay:
                base = pe.snap(ring_base)
                pe.reg_add(ring_base, ring_base, LOADED * FIXED_UNITS // RING)
                pe.wait_ge(M["gained"], 1)
                wait_unit(base, "xk0")
                w = slot_view("xk0")
                two_tiles("xk0", w, 0, mT)
                two_tiles("xk1", w, 256, mT)
                free_unit("xk1")
                transposes("mix", mqT.rearrange("p a s -> p (a s)").rearrange("p (t c k) -> p t c k", t=T, c=KC), 1)
                after("mix_xt3")
                wait_unit(base, "in_fq")
                w = slot_view("in_fq")
                two_tiles("f", w, 256, uT)
                two_tiles("q", w, 0, uT)
                free_unit("q")
                wait_unit(base, "in_ig")
                w = slot_view("in_ig")
                o = begin("i")
                for t in range(T):
                    for c in range(KC):
                        mm = pe.matmul(o[:, t * S:(t + 1) * S], uT[:, c, t * P:t * P + P], w[:, c, 0:256], start=(c == 0), stop=(c == KC - 1))
                mm.then_inc(M["pe_job"], 1)
                two_tiles("g", w, 256, uT)
                free_unit("g")
                wait_unit(base, "xk2")
                two_tiles("xk2", slot_view("xk2"), 0, mT)
                free_unit("xk2")
                level(0)
                wait_unit(base, "in_bc")
                w = slot_view("in_bc")
                two_tiles("b", w, 0, uT)
                level(1)
                two_tiles("c", w, 256, uT)
                free_unit("c")
                level(2)
                wait_unit(base, "in_hq")
                w = slot_view("in_hq")
                two_tiles("hc", w, 0, uT)
                level(3)
                two_tiles("cq", w, 256, uT)
                free_unit("cq")
                level(4)
                wait_unit(base, "in_kv")
                w = slot_view("in_kv")
                o = begin("kv")
                channel_tile(o[:, 0:S], w, 0, P, uT)
                channel_tile(o[:, S:2 * S], w, 64, 96, uT).then_inc(M["pe_job"], 1)
                o = begin("kvs")
                pe.wait_ge(M["swapped"], 1)
                channel_tile(o[:, 0:S], w_kps, 0, ROPE, uT, row0=64).then_inc(M["pe_job"], 1)
                free_unit("kvs")
                wait_unit(base, "xk3")
                two_tiles("xk3", slot_view("xk3"), 0, mT)
                free_unit("xk3")
                pe.wait_ge(M["lat_sq"], 1)
                o = begin("latss")
                sq = mqT.rearrange("p a s -> p (a s)")
                pe.matmul(o[:, 0:S], tb("ones"), sq[:, 0:S], start=True, stop=False)
                pe.matmul(o[:, 0:S], tb("ones"), sq[:, S:2 * S], start=False, stop=True)
                pe.matmul(o[:, S:2 * S], tb("ones"), sq[:, 2 * S:3 * S], start=True, stop=True).then_inc(M["pe_job"], 1)
                pe.wait_ge(M["ktok_scaled"], 1)
                o = begin("ktok")
                for t in range(T):
                    for pair in range(2):
                        mm = pe.transpose(o[:, (t * 2 + pair) * P:(t * 2 + pair + 1) * P], kl[:, pair, t * P:t * P + P], ident)
                mm.then_inc(M["pe_job"], 1)
                after("ktok")
                o = begin("u0")
                for k, ch in enumerate((0, 2)):
                    for pair in range(2):
                        mm = pe.matmul(o[:, (2 * k + pair) * P:(2 * k + pair + 1) * P], ktok[0:64, ch // 2, pair],
                                       ih[0:64, ch // 2, pair * P:pair * P + P], start=True, stop=True)
                mm.then_inc(M["pe_job"], 1)
                o = begin("u1")
                for pair in range(2):
                    mm = pe.matmul(o[:, pair * P:pair * P + P], ktok[64:128, 0, pair],
                                   ih[64:128, 0, pair * P:pair * P + P], start=True, stop=True)
                mm.then_inc(M["pe_job"], 1)
                block_sums("convss", tb("blk64"), cu, M["conv_sq"], 1)
                pe.wait_ge(M["scores_done"], 1)
                o = begin("o_in")
                for pair in range(2):
                    for t in range(T):
                        for odd in range(2):
                            hx = (2 * pair + odd) * HD
                            mm = pe.matmul(o[64 * odd:64 * odd + 64, pair * S + t * P:pair * S + t * P + P],
                                           ih[:, t, hx:hx + HD], sacc[:, odd, t, pair], start=True, stop=True)
                mm.then_inc(M["pe_job"], 1)
                pe.wait_ge(M["state_ready"], 1)
                o = begin("o_st")
                for pair in range(2):
                    for ch in range(1, 4):
                        mm = pe.matmul(o[:, pair * S + ch * CHUNK:pair * S + (ch + 1) * CHUNK], states[:, ch - 1, pair],
                                       ql[:, pair, ch * CHUNK:(ch + 1) * CHUNK], start=True, stop=True)
                mm.then_inc(M["pe_job"], 1)
                block_sums("hgss", tb("blk64"), kl, M["hg_sq"], 1)
                wait_unit(base, "uq")
                slot_q, slot_kv = UNIT_NUMBER["uq"] % RING, UNIT_NUMBER["ukv"] % RING
                wq = ring[slot_q][:, 0:1536].rearrange("p (c n) -> p c n", c=2)
                wkv = ring[slot_kv][:, 0:1024]
                pe.wait_ge(M["lat_ready"], 1)
                for n in range(4):
                    o = begin(f"mq{n}")
                    for k in range(2):
                        mm = channel_tile(o[:, k * S:(k + 1) * S], wq, (2 * n + k) * QK, QK, lat, chunks=2)
                    mm.then_inc(M["pe_job"], 1)
                pe.wait_ge(M["swapped"], 2)
                for n in range(4):
                    o = begin(f"mqs{n}")
                    for k in range(2):
                        mm = channel_tile(o[:, k * S:(k + 1) * S], w_uqs.rearrange("p c h r -> p c (h r)"),
                                          (2 * n + k) * ROPE, ROPE, lat, chunks=2, row0=64)
                    mm.then_inc(M["pe_job"], 1)
                free_unit("mqs3")
                wait_unit(base, "ukv")
                for n in range(4):
                    o = begin(f"mk{n}")
                    for k in range(2):
                        hx = (2 * n + k) * (NOPE + MV)
                        mm = pe.matmul(o[0:NOPE, k * S:(k + 1) * S], wkv[:, hx:hx + NOPE], lat[:, 2], start=True, stop=True)
                    mm.then_inc(M["pe_job"], 1)
                for t in range(T):
                    pe.matmul(begin(f"mv{t}")[:, :], lat[:, 2, t * P:t * P + P],
                              wkv.rearrange("p (h n) -> p h n", h=MH)[:, :, NOPE:NOPE + MV], start=True, stop=True).then_inc(M["pe_job"], 1)
                free_unit("mv1")
                fill_values(0, base)
                after("mv1")
                pe.wait_ge(M["mla_k"], 1)
                pe.wait_ge(M["mla_q"], 1)
                for n in range(2):
                    o = begin(f"ms{n}")
                    for k in range(4):
                        mm = pe.matmul(o[:, k * P:(k + 1) * P], mqT[0:QK, 4 * n + k, 0:P], mkT[0:QK, 4 * n + k, 0:P], start=True, stop=True)
                    mm.then_inc(M["pe_job"], 1)
                for n in range(4):
                    o = begin(f"ms{2 + n}")
                    for k in range(2):
                        mm = pe.matmul(o[:, k * S:(k + 1) * S], mqT[0:QK, 2 * n + k, P:S], mkT[0:QK, 2 * n + k], start=True, stop=True)
                    mm.then_inc(M["pe_job"], 1)
                fill_values(1, base)
                pe.wait_ge(M["mla_p"], 1)
                for n in range(2):
                    o = begin(f"mt{n}")
                    for k in range(4):
                        mm = pe.transpose(o[:, k * P:(k + 1) * P], mp0[:, 4 * n + k], ident)
                    mm.then_inc(M["pe_job"], 1)
                fill_values(2, base)
                pe.wait_ge(M["mla_p"], 2)
                for n in range(4):
                    o = begin(f"mt{2 + n}")
                    for k in range(4):
                        mm = pe.transpose(o[:, k * P:(k + 1) * P], mp1[:, 4 * (n % 2) + k, (n // 2) * P:(n // 2 + 1) * P], ident)
                    mm.then_inc(M["pe_job"], 1)
                after("mt5")
                for n in range(2):
                    o = begin(f"mo{n}")
                    for t in range(T):
                        for k in range(4):
                            hx = 4 * n + k
                            dst = o[64 * (k % 2):64 * (k % 2) + 64, (k // 2) * S + t * P:(k // 2) * S + (t + 1) * P]
                            for kt in range(t + 1):
                                mm = pe.matmul(dst, mV[:, kt, hx * MV:(hx + 1) * MV], mpt1[:, kt, hx] if t else mpt0[:, hx],
                                               start=(kt == 0), stop=(kt == t))
                    mm.then_inc(M["pe_job"], 1)
                for n in range(2):
                    block_sums(f"mss{n}", tb("blk64"), mqT[:, 4 + 2 * n:6 + 2 * n], M["mla_osq"], n + 1)
                fill_values(3, base)
                pe.wait_ge(M["mixed"], 3)
                add_to_rows("out", uT, base)

                transposes("cross", qT.rearrange("p a s -> p (a s)").rearrange("p (t c k) -> p t c k", t=T, c=KC), 2)
                after("cross_xt3")
                for n in range(2):
                    wait_unit(base, f"xq{n}")
                    w = slot_view(f"xq{n}")
                    two_tiles(f"xq{2 * n}", w, 0, uT)
                    two_tiles(f"xq{2 * n + 1}", w, 256, uT)
                    free_unit(f"xq{2 * n + 1}")
                after("xq3")
                for t in range(T):
                    for n in range(2):
                        o = begin(f"xs{2 * t + n}")
                        for k in range(2):
                            hx = 2 * n + k
                            for c in range(2):
                                mm = pe.matmul(o[:, k * S:(k + 1) * S], qT[:, 2 * hx + c, t * P:t * P + P], kT[:, 2 * hx + c],
                                               start=(c == 0), stop=(c == 1))
                        mm.then_inc(M["pe_job"], 1)
                for t in range(T):
                    pe.wait_ge(M["x_p"], t + 1)
                    for kt in range(T):
                        o = begin(f"xt{2 * t + kt}")
                        for hx in range(XH):
                            mm = pe.transpose(o[:, hx * P:(hx + 1) * P], pr[:, t, hx, kt * P:(kt + 1) * P], ident)
                        mm.then_inc(M["pe_job"], 1)
                after("xt3")
                for n in range(4):
                    o = begin(f"xo{n}")
                    for k in range(2):
                        for kt in range(T):
                            mm = pe.matmul(o[:, k * S:(k + 1) * S], vv[:, kt, (2 * n + k) * P:(2 * n + k + 1) * P], pT[:, kt, n],
                                           start=(kt == 0), stop=(kt == 1))
                    mm.then_inc(M["pe_job"], 1)
                after("xo3")
                add_to_rows("xout", oT, base)

                transposes("ffn", hn, 3)
                after("ffn_xt3")
                pe.wait_ge(M["params"], 32)
                o = begin("router")
                for t in range(T):
                    for c in range(KC):
                        mm = pe.matmul(o[:, t * 64:t * 64 + NG + NE], uT[:, c, t * P:t * P + P], w_rout[:, c], start=(c == 0), stop=(c == KC - 1))
                mm.then_inc(M["pe_job"], 1)
                pe.wait_ge(M["r_chosen"], 1)
                o = begin("places")
                pe.matmul(o[:, 0:NE], tb("before"), chosen[:, 0], start=True, stop=True)
                pe.matmul(o[:, NE:2 * NE], tb("before"), chosen[:, 1], start=True, stop=False)
                pe.matmul(o[:, NE:2 * NE], tb("ones"), chosen[:, 0], start=False, stop=True)
                pe.matmul(o[:, 2 * NE:3 * NE], tb("ones"), chosen[:, 0], start=True, stop=False)
                pe.matmul(o[:, 2 * NE:3 * NE], tb("ones"), chosen[:, 1], start=False, stop=True).then_inc(M["pe_job"], 1)

                pe.wait_ge(M["rounds"], 1)
                after("places")
                r = pe.value_load(rounds_i[0:1, 0:1], min_val=1, max_val=8)
                with pe.Fori(0, r) as rnd:
                    with pe.Fori(0, MOE_STEPS) as j:
                        step = rnd * MOE_STEPS + j
                        base_j = pe.snap(ring_base)
                        pe.reg_add(ring_base, ring_base, LOADED * STEP_UNITS // RING)
                        pe.wait_ge(M["slots"], step + 1)
                        for g in range(QUADS_PER_STEP):
                            quad(step, g, base_j)
                pe.sem_inc(M["arrived"], 1)
                pe.wait_ge(released, lay + 1)

        @block.scalar
        def _(act):
            steps = [0]

            def tick():
                steps[0] += 1
                return 1

            def settle():
                act.wait_ge(M["act_step"], steps[0])

            def job(name):
                act.wait_ge(M["pe_job"], INDEX[name] + 1)
                return bank[INDEX[name] % 8]

            def sum_squares(src, junk):
                for t in range(T):
                    act.activation(junk[:, t], src[:, t], ACT.Square, accum_out=ss[:, t:t + 1]).then_inc(M["sumsq"], 1)

            def first_rstd(k):
                act.wait_ge(M["meansq"], k)
                act.activation(nt[:, :], ms[:, :], ACT.Ln).then_inc(M["act_step"], tick())
                settle()
                act.activation(rs0[:, :], nt[:, :], ACT.Exp, scale=-0.5).then_inc(M["rstd0"], 1)

            def empty_transposes(prefix, dst, gain):
                for n in range(4):
                    o = job(f"{prefix}_xt{n}")
                    for c in range(2):
                        i = act.activation(dst[:, 2 * n + c], o[:, c * S:(c + 1) * S], ACT.Identity, scale=gains[:, gain, 2 * n + c:2 * n + c + 1])
                    i.then_inc(M["act_emptied"], 1)

            def copy_out(name, dst, src=None):
                o = job(name)
                act.activation(dst, o[:, :] if src is None else src(o), ACT.Copy).then_inc(M["act_emptied"], 1)

            def load_tables(which):
                act.add_instruction(mybir.InstLoadActFuncSet(act_func_set_id=which, name=nc.get_next_instruction_name(), ins=[], outs=[]))

            flat = lambda x: x.rearrange("p c s -> p (c s)")
            act.dma_start(ptab[:, :, :], a["params"][:, :, :]).then_inc(params_in, 16)
            act.dma_start(sinT[64:96, :].bitcast(I32), a["positions"].broadcast_to([ROPE, S])).then_inc(positions_in, 16)
            act.dma_start(uT.rearrange("p c s -> p (c s)")[:, 0:LEVELS * P], level_masks[:, :]).then_inc(masks_in, 16)
            load_tables(LN_EXP_TABLES)
            act.wait_ge(lb_x, 1)
            act.activation(lb_tmp[:, 0:L], lb_tmp[:, 0:L], ACT.Exp).then_inc(lb_x, 1)
            act.wait_ge(mem_in, 16)
            mrow = kT.rearrange("p c s -> p (c s)").rearrange("p (t d) -> p t d", t=T)
            for t in range(T):
                act.activation(vv[:, t], mrow[:, t], ACT.Square, accum_out=ss[:, t:t + 1]).then_inc(mem_sumsq, 1)
            act.wait_ge(mem_meansq, 1)
            act.activation(nt[:, :], ms[:, :], ACT.Ln).then_inc(mem_step, 1)
            act.wait_ge(mem_step, 1)
            act.activation(rs0[:, :], nt[:, :], ACT.Exp, scale=-0.5).then_inc(mem_rstd, 1)
            for n in range(4):
                act.wait_ge(mem_turned, n + 1)
                act.activation(memN[:, 2 * n:2 * n + 2].rearrange("p c s -> p (c s)"), bank[n][:, :], ACT.Copy).then_inc(mem_kept, 1)
            act.wait_ge(angles, 1)
            act.activation(sinT[64:96], sinT[64:96], ACT.Sin).then_inc(rotary, 1)
            act.activation(cosT[64:96], cosT[64:96], ACT.Sin).then_inc(rotary, 1)
            act.wait_ge(x_in, 16)
            with act.Fori(0, L) as lay:
                steps[0] = 0
                row = bass.ds(lay, 1)
                act.dma_start(w_rout.rearrange("p c n -> p (c n)"), a["router_w"][row].rearrange("l p n -> p (l n)")).then_inc(M["params"], 16)
                act.dma_start(b_rout[:, :], a["router_b"][row].broadcast_to([P, NG + NE])).then_inc(M["params"], 16)

                nrow = mqT.rearrange("p a s -> p (a s)").rearrange("p (t c) -> p t c", t=T)
                load_tables(LN_EXP_TABLES)
                sum_squares(h, nrow)
                first_rstd(1)
                act.wait_ge(M["par_ready"], 1)
                for n in range(2):
                    copy_out(f"xk{n}", kT[:, 2 * n:2 * n + 2].rearrange("p c s -> p (c s)"))
                empty_transposes("mix", uT, 0)
                act.activation(flat(dl), job("f")[:, :], ACT.Exp, scale=-1.0).then_inc(M["act_emptied"], 1)
                act.activation(flat(ql), job("q")[:, :], ACT.Exp, scale=-1.0).then_inc(M["sig_q"], 1)
                copy_out("i", ih.rearrange("p t s -> p (t s)"))
                act.wait_ge(M["fgate"], 1)
                act.activation(flat(dl), flat(dl), ACT.Ln).then_inc(M["logf"], 1)
                act.activation(flat(kl), job("g")[:, :], ACT.Exp, scale=-1.0).then_inc(M["sig_g"], 1)

                def exp_level(lv):
                    act.wait_ge(M["diff"], lv + 1)
                    if lv == 0:
                        act.activation(flat(ql), flat(dl), ACT.Exp).then_inc(M["act_step"], tick())
                        act.activation(flat(kl), flat(dl), ACT.Exp, scale=-1.0).then_inc(M["expdiff"], 1)
                    else:
                        act.activation(flat(dl), flat(dl), ACT.Exp).then_inc(M["expdiff"], 1)
                exp_level(0)
                copy_out("xk2", kT[:, 4:6].rearrange("p c s -> p (c s)"))
                exp_level(1)
                copy_out("b", flat(cb))
                exp_level(2)
                copy_out("c", flat(cu))
                exp_level(3)
                exp_level(4)
                copy_out("cq", flat(lat[:, 0:2]))
                o = job("kv")
                act.activation(lat[:, 2], o[:, 0:S], ACT.Copy).then_inc(M["act_step"], tick())
                act.activation(mkT[64:96, 0], o[64:96, S:2 * S], ACT.Copy).then_inc(M["act_emptied"], 1)
                settle()
                act.wait_ge(M["act_emptied"], emptied("kv"))
                act.activation(mqT.rearrange("p a s -> p (a s)")[:, 0:3 * S], flat(lat), ACT.Square).then_inc(M["lat_sq"], 1)
                act.wait_ge(M["qk_state"], 1)
                act.activation(flat(ql), flat(bcum), ACT.Exp).then_inc(M["act_step"], tick())
                act.activation(flat(kl), flat(dl), ACT.Exp).then_inc(M["expdiff"], 1)
                copy_out("xk3", kT[:, 6:8].rearrange("p c s -> p (c s)"))
                o = job("latss")
                rl = mkT[:, 4:6]
                act.activation(rl[:, 0], o[:, 0:S], ACT.Ln, bias=tb("eps"), scale=1.0 / 256).then_inc(M["act_step"], tick())
                act.activation(rl[:, 1], o[:, S:2 * S], ACT.Ln, bias=tb("eps"), scale=1.0 / 128).then_inc(M["act_emptied"], 1)
                settle()
                act.wait_ge(M["act_emptied"], emptied("latss"))
                act.activation(flat(rl), flat(rl), ACT.Exp, scale=-0.5).then_inc(M["lat_rstd"], 1)
                copy_out("ktok", ktok.rearrange("p t c s -> p (t c s)"))
                act.wait_ge(M["conv_yb"], 1)
                act.activation(flat(cu), flat(cy), ACT.Square).then_inc(M["conv_sq"], 1)
                group_rstd_done(act, job, "convss", flat(cb), 64, M, tick, settle, tb, M["conv_rstd"])
                copy_out("o_in", flat(dl))
                act.wait_ge(M["o_sum"], 1)
                act.activation(flat(kl), flat(dl), ACT.Square).then_inc(M["hg_sq"], 1)
                group_rstd_done(act, job, "hgss", flat(ql), 64, M, tick, settle, tb, M["hg_rstd"])
                for n in range(4):
                    copy_out(f"mq{n}", mqT[0:QK, 2 * n:2 * n + 2].rearrange("p c s -> p (c s)"), lambda o: o[0:QK, :])
                for n in range(4):
                    copy_out(f"mk{n}", mkT[0:NOPE, 2 * n:2 * n + 2].rearrange("p c s -> p (c s)"), lambda o: o[0:NOPE, :])
                for t in range(T):
                    copy_out(f"mv{t}", mV[:, t])

                def keep_values(n):
                    copy_out(f"xv{n}", vv[:, n % 2, 512 * (n // 2):512 * (n // 2) + 512])
                keep_values(0)
                for t, mp in enumerate((mp0, mp1)):
                    act.wait_ge(M["mla_neg"], t + 1)
                    for k in range(MH):
                        x = 8 * t + k
                        act.activation(mp[:, k], mp[:, k], ACT.Exp, bias=small[:, x:x + 1],
                                       accum_out=small[:, 16 + x:17 + x]).then_inc(M["mla_exp"], 1)
                keep_values(1)
                for n in range(2):
                    copy_out(f"mt{n}", mpt0[:, 4 * n:4 * n + 4].rearrange("p c s -> p (c s)"))
                keep_values(2)
                for n in range(4):
                    copy_out(f"mt{2 + n}", mpt1[:, n // 2, 4 * (n % 2):4 * (n % 2) + 4].rearrange("p c s -> p (c s)"))
                for n in range(2):
                    copy_out(f"mo{n}", mqT[:, 2 * n:2 * n + 2].rearrange("p c s -> p (c s)"))
                for n in range(2):
                    act.wait_ge(M["act_emptied"], emptied(f"mo{n}"))
                    act.activation(mqT[:, 4 + 2 * n:6 + 2 * n], mqT[:, 2 * n:2 * n + 2], ACT.Square).then_inc(M["mla_osq"], 1)
                for n in range(2):
                    group_rstd_done(act, job, f"mss{n}", mkT[:, 2 * n:2 * n + 2].rearrange("p c s -> p (c s)"), 64, M, tick, settle, tb, M["mla_rstd"])

                keep_values(3)
                act.wait_ge(M["dve_emptied"], emptied("out3"))
                sum_squares(h, qT.rearrange("p a s -> p (a s)").rearrange("p (t c) -> p t c", t=T))
                first_rstd(2)
                empty_transposes("cross", uT, 1)
                for n in range(4):
                    copy_out(f"xq{n}", qT[:, 2 * n:2 * n + 2].rearrange("p c s -> p (c s)"))
                for n in range(4):
                    act.wait_ge(M["x_max"], n + 1)
                    o = job(f"xs{n}")
                    for k in range(2):
                        x = 2 * n + k
                        i = act.activation(pr[:, n // 2, 2 * (n % 2) + k], o[:, k * S:(k + 1) * S], ACT.Exp, bias=xsm[:, x:x + 1],
                                           scale=XD ** -0.5, accum_out=xsm[:, 8 + x:9 + x])
                        i.then_inc(M["x_exp"], 1)
                    act.wait_ge(M["x_exp"], 2 * n + 2)
                    act.sem_inc(M["act_emptied"], 1)
                for n in range(4):
                    t, kt = n // 2, n % 2
                    o = job(f"xt{n}")
                    act.activation(pT[:, kt, :, t * P:(t + 1) * P], o[:, :].rearrange("p (h s) -> p h s", h=XH), ACT.Copy).then_inc(M["act_emptied"], 1)

                act.wait_ge(M["dve_emptied"], emptied("xout3"))
                sum_squares(h, hn.rearrange("p t c k -> p t (c k)"))
                first_rstd(3)
                empty_transposes("ffn", uT, 3)
                act.wait_ge(M["r_exp"], 1)
                act.activation(rt[:, 8:16], rt[:, 8:16], ACT.Exp).then_inc(M["r_exp_e"], 1)
                act.wait_ge(M["r_exp"], 2)
                act.activation(rt[:, 128:130], rt[:, 128:130], ACT.Exp).then_inc(M["r_exp_e"], 1)
                load_tables(SILU_TABLES)
                act.wait_ge(M["rounds"], 1)
                r = act.value_load(rounds_i[0:1, 0:1], min_val=1, max_val=8)
                with act.Fori(0, r) as rnd:
                    with act.Fori(0, MOE_STEPS) as j:
                        step = rnd * MOE_STEPS + j
                        for g in range(QUADS_PER_STEP):
                            q = step * QUADS_PER_STEP + g
                            act.wait_ge(M["m_gather"], q * 4 + 3)
                            act.activation(cT.rearrange("p t s -> p (t s)"), bank[0][:, 0:S], ACT.Copy).then_inc(M["ct_ready"], 1)
                            act.wait_ge(M["m_up"], q * 4 + 4)
                            act.activation(sg[:, :], bank[2 + g % 2][:, 0:FE], ACT.Silu).then_inc(M["silu"], 1)
                            act.wait_ge(M["m_gather"], q * 4 + 4)
                            act.activation(hidT.rearrange("p c s -> p (c s)"), bank[1][:, 0:S], ACT.Copy).then_inc(M["hidT_ready"], 1)
                            act.wait_ge(M["m_down"], q * 2 + 1)
                            act.activation(yy[:, 0:512], bank[4][:, :], ACT.Copy).then_inc(M["ya_ready"], 1)
                act.sem_inc(M["arrived"], 1)
                act.wait_ge(released, lay + 1)
            act.dma_start(frow[:, :], a["final_norm"].rearrange("(l d) -> l d", l=1).broadcast_to([P, D])).then_inc(M["params"], 16)
            steps[0] = 0
            load_tables(LN_EXP_TABLES)
            sum_squares(h, hn.rearrange("p t c k -> p t (c k)"))
            first_rstd(1)
            for t in range(T):
                act.wait_ge(M["normed"], t + 1)
                act.dma_start(out.rearrange("b (t p) d -> p (b t) d", p=P)[:, t], h[:, t]).then_inc(stored, 16)

        @block.vector
        def _(dve):
            steps = [0]

            def tick():
                steps[0] += 1
                return 1

            def settle():
                dve.wait_ge(M["dve_step"], steps[0])

            def st(i):
                i.then_inc(M["dve_step"], tick())

            def job(name):
                dve.wait_ge(M["pe_job"], INDEX[name] + 1)
                return bank[INDEX[name] % 8]

            def gone(i):
                i.then_inc(M["dve_emptied"], 1)

            flat = lambda x: x.rearrange("p c s -> p (c s)")

            def mean_square(k):
                dve.wait_ge(M["sumsq"], 2 * k)
                dve.tensor_scalar(ms[:, :], ss[:, :], 1.0 / D, EPS, ALU.mult, ALU.add).then_inc(M["meansq"], 1)

            def refine(k):
                dve.wait_ge(M["rstd0"], k)
                st(dve.tensor_tensor(nt[:, :], rs0[:, :], rs0[:, :], ALU.mult))
                settle()
                st(dve.tensor_tensor(nt[:, :], nt[:, :], ms[:, :], ALU.mult))
                settle()
                st(dve.tensor_scalar(nt[:, :], nt[:, :], -0.5, 1.5, ALU.mult, ALU.add))
                settle()
                st(dve.tensor_tensor(rs[:, :], rs0[:, :], nt[:, :], ALU.mult))
                settle()

            def norm_rows(dst, src, k):
                mean_square(k)
                refine(k)
                for t in range(T):
                    i = dve.tensor_scalar(dst[:, t].rearrange("p (c k) -> p c k", c=KC),
                                          src[:, t].rearrange("p (k c) -> p c k", c=KC), rs[:, t:t + 1], None, ALU.mult)
                    if t == 0:
                        st(i)
                settle()
                i.then_inc(M["normed"], 1)

            dve.wait_ge(params_in, 16)
            dve.tensor_tensor(lb_tmp[:, 2], lb_raw[:, 0], lb_raw[:, 1], ALU.max).then_inc(setup_done, 1)
            dve.wait_ge(setup_done, 1)
            for l in range(L):
                i = dve.tensor_tensor(lb_tmp[:, l], lb_raw[:, l], lb_tmp[:, 2], ALU.subtract)
                i.then_inc(setup_done, 1)
            dve.wait_ge(setup_done, 3)
            dve.sem_inc(lb_x, 1)
            dve.wait_ge(lb_x, 2)
            dve.tensor_tensor(lb_tmp[:, 2], lb_tmp[:, 0], lb_tmp[:, 1], ALU.add).then_inc(setup_done, 1)
            dve.wait_ge(setup_done, 4)
            dve.reciprocal(lb_tmp[:, 3], lb_tmp[:, 2]).then_inc(setup_done, 1)
            dve.wait_ge(setup_done, 5)
            for l in range(L):
                dve.tensor_tensor(lb_tmp[:, l], lb_tmp[:, l], lb_tmp[:, 3], ALU.mult).then_inc(setup_done, 1)
            dve.wait_ge(setup_done, 7)
            dve.tensor_tensor(lb_tab[:, 0, 0], lb_tmp[:, 0], lb_tmp[:, 0], ALU.subtract).then_inc(setup_done, 1)
            dve.tensor_tensor(lb_tmp[:, 2], lb_tmp[:, 0], lb_tmp[:, 1], ALU.add).then_inc(setup_done, 1)
            dve.wait_ge(setup_done, 9)
            dve.tensor_tensor(lb_tab[:, 0, 1], lb_tmp[:, 2], lb_tmp[:, 0], ALU.subtract).then_inc(setup_done, 1)
            dve.memset(states[:, :, :, :], 0.0).then_inc(setup_done, 1)
            dve.wait_ge(setup_done, 11)
            dve.tensor_scalar(lb_tab[:, 1], lb_tab[:, 0], -1.0, 1.0, ALU.mult, ALU.add).then_inc(setup_done, 1)
            dve.wait_ge(setup_done, 12)

            dve.wait_ge(mem_sumsq, 2)
            dve.tensor_scalar(ms[:, :], ss[:, :], 1.0 / D, EPS, ALU.mult, ALU.add).then_inc(mem_meansq, 1)
            dve.wait_ge(mem_rstd, 1)
            dve.tensor_tensor(nt[:, :], rs0[:, :], rs0[:, :], ALU.mult).then_inc(setup_done, 1)
            dve.wait_ge(setup_done, 13)
            dve.tensor_tensor(nt[:, :], nt[:, :], ms[:, :], ALU.mult).then_inc(setup_done, 1)
            dve.wait_ge(setup_done, 14)
            dve.tensor_scalar(nt[:, :], nt[:, :], -0.5, 1.5, ALU.mult, ALU.add).then_inc(setup_done, 1)
            dve.wait_ge(setup_done, 15)
            dve.tensor_tensor(rs[:, :], rs0[:, :], nt[:, :], ALU.mult).then_inc(setup_done, 1)
            dve.wait_ge(setup_done, 16)
            mrow = kT.rearrange("p c s -> p (c s)").rearrange("p (t d) -> p t d", t=T)
            nrow = mqT.rearrange("p a s -> p (a s)").rearrange("p (t c) -> p t c", t=T)
            for t in range(T):
                i = dve.tensor_scalar(nrow[:, t].rearrange("p (c k) -> p c k", c=KC),
                                      mrow[:, t].rearrange("p (k c) -> p c k", c=KC), rs[:, t:t + 1], None, ALU.mult)
                i.then_inc(setup_done, 1)
            dve.wait_ge(setup_done, 18)
            dve.sem_inc(mem_normed, 1)
            dve.wait_ge(tables_in, 16)
            dve.wait_ge(masks_in, 16)
            dve.tensor_copy(lvmask.rearrange("p l s -> p (l s)"), uT.rearrange("p c s -> p (c s)")[:, 0:LEVELS * P]).then_inc(setup_done, 1)
            dve.wait_ge(setup_done, 19)
            dve.wait_ge(mem_kept, 4)
            dve.wait_ge(x_in, 16)

            with dve.Fori(0, L) as lay:
                steps[0] = 0
                dve.tensor_copy(par[:, :], ptab[:, bass.ds(lay, 1)].rearrange("p l n -> p (l n)")).then_inc(M["par_ready"], 1)
                dve.wait_ge(M["par_ready"], 1)
                dve.tensor_tensor(mT[:, :, :], memN[:, :, :], gains[:, 2].unsqueeze(2).broadcast_to([P, KC, S]), ALU.mult).then_inc(M["gained"], 1)
                st(dve.tensor_copy(lb[:, :, :], lb_tab[:, :, bass.ds(lay, 1), :].rearrange("p w l c -> p w (l c)")))
                settle()
                nrow = mqT.rearrange("p a s -> p (a s)").rearrange("p (t c) -> p t c", t=T)
                norm_rows(nrow, h, 1)
                R = slice(64, 96)

                def inverse_of_one_more(x):
                    st(dve.tensor_scalar(x, x, 1.0, 3e38, ALU.add, ALU.min))
                    settle()
                    st(dve.reciprocal(x, x))
                    settle()
                dve.wait_ge(M["act_emptied"], emptied("f"))
                inverse_of_one_more(flat(dl))
                for ct in range(2):
                    st(dve.tensor_scalar(dl[:, ct], dl[:, ct], lb[:, 1, ct:ct + 1], lb[:, 0, ct:ct + 1], ALU.mult, ALU.add))
                settle()
                st(dve.tensor_scalar(flat(dl), flat(dl), 1e-6, 1.0, ALU.max, ALU.min))
                settle()
                dve.tensor_scalar(flat(kh), flat(dl), -1.0, 1.0, ALU.mult, ALU.add).then_inc(M["fgate"], 1)
                dve.wait_ge(M["sig_q"], 1)
                inverse_of_one_more(flat(ql))
                gone(dve.tensor_tensor(flat(qh), flat(ql), job("q")[:, :], ALU.mult))
                dve.wait_ge(M["logf"], 1)
                for ct in range(2):
                    st(dve.tensor_tensor_scan(bcum[:, ct], tb("restart"), dl[:, ct], 0.0, ALU.mult, ALU.add))
                dve.wait_ge(M["sig_g"], 1)
                inverse_of_one_more(flat(kl))
                gone(dve.tensor_tensor(flat(gate), flat(kl), job("g")[:, :], ALU.mult))
                settle()

                def differences(lv):
                    blk = 4 << lv
                    b4 = flat(bcum).rearrange("p (n k) -> p n k", k=blk)
                    d4 = flat(dl).rearrange("p (n k) -> p n k", k=blk)
                    ref = (blk - 1) if lv == 0 else blk // 2 - 1
                    r4 = b4[:, :, ref:ref + 1].broadcast_to([P, 2 * S // blk, blk])
                    if lv == 0:
                        dve.tensor_tensor(d4, b4, r4, ALU.subtract).then_inc(M["diff"], 1)
                    else:
                        st(dve.tensor_tensor(d4, b4, r4, ALU.subtract))
                        settle()
                        dve.scalar_tensor_tensor(flat(dl), flat(dl), -1.0, flat(dl), ALU.mult, ALU.min).then_inc(M["diff"], 1)

                def scale_level(lv):
                    dve.wait_ge(M["expdiff"], lv + 1)
                    if lv:
                        dve.wait_ge(M["pe_job"], INDEX[f"lv{lv - 1}o"] + 1)
                    else:
                        dve.wait_ge(M["act_step"], 2)
                    st(dve.tensor_tensor(flat(ql), flat(qh), flat(dl if lv else ql), ALU.mult))
                    settle()
                    dve.tensor_tensor(flat(kl), flat(kh), flat(dl if lv else kl), ALU.mult).then_inc(M["levels_ready"], 1)

                def keep_level(lv):
                    for odd in range(2):
                        o = job(f"lv{lv}{'eo'[odd]}")
                        gone(dve.copy_predicated(sacc[:, odd].rearrange("p t c s -> p (t c) s"),
                                                 lvmask[:, lv:lv + 1].broadcast_to([P, 4, P]),
                                                 o[:, :].rearrange("p (n s) -> p n s", n=4)))

                dve.wait_ge(M["dve_emptied"], emptied("g"))
                st(dve.memset(sacc[:, :, :, :, :], 0.0))
                differences(0)
                scale_level(0)
                for lv in range(1, LEVELS):
                    dve.wait_ge(M["levels_ready"], lv)
                    differences(lv)
                    scale_level(lv)
                    keep_level(lv - 1)
                    if lv == 3:
                        dve.wait_ge(M["act_emptied"], emptied("c"))
                        gone(dve.tensor_tensor(flat(cu), flat(cu), job("hc")[:, :], ALU.mult))
                dve.wait_ge(M["dve_emptied"], emptied("hc"))
                for ct in range(2):
                    st(dve.tensor_scalar(cy[:, ct], cu[:, ct], w_conv[:, 2, ct:ct + 1], None, ALU.mult))
                settle()
                for k in (1, 2):
                    for ct in range(2):
                        st(dve.scalar_tensor_tensor(cy[:, ct, k:], cu[:, ct, 0:S - k], w_conv[:, 2 - k, ct:ct + 1], cy[:, ct, k:], ALU.mult, ALU.add))
                    settle()
                dve.wait_ge(M["act_emptied"], emptied("b"))
                dve.tensor_tensor(flat(cy), flat(cy), flat(cb), ALU.mult).then_inc(M["conv_yb"], 1)
                keep_level(4)
                dve.wait_ge(M["dve_emptied"], emptied("lv4o"))
                dve.sem_inc(M["scores_done"], 1)
                b4 = flat(bcum).rearrange("p (n k) -> p n k", k=CHUNK)
                st(dve.tensor_tensor(flat(dl).rearrange("p (n k) -> p n k", k=CHUNK),
                                     b4[:, :, CHUNK - 1:CHUNK].broadcast_to([P, 2 * S // CHUNK, CHUNK]), b4, ALU.subtract))
                settle()
                dve.sem_inc(M["qk_state"], 1)
                o = job("kvs")
                dve.wait_ge(rotary_ready, 1)
                dve.wait_ge(M["act_emptied"], emptied("kv"))
                st(dve.tensor_tensor(mkT[R, 0], mkT[R, 0], cosT[R], ALU.mult))
                settle()
                gone(dve.tensor_tensor(mkT[R, 1], o[R, 0:S], sinT[R], ALU.mult))
                dve.wait_ge(M["dve_emptied"], emptied("kvs"))
                st(dve.tensor_tensor(mkT[R, 2], mkT[R, 0], mkT[R, 1], ALU.add))
                dve.wait_ge(M["lat_rstd"], 1)
                for c in range(3):
                    i = dve.scalar_tensor_tensor(lat[:, c], lat[:, c], g_lat[:, c:c + 1], mkT[:, 4 if c < 2 else 5], ALU.mult, ALU.mult)
                    st(i)
                settle()
                dve.sem_inc(M["lat_ready"], 1)
                for k in (0, 1):
                    st(dve.tensor_copy(mkT[R, k], mkT[R, 2]))
                st(dve.tensor_copy(mkT[R, 3:8], mkT[R, 2:3].broadcast_to([ROPE, 5, S])))
                settle()
                dve.sem_inc(M["mla_k"], 1)
                dve.wait_ge(M["expdiff"], 6)
                st(dve.tensor_copy(small[:, 48:56].rearrange("p (c n) -> p c n", c=2), ql[:, :, CHUNK - 1::CHUNK]))
                settle()
                st(dve.tensor_tensor(flat(kl), flat(kh), flat(kl), ALU.mult))
                settle()
                dve.sem_inc(M["ktok_scaled"], 1)
                st(dve.tensor_tensor(flat(ql), flat(qh), flat(ql), ALU.mult))
                o0, o1 = job("u0"), job("u1")

                def diag(x, pair, odd):
                    return x[64 * odd:64 * odd + 64, pair * P + 64 * odd:pair * P + 64 * odd + 64]

                for odd in range(2):
                    for pair in range(2):
                        lo = slice(64 * odd, 64 * odd + 64)
                        st(dve.tensor_copy(states[lo, 0, pair, lo], diag(o0, pair, odd)))
                for ch, (o, off) in ((1, (o1, 0)), (2, (o0, 2))):
                    settle()
                    for odd in range(2):
                        for pair in range(2):
                            lo = slice(64 * odd, 64 * odd + 64)
                            st(dve.scalar_tensor_tensor(states[lo, ch, pair, lo], states[lo, ch - 1, pair, lo],
                                                        small[lo, 48 + 4 * pair + ch:49 + 4 * pair + ch], diag(o, pair + off, odd), ALU.mult, ALU.add))
                settle()
                dve.sem_inc(M["dve_emptied"], 2)
                dve.sem_inc(M["state_ready"], 1)
                dve.wait_ge(M["pe_job"], INDEX["kvs"] + 1)
                dve.wait_ge(M["conv_rstd"], 1)
                for ct in range(2):
                    st(dve.scalar_tensor_tensor(uT[:, 2 + ct], cy[:, ct], g_conv[:, ct:ct + 1], cb[:, ct], ALU.mult, ALU.mult))
                settle()
                dve.sem_inc(M["mixed"], 1)
                dve.wait_ge(M["act_emptied"], emptied("o_in"))
                o = job("o_st")
                dv = dl[:, :, CHUNK:S]
                gone(dve.tensor_tensor(dv, dv, o[:, :].rearrange("p (c s) -> p c s", c=2)[:, :, CHUNK:S], ALU.add))
                dve.wait_ge(M["dve_emptied"], emptied("o_st"))
                dve.sem_inc(M["o_sum"], 1)
                st(dve.scalar_tensor_tensor(flat(gate), flat(gate), g_hgrn[:, 0:1], flat(dl), ALU.mult, ALU.mult))
                settle()
                dve.wait_ge(M["hg_rstd"], 1)
                st(dve.tensor_tensor(flat(uT[:, 0:2]), flat(gate), flat(ql), ALU.mult))
                settle()
                dve.sem_inc(M["mixed"], 1)
                for n in range(4):
                    dve.wait_ge(M["act_emptied"], emptied(f"mq{n}"))
                    o = job(f"mqs{n}")
                    q = mqT[R, 2 * n:2 * n + 2]
                    tmp = dl[R]
                    st(dve.tensor_tensor(q, q, cosT[R].unsqueeze(1).broadcast_to([ROPE, 2, S]), ALU.mult))
                    gone(dve.tensor_tensor(tmp, o[R, :].rearrange("p (c s) -> p c s", c=2), sinT[R].unsqueeze(1).broadcast_to([ROPE, 2, S]), ALU.mult))
                    settle()
                    dve.wait_ge(M["dve_emptied"], emptied(f"mqs{n}"))
                    st(dve.tensor_tensor(q, q, tmp, ALU.add))
                    settle()
                dve.sem_inc(M["mla_q"], 1)
                for t, mp in enumerate((mp0, mp1)):
                    keys = P * (t + 1)
                    per = 4 if t == 0 else 2
                    for n in range(2 if t == 0 else 4):
                        o = job(f"ms{n if t == 0 else 2 + n}")[:, :].rearrange("p (k s) -> p k s", k=per)
                        dst = mp[:, n * per:(n + 1) * per]
                        st(dve.tensor_scalar(dst[:, :, 0:keys - 64], o[:, :, 0:keys - 64], QK ** -0.5, None, ALU.mult))
                        dve.wait_ge(M["dve_step"], steps[0])
                        gone(dve.tensor_scalar(dst[:, :, keys - 64:keys], o[:, :, keys - 64:keys], QK ** -0.5, tb("chunkmask"), ALU.mult, ALU.add))
                    dve.wait_ge(M["dve_emptied"], emptied(f"ms{1 if t == 0 else 5}"))
                    st(dve.tensor_reduce(small[:, 8 * t:8 * t + 8], mp[:, :, :], AX.X, ALU.max))
                    settle()
                    dve.tensor_scalar(small[:, 8 * t:8 * t + 8], small[:, 8 * t:8 * t + 8], -1.0, None, ALU.mult).then_inc(M["mla_neg"], 1)
                for t, mp in enumerate((mp0, mp1)):
                    dve.wait_ge(M["mla_exp"], 8 * (t + 1))
                    st(dve.reciprocal(small[:, 32 + 8 * t:40 + 8 * t], small[:, 16 + 8 * t:24 + 8 * t]))
                    settle()
                    dve.tensor_tensor(mp[:, :, :], mp[:, :, :], small[:, 32 + 8 * t:40 + 8 * t].unsqueeze(2).broadcast_to([P, MH, P * (t + 1)]),
                                      ALU.mult).then_inc(M["mla_p"], 1)
                dve.wait_ge(M["mla_rstd"], 2)
                for ct in range(4):
                    st(dve.scalar_tensor_tensor(uT[:, 4 + ct], mqT[:, ct], g_out[:, ct:ct + 1], mkT[:, ct], ALU.mult, ALU.mult))
                settle()
                dve.sem_inc(M["mixed"], 1)
                add_rows(dve, job, gone, "out", h, M)

                norm_rows(qT.rearrange("p a s -> p (a s)").rearrange("p (t c) -> p t c", t=T), h, 2)
                for n in range(4):
                    o = job(f"xs{n}")
                    st(dve.tensor_reduce(xsm[:, 2 * n:2 * n + 2], o[:, :].rearrange("p (k s) -> p k s", k=2), AX.X, ALU.max))
                    settle()
                    dve.tensor_scalar(xsm[:, 2 * n:2 * n + 2], xsm[:, 2 * n:2 * n + 2], -XD ** -0.5, None, ALU.mult).then_inc(M["x_max"], 1)
                for t in range(T):
                    dve.wait_ge(M["x_exp"], 4 * (t + 1))
                    st(dve.reciprocal(xsm[:, 16 + 4 * t:20 + 4 * t], xsm[:, 8 + 4 * t:12 + 4 * t]))
                    settle()
                    dve.tensor_tensor(pr[:, t], pr[:, t], xsm[:, 16 + 4 * t:20 + 4 * t].unsqueeze(2).broadcast_to([P, XH, S]), ALU.mult).then_inc(M["x_p"], 1)
                for n in range(4):
                    gone(dve.tensor_copy(oT[:, 2 * n:2 * n + 2].rearrange("p c s -> p (c s)"), job(f"xo{n}")[:, :]))
                add_rows(dve, job, gone, "xout", h, M)

                norm_rows(hn.rearrange("p t c k -> p t (c k)"), h, 3)
                dve.wait_ge(M["params"], 32)
                o = job("router")
                gone(dve.tensor_tensor(lg[:, :, :], o[:, 0:128].rearrange("p (t n) -> p t n", t=T)[:, :, 0:NG + NE],
                                       b_rout[:, :].unsqueeze(1).broadcast_to([P, T, NG + NE]), ALU.add))
                dve.wait_ge(M["dve_emptied"], emptied("router"))

                def seg(x, *shape):
                    n = int(np.prod(shape))
                    v = rt[:, x:x + n]
                    return v if len(shape) == 1 else v.rearrange("p (a b) -> p a b", a=shape[0])

                def one_hot(dst, x, top, n, tmp, low):
                    st(dve.tensor_reduce(top, x, AX.X, ALU.max))
                    settle()
                    bt = top.unsqueeze(2).broadcast_to([P, T, n])
                    st(dve.tensor_tensor(tmp, x, bt, ALU.is_equal))
                    st(dve.tensor_scalar(dst, tb("iota8")[:, 0:n].unsqueeze(1).broadcast_to([P, T, n]), -8.0, None, ALU.add))
                    settle()
                    st(dve.tensor_tensor(tmp, tmp, dst, ALU.mult))
                    settle()
                    st(dve.tensor_reduce(low, tmp, AX.X, ALU.min))
                    settle()
                    st(dve.tensor_tensor(dst, dst, low.unsqueeze(2).broadcast_to([P, T, n]), ALU.is_equal))
                    settle()

                oh_g, tmp4, top_g, low = seg(0, T, NG), seg(16, T, NG), seg(24, T), seg(26, T)
                gl = lg[:, :, 0:NG]
                one_hot(oh_g, gl, top_g, NG, tmp4, low)
                st(dve.tensor_tensor(seg(8, T, NG), gl, top_g.unsqueeze(2).broadcast_to([P, T, NG]), ALU.subtract))
                settle()
                dve.sem_inc(M["r_exp"], 1)
                picked = seg(160, T * NG, EG)
                for t in range(T):
                    st(dve.tensor_tensor(picked[:, t * NG:(t + 1) * NG], lg[:, t, NG:].rearrange("p (g e) -> p g e", g=NG),
                                         oh_g[:, t].unsqueeze(2).broadcast_to([P, NG, EG]), ALU.mult))
                settle()
                own = seg(32, T, EG)
                st(dve.tensor_reduce(own, picked.rearrange("p (t g) e -> p t e g", t=T), AX.X, ALU.add))
                settle()
                oh1, oh2, tmp8, top1, top2 = seg(48, T, EG), seg(64, T, EG), seg(80, T, EG), seg(28, T), seg(30, T)
                one_hot(oh1, own, top1, EG, tmp8, low)
                rest = seg(96, T, EG)
                st(dve.scalar_tensor_tensor(rest, oh1, -1e30, own, ALU.mult, ALU.add))
                settle()
                one_hot(oh2, rest, top2, EG, tmp8, low)
                st(dve.tensor_tensor(rt[:, 128:130], top2, top1, ALU.subtract))
                settle()
                dve.sem_inc(M["r_exp"], 1)
                dve.wait_ge(M["r_exp_e"], 1)
                st(dve.tensor_reduce(rt[:, 130:132], seg(8, T, NG), AX.X, ALU.add))
                dve.wait_ge(M["r_exp_e"], 2)
                st(dve.tensor_scalar(rt[:, 132:134], rt[:, 128:130], 1.0, None, ALU.add))
                settle()
                st(dve.tensor_tensor(rt[:, 134:136], rt[:, 130:132], rt[:, 132:134], ALU.mult))
                settle()
                w1, w2 = rt[:, 136:138], rt[:, 138:140]
                st(dve.reciprocal(w1, rt[:, 134:136]))
                settle()
                st(dve.tensor_tensor(w2, w1, rt[:, 128:130], ALU.mult))
                settle()
                both, cw = seg(96, T, EG), seg(112, T, EG)
                st(dve.tensor_tensor(both, oh1, oh2, ALU.add))
                st(dve.tensor_tensor(cw, oh1, w1.unsqueeze(2).broadcast_to([P, T, EG]), ALU.mult))
                st(dve.tensor_tensor(tmp8, oh2, w2.unsqueeze(2).broadcast_to([P, T, EG]), ALU.mult))
                settle()
                st(dve.tensor_tensor(cw, cw, tmp8, ALU.add))
                settle()
                for t in range(T):
                    ohb = oh_g[:, t].unsqueeze(2).broadcast_to([P, NG, EG])
                    for dst, src in ((chosen, both), (combine, cw)):
                        st(dve.tensor_tensor(dst[:, t].rearrange("p (g e) -> p g e", g=NG), ohb,
                                             src[:, t:t + 1].broadcast_to([P, NG, EG]), ALU.mult))
                settle()
                dve.sem_inc(M["r_chosen"], 1)
                o = job("places")
                st(dve.scalar_tensor_tensor(place.rearrange("p t e -> p (t e)"), o[:, 0:2 * NE], 1e6, chosen.rearrange("p t e -> p (t e)"), ALU.add, ALU.mult))
                gone(dve.tensor_reduce(rounds_f[:, :], o[:, 2 * NE:3 * NE], AX.X, ALU.max))
                settle()
                st(dve.tensor_scalar(place[:, :, :], place[:, :, :], 1e6, None, ALU.subtract))
                dve.wait_ge(M["dve_emptied"], emptied("places"))
                st(dve.tensor_tensor(rt[:, 0:8], rounds_f[:, 0:1].broadcast_to([P, 8]), tb("thresholds"), ALU.is_gt))
                settle()
                st(dve.tensor_reduce(rounds_f[:, :], rt[:, 0:8], AX.X, ALU.add))
                settle()
                dve.wait_ge(sp_took, lay + 1)
                dve.tensor_copy(rounds_i[:, :], rounds_f[:, :]).then_inc(M["rounds"], 1)
                dve.wait_ge(M["rounds"], 1)
                dve.sem_inc(sp_rounds, 1)
                dve.sem_inc(M["added"], 1)
                r = dve.value_load(rounds_i[0:1, 0:1], min_val=1, max_val=8)
                with dve.Fori(0, r) as rnd:
                    with dve.Fori(0, MOE_STEPS) as j:
                        step = rnd * MOE_STEPS + j
                        ne = QUADS_PER_STEP * QUAD
                        for t in range(T):
                            dve.tensor_tensor(sel[:, t], place[:, t, bass.ds(j * ne, ne)].unsqueeze(2).broadcast_to([P, ne, SLOTS]),
                                              tb("iota32").unsqueeze(1).broadcast_to([P, ne, SLOTS]), ALU.is_equal).then_inc(M["sel_written"], 1)
                        dve.wait_ge(M["sel_written"], step * 2 + 2)
                        for t in range(T):
                            i = dve.tensor_tensor(comb[:, t], sel[:, t], combine[:, t, bass.ds(j * ne, ne)].unsqueeze(2).broadcast_to([P, ne, SLOTS]), ALU.mult)
                            if t == T - 1:
                                i.then_inc(M["slots"], 1)
                        for g in range(QUADS_PER_STEP):
                            q = step * QUADS_PER_STEP + g
                            for half in range(2):
                                dve.wait_ge(M["m_gather"], q * 4 + (half + 1))
                                dve.tensor_tensor(xT[:, 4 * half:4 * half + 4], bank[half][:, :].rearrange("p (c s) -> p c s", c=4),
                                                  gains[:, 3, 4 * half:4 * half + 4].unsqueeze(2).broadcast_to([P, 4, P]), ALU.mult).then_inc(M["xt_ready"], 1)
                            dve.wait_ge(M["silu"], q + 1)
                            dve.wait_ge(M["m_up"], q * 4 + 4)
                            dve.tensor_tensor(hid[:, :], sg[:, :], bank[2 + g % 2][:, FE:2 * FE], ALU.mult).then_inc(M["hid_ready"], 1)
                            dve.wait_ge(M["m_down"], q * 2 + 2)
                            dve.tensor_copy(yy[:, 512:1024], bank[5][:, :]).then_inc(M["yv_ready"], 1)
                            for t in range(T):
                                for n in range(2):
                                    k = 2 * t + n
                                    dve.wait_ge(M["m_scatter"], q * 4 + (k + 1))
                                    dve.wait_ge(M["added"], q * 4 + (k + 1))
                                    hx = h[:, t, 512 * n:512 * n + 512]
                                    dve.tensor_tensor(hx, hx, bank[6 + n][:, :], ALU.add).then_inc(M["added"], 1)
                    dve.tensor_scalar(place[:, :, :], place[:, :, :], float(SLOTS), None, ALU.subtract).then_inc(M["places_moved"], 1)
                    dve.wait_ge(M["places_moved"], rnd + 1)
                dve.wait_ge(M["arrived"], 3)
                dve.sem_clear(per_layer_range)
                dve.sem_inc(released, 1)
            steps[0] = 0
            mean_square(1)
            refine(1)
            dve.wait_ge(M["params"], 16)
            for t in range(T):
                dve.scalar_tensor_tensor(h[:, t], h[:, t], rs[:, t:t + 1], frow[:, :], ALU.mult, ALU.mult).then_inc(M["normed"], 1)

        @block.gpsimd
        def _(pool):
            ring_at = pool.alloc_register("ring_at")
            pool.reg_mov(ring_at, 0)
            half = ROPE // 2
            rope = [0]

            def step(i):
                rope[0] += 1
                i.then_inc(rope_step, 1)
                pool.wait_ge(rope_step, rope[0])
            pool.wait_ge(tables_in, 16)
            pool.wait_ge(positions_in, 16)
            R = slice(64, 96)
            ang, kk, turns = mkT[R, 1], mkT[R, 2], mkT[R, 3]
            step(pool.tensor_copy(ang, sinT[R].bitcast(I32)))
            step(pool.tensor_scalar(ang, ang, tb("invfreq")[R], None, ALU.mult))
            TWO_PI = (6.28125, 0.0019340515136718750, 2 * np.pi - 6.28125 - 0.0019340515136718750)
            for dst, quarter in ((sinT[R], 0.0), (cosT[R], 0.25)):
                step(pool.tensor_scalar(kk, ang, 1.0 / (2 * np.pi), quarter, ALU.mult, ALU.add))
                step(pool.tensor_scalar(kk, kk, 12582912.0, None, ALU.add))
                step(pool.tensor_scalar(kk, kk, 12582912.0, None, ALU.subtract))
                src = ang
                for part in TWO_PI:
                    step(pool.tensor_scalar(turns, kk, -float(part), None, ALU.mult))
                    step(pool.tensor_tensor(dst, turns, src, ALU.add))
                    src = dst
                step(pool.tensor_scalar(dst, dst, float(np.pi / 2) if quarter else 0.0, 3.1415925, ALU.add, ALU.min))
                step(pool.tensor_scalar(dst, dst, -3.1415925, None, ALU.max))
            pool.sem_inc(angles, 1)
            pool.wait_ge(rotary, 2)
            pool.tensor_scalar(sinT[R], sinT[R], tb("sinsign")[R], None, ALU.mult).then_inc(rotary_ready, 1)
            pool.wait_ge(rotary_ready, 1)
            with pool.Fori(0, L) as lay:
                pool.wait_ge(M["act_emptied"], emptied("mix_xt0"))
                base = pool.snap(ring_at)
                for name in ("in_kv", "uq"):
                    n = UNIT_NUMBER[name]
                    slot = ring[n % RING]
                    pool.wait_ge(unit_in[n % RING], base + LOADED * (n // RING + 1))
                    pool.sem_inc(pool_saw, 1)
                    if name == "in_kv":
                        src = slot[:, 0:KC * 160].rearrange("p (c n) -> p c n", c=KC)[:, :, 128:160]
                        for k in range(2):
                            i = pool.tensor_copy(w_kps[:, :, k * half:(k + 1) * half], src[:, :, (1 - k) * half:(2 - k) * half])
                    else:
                        src = slot[:, 0:1536].rearrange("p (c h n) -> p c h n", c=2, h=MH)
                        for c in range(2):
                            for k in range(2):
                                i = pool.tensor_copy(w_uqs[:, c, :, k * half:(k + 1) * half], src[:, c, :, NOPE + (1 - k) * half:NOPE + (2 - k) * half])
                    i.then_inc(M["swapped"], 1)
                pool.wait_ge(M["rounds"], 1)
                r = pool.value_load(rounds_i[0:1, 0:1], min_val=1, max_val=8)
                pool.reg_add(ring_at, ring_at, LOADED * FIXED_UNITS // RING)
                with pool.Fori(0, r):
                    pool.reg_add(ring_at, ring_at, MOE_STEPS * LOADED * STEP_UNITS // RING)
                pool.sem_inc(M["arrived"], 1)
                pool.wait_ge(released, lay + 1)


def group_rstd_done(act, job, name, dst, n, M, tick, settle, tb, done):
    o = job(name)
    act.activation(dst, o[:, :], ACT.Ln, bias=tb("eps"), scale=1.0 / n).then_inc(M["act_emptied"], 1)
    act.wait_ge(M["act_emptied"], emptied(name))
    act.activation(dst, dst, ACT.Exp, scale=-0.5).then_inc(done, 1)


def add_rows(dve, job, gone, prefix, h, M):
    for n in range(2):
        for t in range(T):
            hx = h[:, t, 512 * n:512 * n + 512]
            gone(dve.tensor_tensor(hx, hx, job(f"{prefix}{2 * n + t}")[:, :], ALU.add))
    dve.wait_ge(M["dve_emptied"], emptied(f"{prefix}3"))


def pack_params(a):
    def chunks(x, n):
        return x.reshape(L, n, P).transpose(2, 0, 1)
    parts = [a[n].reshape(L, P, KC).transpose(1, 0, 2) for n in ("norm_mix", "norm_cross", "norm_mem", "norm_ffn")]
    parts.append(np.concatenate([a["hgrn_norm"]] * (P // HD), axis=1).reshape(L, P, 1).transpose(1, 0, 2))
    parts += [chunks(a["conv_norm"], 2), chunks(a["mla_q_norm"], 2), chunks(a["mla_kv_norm"], 1), chunks(a["mla_out_norm"], 4)]
    parts.append(a["conv_w"].reshape(L, 3, 2, P).transpose(3, 0, 1, 2).reshape(P, L, 6))
    parts.append(chunks(a["hgrn_lower_bounds"], 2))
    return np.concatenate(parts, axis=2)


def pack_router(a):
    w = np.concatenate([a["router_group_w"], a["router_expert_w"].transpose(0, 2, 1, 3).reshape(L, D, NE)], axis=2)
    b = np.concatenate([a["router_group_b"], a["router_expert_b"].reshape(L, NE)], axis=1)
    return w.reshape(L, P, KC * (NG + NE)), b


_INS = ["x", "mem", "positions", "w_in", "mla_w_uq", "mla_w_ukv", "w_out", "xa_wq", "xa_wk", "xa_wv", "xa_wo",
        "expert_w_gate", "expert_w_up", "expert_w_down", "final_norm"]


def kernel(**inputs):
    import numpy as _np
    import concourse.bacc as _bacc
    from concourse import mybir as _mybir
    from concourse.bass_utils import run_bass_kernel_spmd as _run

    nc = _bacc.Bacc("TRN2", target_bir_lowering=False, num_devices=1)
    arrays, aps = {}, {}
    tables, level_masks = shape_tables()
    given = {n: inputs[n] for n in _INS}
    small = {n: _np.asarray(x) for n, x in inputs.items() if n not in _INS}
    given["params"] = pack_params(small)
    given["router_w"], given["router_b"] = pack_router(small)
    given["tables"], given["level_masks"] = tables, level_masks
    for name, x in given.items():
        x = _np.ascontiguousarray(x)
        arrays[f"in_{name}"] = x
        aps[name] = nc.dram_tensor(f"in_{name}", x.shape, _mybir.dt.from_np(x.dtype), kind="ExternalInput").ap()
    out = nc.dram_tensor("out_rows", (1, S, D), _mybir.dt.float32, kind="ExternalOutput").ap()
    hybrid_trunk(nc, aps.pop("tables"), aps.pop("level_masks"), aps, out)
    r = _run(nc, [arrays], core_ids=[0])
    return r.results[0]["out_rows"]
```

```python
from contextlib import ExitStack

import numpy as np

import concourse.bass as bass
from concourse import mybir

F32 = mybir.dt.float32
I32 = mybir.dt.int32
U8 = mybir.dt.uint8
ALU = mybir.AluOpType
ACT = mybir.ActivationFunctionType
AX = mybir.AxisListType

P = 128
L = 2
S = 256
D = 1024
T = S // P
KC = D // P
CHUNK = 64
EPS = 1e-6
DIN = 2208
HD = 64
MH, NOPE, ROPE, MV = 8, 64, 32, 64
QK = NOPE + ROPE
XH, XD = 4, 256
NG, EG = 4, 8
NE = NG * EG
FE = 256
SLOTS = 32
QUAD = 4
RING = 6
UNIT = 4096
LEVELS = 5
UNIT_DMAS = 2
LOADED = 16 * UNIT_DMAS
UNITS = [("xk0", "xa_wk", 0, 256, "(p c)"), ("xk1", "xa_wk", 256, 512, "(p c)"), ("in_fq", "w_in", 0, 512, "(p c)"),
         ("in_i", "w_in", 512, 768, "(p c)"), ("in_g", "w_in", 768, 1024, "(p c)"), ("xk2", "xa_wk", 512, 768, "(p c)"),
         ("in_b", "w_in", 1024, 1280, "(p c)"), ("in_c", "w_in", 1280, 1536, "(p c)"),
         ("in_hq", "w_in", 1536, 2048, "(p c)"), ("in_kv", "w_in", 2048, DIN, "(p c)"),
         ("xk3", "xa_wk", 768, 1024, "(p c)"), ("uq", "mla_w_uq", 0, 768, None), ("ukv", "mla_w_ukv", 0, 1024, None),
         ("xv0", "xa_wv", 0, 512, "(p c)"), ("xv1", "xa_wv", 512, 1024, "(p c)"),
         ("out0", "w_out", 0, 512, "(c p)"), ("out1", "w_out", 512, 1024, "(c p)"),
         ("xq0", "xa_wq", 0, 512, "(p c)"), ("xq1", "xa_wq", 512, 1024, "(p c)"),
         ("xout0", "xa_wo", 0, 512, "(c p)"), ("xout1", "xa_wo", 512, 1024, "(c p)")]
UNIT_NUMBER = {unit[0]: n for n, unit in enumerate(UNITS)}
FIXED_UNITS = len(UNITS)
QUADS_PER_STEP = 4
UNITS_PER_QUAD = 6
STEP_UNITS = QUADS_PER_STEP * UNITS_PER_QUAD
EARLY = 3
EARLY_QUAD = 1
EARLY_FIRST = 3
STRETCH = FIXED_UNITS + STEP_UNITS - EARLY
assert STEP_UNITS % RING == 0 and STRETCH % RING == 0
MOE_STEPS = NE // QUAD // QUADS_PER_STEP

TABLES = {}
_at = 0
for _name, _w in [("ident", P), ("ones", P), ("blk64", P), ("before", P), ("restart", S),
                  ("low_numbers", NE), ("thresholds", 8), ("chunkmask", 1), ("invfreq", 1),
                  ("sinsign", 1), ("eps", 1)]:
    TABLES[_name] = (_at, _w)
    _at += _w
TABLE_W = _at

PARAMS = {}
_at = 0
for _name, _w in [("gains", 4 * KC), ("g_hgrn", 1), ("g_conv", 2), ("g_lat", 3), ("g_out", 4), ("w_conv", 6), ("lb_raw", 2)]:
    PARAMS[_name] = (_at, _w)
    _at += _w
PARAM_W = _at
LN_EXP_TABLES, SILU_TABLES = 6, 18


def shape_tables():
    t = np.zeros((P, TABLE_W), np.float32)
    i = np.arange(P)

    def put(name, value):
        a, w = TABLES[name]
        t[:, a:a + w] = value

    put("ident", np.eye(P))
    put("ones", 1.0)
    put("blk64", (i[:, None] // 64 == i[None] // 64))
    put("before", i[:, None] < i[None])
    put("restart", (np.arange(S) % CHUNK != 0)[None])
    put("low_numbers", np.arange(NE)[None] - NE)
    put("thresholds", SLOTS * np.arange(8)[None])
    put("chunkmask", np.where(i < CHUNK, -1e30, 0.0)[:, None])
    half = ROPE // 2
    freq = np.float32(10000.0) ** (-np.arange(half, dtype=np.float32) * np.float32(2.0) / np.float32(ROPE))
    put("invfreq", freq[i % half][:, None])
    put("sinsign", np.where(i % ROPE < half, -1.0, 1.0)[:, None])
    put("eps", EPS)
    m = np.zeros((P, LEVELS, P), np.float32)
    s, q = i[:, None], i[None]
    m[:, 0] = (s // 4 == q // 4) & (s <= q)
    for lv in range(1, LEVELS):
        b = 4 << lv
        m[:, lv] = (s // b == q // b) & (s % b < b // 2) & (q % b >= b // 2)
    return t, m.reshape(P, LEVELS * P)


JOBS = [("xk0", "A"), ("xk1", "A")] + [(f"mix_xt{n}", "V") for n in range(4)]
JOBS += [("f", "A"), ("q", "V"), ("i", "A"), ("g", "V"), ("xk2", "A"), ("lv0e", "V"), ("lv0o", "V"),
         ("b", "A"), ("lv1e", "V"), ("lv1o", "V"), ("c", "A"), ("lv2e", "V"), ("lv2o", "V"),
         ("hc", "V"), ("lv3e", "V"), ("lv3o", "V"), ("cq", "A"), ("lv4e", "V"), ("lv4o", "V"),
         ("kv", "A"), ("kvs", "V"), ("xk3", "A"), ("latss", "A"), ("ktok", "A"), ("u0", "V"), ("u1", "V"), ("convss", "A"),
         ("o_in", "A"), ("mq0", "A"), ("mq1", "A"), ("o_st", "V"), ("mq2", "A"), ("hgss", "A"), ("mq3", "A")]
JOBS += [(f"mqs{n}", "V") for n in range(4)]
JOBS += [(f"mk{n}", "A") for n in range(4)] + [("mv0", "A"), ("mv1", "A"), ("xv0", "A")]
JOBS += [(f"ms{n}", "V") for n in range(6)] + [("xv1", "A"), ("mt0", "A"), ("mt1", "A"), ("xv2", "A")]
JOBS += [(f"mt{n}", "A") for n in range(2, 6)]
JOBS += [("mo0", "A"), ("mo1", "A"), ("mss0", "A"), ("mss1", "A"), ("xv3", "A")]
JOBS += [("out0", "V"), ("out1", "V"), ("out2", "V"), ("cross_xt0", "V"), ("cross_xt1", "V"), ("out3", "V")]
JOBS += [("xq0", "A"), ("xq1", "A"), ("cross_xt2", "V"), ("cross_xt3", "V"), ("xs0", "A"), ("xs1", "A")]
JOBS += [("xq2", "A"), ("xq3", "A"), ("xt0", "A"), ("xt1", "A"), ("xs2", "A"), ("xs3", "A")]
JOBS += [("xo0", "V"), ("xo1", "V"), ("xout0", "V"), ("xt2", "A"), ("xt3", "A"), ("xo2", "V"), ("xo3", "V")]
JOBS += [("xout1", "V"), ("xout2", "V"), ("ffn_xt0", "V"), ("ffn_xt1", "V"), ("xout3", "V")]
JOBS += [("router0", "V"), ("ffn_xt2", "V"), ("ffn_xt3", "V"), ("router1", "V"), ("places", "V")]
INDEX = {name: n for n, (name, _) in enumerate(JOBS)}


def emptied(name):
    n = INDEX[name]
    return sum(c == JOBS[n][1] for _, c in JOBS[:n + 1])


def hybrid_trunk(nc, tables, level_masks, a, out):
    with ExitStack() as ctx:
        def sb(name, shape, dt=F32, stack=ctx):
            return stack.enter_context(nc.sbuf_tensor(name, shape, dt))

        def sem(name):
            return ctx.enter_context(nc.semaphore(name))

        ring = [sb(f"ring{n}", [P, UNIT]) for n in range(RING)]
        h = sb("h", [P, T, D])
        uT = sb("uT", [P, KC, S])
        tab = sb("tab", [P, TABLE_W])
        lvmask = sb("lvmask", [P, LEVELS, P], U8)
        states = sb("states", [P, 3, 2, P])
        memN = sb("memN", [P, KC, S])
        ptab = sb("ptab", [P, L, PARAM_W])
        par = sb("par", [P, PARAM_W])
        w_rout = sb("w_rout", [P, KC, NG + NE])
        b_rout = sb("b_rout", [P, NG + NE])
        cosT = sb("cosT", [P, S])
        sinT = sb("sinT", [P, S])

        def pm(name):
            x, w = PARAMS[name]
            return par[:, x:x + w]

        gains = pm("gains").rearrange("p (g c) -> p g c", g=4)
        g_hgrn, g_conv, g_lat, g_out = pm("g_hgrn"), pm("g_conv"), pm("g_lat"), pm("g_out")
        w_conv = pm("w_conv").rearrange("p (t c) -> p t c", t=3)
        lb_raw = ptab[:, :, PARAMS["lb_raw"][0]:PARAM_W]
        lb_tab = sb("lb_tab", [P, 2, L, 2])
        lb = sb("lb", [P, 2, 2])
        lb_tmp = sb("lb_tmp", [P, 4, 2])
        ss = sb("ss", [P, 4])
        ms = sb("ms", [P, 2])
        rs0 = sb("rs0", [P, 2])
        rs = sb("rs", [P, 2])
        nt = sb("nt", [P, 2])
        rounds_f = sb("rounds_f", [P, 1])
        rounds_i = sb("rounds_i", [P, 1], I32)

        def tb(name):
            x, w = TABLES[name]
            return tab[:, x:x + w]

        with ExitStack() as st:
            early = [sb(f"early{n}", [P, UNIT], F32, st) for n in (2, 1, 0)][::-1]
        kT = sb("kT", [P, KC, S])
        vv = sb("vv", [P, T, D])
        mT = sb("mT", [P, KC, S])
        EARLY_REST = EARLY * UNIT - 3 * KC * S

        with ExitStack() as st:
            mqT = sb("mqT", [P, MH, S], F32, st)
            mkT = sb("mkT", [P, MH, S], F32, st)
            mV = sb("mV", [P, T, MH * MV], F32, st)
            hg2 = sb("hg2", [P, 4, S], F32, st)
            qh, bcum = hg2[:, 0:2], hg2[:, 2:4]
            mpt0 = hg2.rearrange("p a (b s) -> p (a b) s", b=2)
            kh = sb("kh", [P, 2, S], F32, st)
            ih = sb("ih", [P, T, S], F32, st)
            gate = sb("gate", [P, 2, S], F32, st)
            small = sb("small", [P, 64], F32, st)
            with ExitStack() as s1:
                lat = sb("lat", [P, 3, S], F32, s1)
                w_uqs = sb("w_uqs", [P, 2, MH, ROPE], F32, s1)
                w_kps = sb("w_kps", [P, KC, ROPE], F32, s1)
                cb = sb("cb", [P, 2, S], F32, s1)
                cu = sb("cu", [P, 2, S], F32, s1)
                cy = sb("cy", [P, 2, S], F32, s1)
                dl = sb("dl", [P, 2, S], F32, s1)
                ql = sb("ql", [P, 2, S], F32, s1)
                kl = sb("kl", [P, 2, S], F32, s1)
                sacc = sb("sacc", [P, 2, T, 2, P], F32, s1)
            ktok = mqT[:, 4:6].rearrange("p t (c s) -> p t c s", c=2)
            with ExitStack() as s1:
                mp0 = sb("mp0", [P, MH, P], F32, s1)
                mp1 = sb("mp1", [P, MH, S], F32, s1)
                mpt1 = sb("mpt1", [P, 2, MH, P], F32, s1)
        with ExitStack() as st:
            sb("early_rest_cross", [P, EARLY_REST], F32, st)
            qT = sb("qT", [P, KC, S], F32, st)
            oT = qT
            pr = sb("pr", [P, T, XH, S], F32, st)
            pT = sb("pT", [P, T, XH, S], F32, st)
            xsm = sb("xsm", [P, 64], F32, st)
        with ExitStack() as st:
            sb("early_rest_experts", [P, EARLY_REST], F32, st)
            sel = sb("sel", [P, T, QUADS_PER_STEP * QUAD, SLOTS], F32, st)
            comb = sb("comb", [P, T, QUADS_PER_STEP * QUAD, SLOTS], F32, st)
            hn = sb("hn", [P, T, KC, P], F32, st)
            xT = sb("xT", [P, KC, P], F32, st)
            cT = sb("cT", [P, T, P], F32, st)
            sg = sb("sg", [P, FE], F32, st)
            hid = sb("hid", [P, FE], F32, st)
            hidT = sb("hidT", [P, 2, P], F32, st)
            yy = sb("yy", [P, D], F32, st)
            lg = yy[:, 0:T * (NG + NE)].rearrange("p (t n) -> p t n", t=T)
            combine = sb("combine", [P, T, NE], F32, st)
            chosen = sb("chosen", [P, T, NE], F32, st)
            place = sb("place", [P, T, NE], F32, st)
            rt = yy
        frow = kT.rearrange("p c s -> p (c s)")[:, 0:D]
        bank = [ctx.enter_context(nc.psum_tensor(f"bank{n}", [P, 512], F32)) for n in range(8)]

        per_layer = ["params", "pe_job", "act_emptied", "dve_emptied", "act_step", "dve_step", "sumsq",
                     "meansq", "rstd0", "normed", "par_ready", "sig_q", "sig_g", "fgate", "logf", "diff",
                     "expdiff", "levels_ready", "qk_state", "ktok_scaled", "state_ready", "scores_done",
                     "o_sum", "hg_sq", "hg_rstd", "conv_yb", "conv_sq", "conv_rstd", "lat_sq", "lat_rstd",
                     "lat_ready", "swapped", "mixed", "mla_k", "mla_q", "mla_neg", "mla_exp", "mla_p",
                     "mla_osq", "mla_rstd", "gained", "x_max", "x_exp", "x_p", "r_exp", "r_exp_e", "r_chosen",
                     "rounds", "slots", "places_moved", "m_gather", "m_up", "m_down", "m_scatter", "xt_ready",
                     "ct_ready", "silu", "hid_ready", "hidT_ready", "ya_ready", "yv_ready", "added",
                     "sel_written", "arrived"]
        M = {n: sem(n) for n in per_layer}
        nums = [M[n].num for n in per_layer]
        assert nums == list(range(nums[0], nums[0] + len(nums)))
        per_layer_range = range(nums[0], nums[-1] + 1)
        released = sem("released")
        unit_in = [sem(f"unit_in{n}") for n in range(RING)]
        early_in = [sem(f"early_in{n}") for n in range(EARLY)]
        unit_free = sem("unit_free")
        mem_in = [sem(f"mem_in{t}") for t in range(T)]
        x_in = sem("x_in")
        tables_in = sem("tables_in")
        params_in = sem("params_in")
        masks_in = sem("masks_in")
        positions_in = sem("positions_in")
        mem_sumsq = sem("mem_sumsq")
        mem_meansq = sem("mem_meansq")
        mem_step = sem("mem_step")
        mem_rstd = sem("mem_rstd")
        mem_normed = sem("mem_normed")
        mem_turned = sem("mem_turned")
        mem_gained = sem("mem_gained")
        mem_kept = sem("mem_kept")
        rope_step = sem("rope_step")
        angles = sem("angles")
        sine_angles = sem("sine_angles")
        rotary = sem("rotary")
        rotary_ready = sem("rotary_ready")
        lb_x = sem("lb_x")
        setup_done = sem("setup_done")
        sp_rounds = sem("sp_rounds")
        sp_took = sem("sp_took")
        sp_saw = sem("sp_saw")
        pool_saw = sem("pool_saw")
        dve_saw = sem("dve_saw")
        stored = sem("stored")

        def cols(w, n0, n1, rows="(p c)"):
            return w[:, :, n0:n1].rearrange(f"l {rows} n -> l p c n", p=P)

        gate_w = a["expert_w_gate"].rearrange("l e (p c) f -> (l e) p (c f)", p=P)
        up_w = a["expert_w_up"].rearrange("l e (p c) f -> (l e) p (c f)", p=P)
        down_w = a["expert_w_down"].rearrange("l e (c p) n -> (l e) p c n", p=P)

        block = ctx.enter_context(nc.Block())

        @block.sync
        def _(sp):
            issued = sp.alloc_register("issued")
            sp.reg_mov(issued, 0)
            for t in range(T):
                sp.dma_start(kT.rearrange("p c s -> p (c s)")[:, t * D:(t + 1) * D],
                             a["mem"].rearrange("b (t p) d -> p (b t) d", p=P)[:, t]).then_inc(mem_in[t], 16)
            sp.dma_start(tab[:, :], tables[:, :]).then_inc(tables_in, 16)
            sp.dma_start(h[:, :, :], a["x"].rearrange("b (t p) d -> p (b t) d", p=P)).then_inc(x_in, 16)
            sp.sem_inc(sp_took, 1)

            def unit(base, n, slot, first, second):
                sp.wait_ge(unit_free, base + (n + 1))
                for dst, src in (first, second):
                    sp.dma_start(dst, src).then_inc(unit_in[slot], 16)

            def column_unit(base, n, w, lay, n0, n1, rows="(p c)"):
                slot = n % RING
                v = ring[slot][:, 0:KC * (n1 - n0)].rearrange("p (c n) -> p c n", c=KC)
                src = cols(w, n0, n1, rows)
                hc = KC // 2
                unit(base, n, slot,
                     (v[:, 0:hc], src[bass.ds(lay, 1), :, 0:hc].rearrange("l p c n -> p (l c) n")),
                     (v[:, hc:KC], src[bass.ds(lay, 1), :, hc:KC].rearrange("l p c n -> p (l c) n")))

            def expert_unit(lay, j, g, n, v):
                e0 = lay * NE + (j * QUADS_PER_STEP + g) * QUAD
                if n < 4:
                    v = v.rearrange("p (w e x) -> p w e x", e=QUAD, w=2)
                    x = slice(n * 2 * FE, (n + 1) * 2 * FE)
                    return ((v[:, 0], gate_w[bass.ds(e0, QUAD), :, x].rearrange("e p x -> p e x")),
                            (v[:, 1], up_w[bass.ds(e0, QUAD), :, x].rearrange("e p x -> p e x")))
                v = v.rearrange("p (e c x) -> p e c x", e=QUAD, c=2)
                x = slice((n - 4) * 512, (n - 3) * 512)
                dn = down_w[bass.ds(e0, QUAD), :, :, x].rearrange("e p c x -> p e c x")
                return (v[:, 0:2], dn[:, 0:2]), (v[:, 2:4], dn[:, 2:4])

            def load_early(lay, n):
                for dst, src in expert_unit(lay, 0, EARLY_QUAD, EARLY_FIRST + n, early[n]):
                    sp.dma_start(dst, src).then_inc(early_in[n], 16)

            def step_units(base, lay, j):
                for u in range(STEP_UNITS):
                    unit(base, u, u % RING, *expert_unit(lay, j, u // UNITS_PER_QUAD, u % UNITS_PER_QUAD, ring[u % RING]))

            with sp.Fori(0, L) as lay:
                base = sp.snap(issued)
                for n, (name, w, n0, n1, rows) in enumerate(UNITS):
                    if rows:
                        column_unit(base, n, a[w], lay, n0, n1, rows)
                    else:
                        chunks = a[w].shape[1] // P
                        v = ring[n % RING][:, 0:chunks * n1].rearrange("p (c n) -> p c n", c=chunks)
                        src = a[w].rearrange("l (c p) n -> l p c n", p=P)
                        half = n1 // 2
                        unit(base, n, n % RING,
                             (v[:, :, 0:half], src[bass.ds(lay, 1), :, :, 0:half].rearrange("l p c n -> p (l c) n")),
                             (v[:, :, half:n1], src[bass.ds(lay, 1), :, :, half:n1].rearrange("l p c n -> p (l c) n")))
                in_ring = [k for k in range(STEP_UNITS) if k // UNITS_PER_QUAD != EARLY_QUAD or k % UNITS_PER_QUAD < EARLY_FIRST]
                for n, k in enumerate(in_ring, FIXED_UNITS):
                    sp.wait_ge(unit_free, base + (n + 1))
                    if n - RING == UNIT_NUMBER["out0"]:
                        load_early(lay, 0)
                        load_early(lay, 1)
                    if n - RING == UNIT_NUMBER["xout0"]:
                        load_early(lay, 2)
                    for dst, src in expert_unit(lay, 0, k // UNITS_PER_QUAD, k % UNITS_PER_QUAD, ring[n % RING]):
                        sp.dma_start(dst, src).then_inc(unit_in[n % RING], 16)
                sp.reg_add(issued, issued, STRETCH)
                with sp.Fori(1, MOE_STEPS) as j:
                    base_j = sp.snap(issued)
                    step_units(base_j, lay, j)
                    sp.reg_add(issued, issued, STEP_UNITS)
                sp.wait_ge(sp_rounds, lay + 1)
                sp.sem_inc(sp_saw, 1)
                r = sp.value_load(rounds_i[0:1, 0:1], min_val=1, max_val=8)
                sp.sem_inc(sp_took, 1)
                with sp.If(r > 1):
                    with sp.Fori(1, r):
                        with sp.Fori(0, MOE_STEPS) as j2:
                            base_j = sp.snap(issued)
                            step_units(base_j, lay, j2)
                            sp.reg_add(issued, issued, STEP_UNITS)
            sp.wait_ge(stored, 16 * 2 * T)

        @block.tensor
        def _(pe):
            ring_base = pe.alloc_register("ring_base")
            pe.reg_mov(ring_base, 0)
            pe.sem_inc(unit_free, RING)
            ident = tb("ident")

            def begin(name):
                n = INDEX[name]
                if n >= 8:
                    before, who = JOBS[n - 8]
                    pe.wait_ge(M["act_emptied"] if who == "A" else M["dve_emptied"], emptied(before))
                return bank[n % 8]

            def after(name):
                pe.wait_ge(M["act_emptied"] if JOBS[INDEX[name]][1] == "A" else M["dve_emptied"], emptied(name))

            def wait_unit(base, n):
                n = UNIT_NUMBER.get(n, n)
                pe.wait_ge(unit_in[n % RING], base + LOADED * (n // RING + 1))

            def transposes(prefix, src, t):
                pe.wait_ge(M["normed"], {"mix": 0, "cross": 2, "ffn": 4}[prefix] + t + 1)
                for n in range(2):
                    o = begin(f"{prefix}_xt{2 * t + n}")
                    for c in range(4):
                        mm = pe.transpose(o[:, c * P:c * P + P], src[:, t, 4 * n + c], ident)
                    mm.then_inc(M["pe_job"], 1)

            def channel_tile(o, w, c0, m, rhs, chunks=KC, row0=0):
                for c in range(chunks):
                    mm = pe.matmul(o[row0:row0 + m], w[:, c, c0:c0 + m], rhs[:, c], start=(c == 0), stop=(c == chunks - 1))
                return mm

            def two_tiles(name, w, c0, rhs):
                o = begin(name)
                for k in range(2):
                    mm = channel_tile(o[:, k * S:(k + 1) * S], w, c0 + k * P, P, rhs)
                mm.then_inc(M["pe_job"], 1)

            def unit_view(slot, n):
                return ring[slot][:, 0:KC * n].rearrange("p (c n) -> p c n", c=KC)

            def level(lv):
                pe.wait_ge(M["levels_ready"], lv + 1)
                for odd in range(2):
                    o = begin(f"lv{lv}{'eo'[odd]}")
                    lo = CHUNK * odd
                    for t in range(T):
                        for pair in range(2):
                            x = (t * 2 + pair) * P
                            mm = pe.matmul(o[:, x:x + P], kl[lo:lo + HD, pair, t * P:t * P + P],
                                           ql[lo:lo + HD, pair, t * P:t * P + P], start=True, stop=True)
                    mm.then_inc(M["pe_job"], 1)

            def block_sums(name, blk, sq, ready, count):
                pe.wait_ge(ready, count)
                pe.matmul(begin(name)[:, :], blk, sq.rearrange("p c s -> p (c s)"), start=True, stop=True).then_inc(M["pe_job"], 1)

            def slot_view(name):
                n = UNIT_NUMBER[name]
                return unit_view(n % RING, UNITS[n][3] - UNITS[n][2])

            def fill_values(n, base):
                unit = f"xv{n // 2}"
                if n % 2 == 0:
                    wait_unit(base, unit)
                o = begin(f"xv{n}")
                w, t = slot_view(unit), n % 2
                for c in range(KC):
                    mm = pe.matmul(o[:, :], mT[:, c, t * P:t * P + P], w[:, c], start=(c == 0), stop=(c == KC - 1))
                mm.then_inc(M["pe_job"], 1)

            def to_rows(prefix, lhs, base, t, n):
                if t == 0:
                    wait_unit(base, f"{prefix}{n}")
                w = slot_view(f"{prefix}{n}")
                o = begin(f"{prefix}{2 * t + n}")
                for c in range(KC):
                    mm = pe.matmul(o[:, :], lhs[:, c, t * P:t * P + P], w[:, c], start=(c == 0), stop=(c == KC - 1))
                mm.then_inc(M["pe_job"], 1)
            def free_unit(name):
                pe.wait_ge(M["pe_job"], INDEX[name] + 1)
                pe.sem_inc(unit_free, 1)

            def unit_memory(base, u, ahead, lay):
                if ahead is None:
                    wait_unit(base, u)
                    return ring[u % RING]
                pe.wait_ge(early_in[ahead], lay * LOADED + LOADED)
                return early[ahead]

            def quad(step, g, base, first_unit, lay=None):
                q = step * QUADS_PER_STEP + g
                t0, t1, gu, d0, d1, s0, s1 = bank[0], bank[1], bank[2 + g % 2], bank[4], bank[5], bank[6], bank[7]
                x = slice(g * QUAD, (g + 1) * QUAD)
                for half, o in enumerate((t0, t1)):
                    for c in range(4):
                        for t in range(T):
                            mm = pe.matmul(o[:, c * P:c * P + P], hn[:, t, half * 4 + c],
                                           sel[:, t, x].rearrange("p e s -> p (e s)"), start=(t == 0), stop=(t == T - 1))
                    mm.then_inc(M["m_gather"], 1)
                pe.wait_ge(M["xt_ready"], q * 2 + 1)
                if g == 0:
                    pe.wait_ge(M["slots"], step + 1)
                for t in range(T):
                    mm = pe.transpose(t0[:, t * P:t * P + P], comb[:, t, x].rearrange("p e s -> p (e s)"), ident)
                mm.then_inc(M["m_gather"], 1)
                pe.wait_ge(M["xt_ready"], q * 2 + 2)
                for n in range(4):
                    is_early = lay is not None and n >= EARLY_FIRST
                    u = first_unit + n
                    w = unit_memory(base, u, n - EARLY_FIRST if is_early else None, lay).rearrange("p (w e c f) -> p e w c f", e=QUAD, w=2, c=2)
                    for c in range(2):
                        for e in range(QUAD):
                            first, last = n == 0 and c == 0, n == 3 and c == 1
                            mm = pe.matmul(gu[32 * e:32 * e + 32, :], xT[:, 2 * n + c, 32 * e:32 * e + 32],
                                           w[:, e, :, c], start=first, stop=last, tile_position=(0, 32 * e))
                    mm.then_inc(M["m_up"], 1)
                    if not is_early:
                        pe.wait_ge(M["m_up"], q * 4 + (n + 1))
                        pe.sem_inc(unit_free, 1)
                pe.wait_ge(M["hid_ready"], q + 1)
                for c in range(2):
                    mm = pe.transpose(t1[:, c * P:c * P + P], hid[:, c * P:c * P + P], ident)
                mm.then_inc(M["m_gather"], 1)
                pe.wait_ge(M["hidT_ready"], q + 1)
                for n, o in enumerate((d0, d1)):
                    u = first_unit + 4 + n
                    w = unit_memory(base, u, None if lay is None else 4 + n - EARLY_FIRST, lay).rearrange("p (e c x) -> p e c x", e=QUAD, c=2)
                    for c in range(2):
                        for e in range(QUAD):
                            mm = pe.matmul(o[32 * e:32 * e + 32, :], hidT[:, c, 32 * e:32 * e + 32], w[:, e, c],
                                           start=(c == 0), stop=(c == 1), tile_position=(0, 32 * e))
                    mm.then_inc(M["m_down"], 1)
                    if lay is None:
                        pe.wait_ge(M["m_down"], q * 2 + (n + 1))
                        pe.sem_inc(unit_free, 1)
                pe.wait_ge(M["ct_ready"], q + 1)
                for t in range(T):
                    pe.wait_ge(M["added"], q * 4 + (2 * t + 1))
                    for n, o in enumerate((s0, s1)):
                        if t == 0:
                            pe.wait_ge(M["ya_ready"] if n == 0 else M["yv_ready"], q + 1)
                        pe.matmul(o[:, :], cT[:, t], yy[:, n * 512:n * 512 + 512], start=True, stop=True).then_inc(M["m_scatter"], 1)

            pe.wait_ge(tables_in, 16)
            pe.wait_ge(mem_normed, 1)
            rows = mqT.rearrange("p a s -> p (a s)").rearrange("p (t c k) -> p t c k", t=T, c=KC)
            for n in range(4):
                for c in range(2):
                    for t in range(T):
                        mm = pe.transpose(bank[n][:, c * S + t * P:c * S + t * P + P], rows[:, t, 2 * n + c], ident)
                mm.then_inc(mem_turned, 1)

            pe.wait_ge(mem_gained, 4)

            with pe.Fori(0, L) as lay:
                base = pe.snap(ring_base)
                pe.reg_add(ring_base, ring_base, LOADED * STRETCH // RING)
                wait_unit(base, "xk0")
                two_tiles("xk0", slot_view("xk0"), 0, mT)
                wait_unit(base, "xk1")
                two_tiles("xk1", slot_view("xk1"), 0, mT)
                free_unit("xk0")
                for t in range(T):
                    transposes("mix", mqT.rearrange("p a s -> p (a s)").rearrange("p (t c k) -> p t c k", t=T, c=KC), t)
                free_unit("xk1")
                after("mix_xt3")
                wait_unit(base, "in_fq")
                w = slot_view("in_fq")
                two_tiles("f", w, 256, uT)
                two_tiles("q", w, 0, uT)
                wait_unit(base, "in_i")
                w = slot_view("in_i")
                o = begin("i")
                for t in range(T):
                    for c in range(KC):
                        mm = pe.matmul(o[:, t * S:(t + 1) * S], uT[:, c, t * P:t * P + P], w[:, c], start=(c == 0), stop=(c == KC - 1))
                mm.then_inc(M["pe_job"], 1)
                free_unit("q")
                wait_unit(base, "in_g")
                two_tiles("g", slot_view("in_g"), 0, uT)
                free_unit("i")
                wait_unit(base, "xk2")
                two_tiles("xk2", slot_view("xk2"), 0, mT)
                free_unit("g")
                level(0)
                free_unit("xk2")
                wait_unit(base, "in_b")
                two_tiles("b", slot_view("in_b"), 0, uT)
                level(1)
                free_unit("b")
                wait_unit(base, "in_c")
                two_tiles("c", slot_view("in_c"), 0, uT)
                level(2)
                free_unit("c")
                wait_unit(base, "in_hq")
                w = slot_view("in_hq")
                two_tiles("hc", w, 0, uT)
                level(3)
                two_tiles("cq", w, 256, uT)
                level(4)
                free_unit("cq")
                wait_unit(base, "in_kv")
                w = slot_view("in_kv")
                o = begin("kv")
                channel_tile(o[:, 0:S], w, 0, P, uT)
                channel_tile(o[:, S:2 * S], w, 64, 96, uT).then_inc(M["pe_job"], 1)
                o = begin("kvs")
                pe.wait_ge(M["swapped"], 1)
                channel_tile(o[:, 0:S], w_kps, 0, ROPE, uT, row0=64).then_inc(M["pe_job"], 1)
                wait_unit(base, "xk3")
                two_tiles("xk3", slot_view("xk3"), 0, mT)
                free_unit("kvs")
                pe.wait_ge(M["lat_sq"], 1)
                o = begin("latss")
                sq = mqT.rearrange("p a s -> p (a s)")
                pe.matmul(o[:, 0:S], tb("ones"), sq[:, 0:S], start=True, stop=False)
                pe.matmul(o[:, 0:S], tb("ones"), sq[:, S:2 * S], start=False, stop=True)
                pe.matmul(o[:, S:2 * S], tb("ones"), sq[:, 2 * S:3 * S], start=True, stop=True).then_inc(M["pe_job"], 1)
                free_unit("xk3")
                pe.wait_ge(M["ktok_scaled"], 1)
                o = begin("ktok")
                for t in range(T):
                    for pair in range(2):
                        mm = pe.transpose(o[:, (t * 2 + pair) * P:(t * 2 + pair + 1) * P], kl[:, pair, t * P:t * P + P], ident)
                mm.then_inc(M["pe_job"], 1)
                after("ktok")
                o = begin("u0")
                for k, ch in enumerate((0, 2)):
                    for pair in range(2):
                        mm = pe.matmul(o[:, (2 * k + pair) * P:(2 * k + pair + 1) * P], ktok[0:64, ch // 2, pair],
                                       ih[0:64, ch // 2, pair * P:pair * P + P], start=True, stop=True)
                mm.then_inc(M["pe_job"], 1)
                o = begin("u1")
                for pair in range(2):
                    mm = pe.matmul(o[:, pair * P:pair * P + P], ktok[64:128, 0, pair],
                                   ih[64:128, 0, pair * P:pair * P + P], start=True, stop=True)
                mm.then_inc(M["pe_job"], 1)
                block_sums("convss", tb("blk64"), cu, M["conv_sq"], 1)
                pe.wait_ge(M["scores_done"], 1)
                o = begin("o_in")
                for pair in range(2):
                    for t in range(T):
                        for odd in range(2):
                            hx = (2 * pair + odd) * HD
                            mm = pe.matmul(o[64 * odd:64 * odd + 64, pair * S + t * P:pair * S + t * P + P],
                                           ih[:, t, hx:hx + HD], sacc[:, odd, t, pair], start=True, stop=True)
                mm.then_inc(M["pe_job"], 1)
                wait_unit(base, "uq")
                slot_q, slot_kv = UNIT_NUMBER["uq"] % RING, UNIT_NUMBER["ukv"] % RING
                wq = ring[slot_q][:, 0:1536].rearrange("p (c n) -> p c n", c=2)
                wkv = ring[slot_kv][:, 0:1024]
                pe.wait_ge(M["lat_ready"], 1)

                def latent_queries(n):
                    o = begin(f"mq{n}")
                    for k in range(2):
                        mm = channel_tile(o[:, k * S:(k + 1) * S], wq, (2 * n + k) * QK, QK, lat, chunks=2)
                    mm.then_inc(M["pe_job"], 1)
                latent_queries(0)
                latent_queries(1)
                pe.wait_ge(M["state_ready"], 1)
                o = begin("o_st")
                for pair in range(2):
                    for ch in range(1, 4):
                        mm = pe.matmul(o[:, pair * S + ch * CHUNK:pair * S + (ch + 1) * CHUNK], states[:, ch - 1, pair],
                                       ql[:, pair, ch * CHUNK:(ch + 1) * CHUNK], start=True, stop=True)
                mm.then_inc(M["pe_job"], 1)
                latent_queries(2)
                block_sums("hgss", tb("blk64"), kl, M["hg_sq"], 1)
                latent_queries(3)
                pe.wait_ge(M["swapped"], 2)
                for n in range(4):
                    o = begin(f"mqs{n}")
                    for k in range(2):
                        mm = channel_tile(o[:, k * S:(k + 1) * S], w_uqs.rearrange("p c h r -> p c (h r)"),
                                          (2 * n + k) * ROPE, ROPE, lat, chunks=2, row0=64)
                    mm.then_inc(M["pe_job"], 1)
                wait_unit(base, "ukv")
                for n in range(4):
                    o = begin(f"mk{n}")
                    for k in range(2):
                        hx = (2 * n + k) * (NOPE + MV)
                        mm = pe.matmul(o[0:NOPE, k * S:(k + 1) * S], wkv[:, hx:hx + NOPE], lat[:, 2], start=True, stop=True)
                    mm.then_inc(M["pe_job"], 1)
                free_unit("mqs3")
                for t in range(T):
                    pe.matmul(begin(f"mv{t}")[:, :], lat[:, 2, t * P:t * P + P],
                              wkv.rearrange("p (h n) -> p h n", h=MH)[:, :, NOPE:NOPE + MV], start=True, stop=True).then_inc(M["pe_job"], 1)
                fill_values(0, base)
                free_unit("mv1")
                after("mv1")
                pe.wait_ge(M["mla_k"], 1)
                pe.wait_ge(M["mla_q"], 1)
                for n in range(2):
                    o = begin(f"ms{n}")
                    for k in range(4):
                        mm = pe.matmul(o[:, k * P:(k + 1) * P], mqT[0:QK, 4 * n + k, 0:P], mkT[0:QK, 4 * n + k, 0:P], start=True, stop=True)
                    mm.then_inc(M["pe_job"], 1)
                for n in range(4):
                    o = begin(f"ms{2 + n}")
                    for k in range(2):
                        mm = pe.matmul(o[:, k * S:(k + 1) * S], mqT[0:QK, 2 * n + k, P:S], mkT[0:QK, 2 * n + k], start=True, stop=True)
                    mm.then_inc(M["pe_job"], 1)
                fill_values(1, base)
                pe.wait_ge(M["mla_p"], 1)
                for n in range(2):
                    o = begin(f"mt{n}")
                    for k in range(4):
                        mm = pe.transpose(o[:, k * P:(k + 1) * P], mp0[:, 4 * n + k], ident)
                    mm.then_inc(M["pe_job"], 1)
                fill_values(2, base)
                free_unit("xv1")
                pe.wait_ge(M["mla_p"], 2)
                for n in range(4):
                    o = begin(f"mt{2 + n}")
                    for k in range(4):
                        mm = pe.transpose(o[:, k * P:(k + 1) * P], mp1[:, 4 * (n % 2) + k, (n // 2) * P:(n // 2 + 1) * P], ident)
                    mm.then_inc(M["pe_job"], 1)
                after("mt5")
                for n in range(2):
                    o = begin(f"mo{n}")
                    for t in range(T):
                        for k in range(4):
                            hx = 4 * n + k
                            dst = o[64 * (k % 2):64 * (k % 2) + 64, (k // 2) * S + t * P:(k // 2) * S + (t + 1) * P]
                            for kt in range(t + 1):
                                mm = pe.matmul(dst, mV[:, kt, hx * MV:(hx + 1) * MV], mpt1[:, kt, hx] if t else mpt0[:, hx],
                                               start=(kt == 0), stop=(kt == t))
                    mm.then_inc(M["pe_job"], 1)
                for n in range(2):
                    block_sums(f"mss{n}", tb("blk64"), mqT[:, 4 + 2 * n:6 + 2 * n], M["mla_osq"], n + 1)
                fill_values(3, base)
                pe.wait_ge(M["mixed"], 3)
                rows = pr.rearrange("p t h s -> p t (h s)").rearrange("p t (c k) -> p t c k", c=KC)
                to_rows("out", uT, base, 0, 0)
                free_unit("xv3")
                to_rows("out", uT, base, 0, 1)
                to_rows("out", uT, base, 1, 0)
                transposes("cross", rows, 0)
                free_unit("out2")
                to_rows("out", uT, base, 1, 1)

                def queries(t):
                    for n in range(2):
                        if t == 0:
                            wait_unit(base, f"xq{n}")
                        w = slot_view(f"xq{n}")
                        o = begin(f"xq{2 * t + n}")
                        for k in range(4):
                            for c in range(KC):
                                mm = pe.matmul(o[:, k * P:(k + 1) * P], w[:, c, k * P:(k + 1) * P], uT[:, c, t * P:t * P + P],
                                               start=(c == 0), stop=(c == KC - 1))
                        mm.then_inc(M["pe_job"], 1)

                def scores(t):
                    for n in range(2):
                        after(f"xq{2 * t + n}")
                        o = begin(f"xs{2 * t + n}")
                        for k in range(2):
                            hx = 2 * n + k
                            for c in range(2):
                                mm = pe.matmul(o[:, k * S:(k + 1) * S], qT[:, 2 * hx + c, t * P:t * P + P], kT[:, 2 * hx + c],
                                               start=(c == 0), stop=(c == 1))
                        mm.then_inc(M["pe_job"], 1)

                def turn_probabilities(t):
                    pe.wait_ge(M["x_p"], t + 1)
                    for kt in range(T):
                        o = begin(f"xt{2 * t + kt}")
                        for hx in range(XH):
                            mm = pe.transpose(o[:, hx * P:(hx + 1) * P], pr[:, t, hx, kt * P:(kt + 1) * P], ident)
                        mm.then_inc(M["pe_job"], 1)

                def outputs(t):
                    after(f"xt{2 * t + 1}")
                    for n in range(2):
                        o = begin(f"xo{2 * t + n}")
                        for k in range(4):
                            ch = 4 * n + k
                            for kt in range(T):
                                mm = pe.matmul(o[:, k * P:(k + 1) * P], vv[:, kt, ch * P:(ch + 1) * P], pT[:, kt, ch // 2, t * P:t * P + P],
                                               start=(kt == 0), stop=(kt == 1))
                        mm.then_inc(M["pe_job"], 1)

                after("cross_xt1")
                queries(0)
                free_unit("out3")
                transposes("cross", rows, 1)
                scores(0)
                after("cross_xt3")
                queries(1)
                free_unit("xq2")
                turn_probabilities(0)
                free_unit("xq3")
                scores(1)
                outputs(0)
                after("xo1")
                to_rows("xout", oT, base, 0, 0)
                turn_probabilities(1)
                outputs(1)
                to_rows("xout", oT, base, 0, 1)
                after("xo3")
                to_rows("xout", oT, base, 1, 0)
                transposes("ffn", hn, 0)
                free_unit("xout2")
                to_rows("xout", oT, base, 1, 1)

                free_unit("xout3")
                pe.wait_ge(M["params"], 32)
                for t in range(T):
                    if t == 1:
                        transposes("ffn", hn, 1)
                    after(f"ffn_xt{2 * t + 1}")
                    o = begin(f"router{t}")
                    for c in range(KC):
                        mm = pe.matmul(o[:, 0:NG + NE], uT[:, c, t * P:t * P + P], w_rout[:, c], start=(c == 0), stop=(c == KC - 1))
                    mm.then_inc(M["pe_job"], 1)
                pe.wait_ge(M["r_chosen"], 1)
                o = begin("places")
                both = chosen.rearrange("p t e -> p (t e)")
                pe.matmul(o[:, 0:2 * NE], tb("before"), both, start=True, stop=True)
                pe.matmul(o[:, 2 * NE:4 * NE], tb("ones"), both, start=True, stop=True).then_inc(M["pe_job"], 1)

                after("places")
                pe.wait_ge(M["sel_written"], 2)
                for g in range(QUADS_PER_STEP):
                    quad(0, g, base, FIXED_UNITS + g * UNITS_PER_QUAD - (EARLY if g > EARLY_QUAD else 0), lay if g == EARLY_QUAD else None)
                pe.wait_ge(M["rounds"], 1)
                r = pe.value_load(rounds_i[0:1, 0:1], min_val=1, max_val=8)
                with pe.Fori(1, r * MOE_STEPS) as step:
                    base_j = pe.snap(ring_base)
                    pe.reg_add(ring_base, ring_base, LOADED * STEP_UNITS // RING)
                    pe.wait_ge(M["sel_written"], step * 2 + 2)
                    for g in range(QUADS_PER_STEP):
                        quad(step, g, base_j, g * UNITS_PER_QUAD)
                pe.sem_inc(M["arrived"], 1)
                pe.wait_ge(released, lay + 1)

        @block.scalar
        def _(act):
            steps = [0]

            def tick():
                steps[0] += 1
                return 1

            def settle():
                act.wait_ge(M["act_step"], steps[0])

            def job(name):
                act.wait_ge(M["pe_job"], INDEX[name] + 1)
                return bank[INDEX[name] % 8]

            def sum_squares(src, junk, t, ready=None):
                for n in range(2):
                    if ready:
                        act.wait_ge(M["dve_emptied"], emptied(f"{ready}{2 * t + n}"))
                    half = slice(n * D // 2, (n + 1) * D // 2)
                    act.activation(junk[:, half], src[:, t, half], ACT.Square, scale=D ** -0.5,
                                   accum_out=ss[:, 2 * t + n:2 * t + n + 1]).then_inc(M["sumsq"], 1)

            def first_rstd(k, t):
                act.wait_ge(M["meansq"], k + t + 1)
                act.activation(nt[:, t:t + 1], ms[:, t:t + 1], ACT.Ln).then_inc(M["act_step"], tick())
                settle()
                act.activation(rs0[:, t:t + 1], nt[:, t:t + 1], ACT.Exp, scale=-0.5).then_inc(M["rstd0"], 1)

            def copy_out(name, dst, src=None):
                o = job(name)
                act.activation(dst, o[:, :] if src is None else src(o), ACT.Copy).then_inc(M["act_emptied"], 1)

            def group_rstd(name, dst, n, done):
                o = job(name)
                act.activation(dst, o[:, :], ACT.Ln, bias=tb("eps"), scale=1.0 / n).then_inc(M["act_emptied"], 1)
                act.wait_ge(M["act_emptied"], emptied(name))
                act.activation(dst, dst, ACT.Exp, scale=-0.5).then_inc(done, 1)

            def load_tables(which):
                act.add_instruction(mybir.InstLoadActFuncSet(act_func_set_id=which, name=nc.get_next_instruction_name(), ins=[], outs=[]))

            flat = lambda x: x.rearrange("p c s -> p (c s)")
            act.dma_start(ptab[:, :, :], a["params"][:, :, :]).then_inc(params_in, 16)
            act.dma_start(sinT[64:96, :].bitcast(I32), a["positions"].broadcast_to([ROPE, S])).then_inc(positions_in, 16)
            act.dma_start(uT.rearrange("p c s -> p (c s)")[:, 0:LEVELS * P], level_masks[:, :]).then_inc(masks_in, 16)
            load_tables(LN_EXP_TABLES)
            act.wait_ge(lb_x, 1)
            act.activation(lb_tmp[:, 0:L], lb_tmp[:, 0:L], ACT.Exp).then_inc(lb_x, 1)
            mrow = kT.rearrange("p c s -> p (c s)").rearrange("p (t d) -> p t d", t=T)
            for t in range(T):
                act.wait_ge(mem_in[t], 16)
                act.activation(vv[:, t], mrow[:, t], ACT.Square, accum_out=ss[:, t:t + 1]).then_inc(mem_sumsq, 1)
            act.wait_ge(mem_meansq, 1)
            act.activation(nt[:, :], ms[:, :], ACT.Ln).then_inc(mem_step, 1)
            act.wait_ge(mem_step, 1)
            act.activation(rs0[:, :], nt[:, :], ACT.Exp, scale=-0.5).then_inc(mem_rstd, 1)
            for n in range(4):
                act.wait_ge(mem_turned, n + 1)
                act.activation(memN[:, 2 * n:2 * n + 2].rearrange("p c s -> p (c s)"), bank[n][:, :], ACT.Copy).then_inc(mem_kept, 1)
            act.wait_ge(angles, 1)
            act.activation(cosT[64:96], cosT[64:96], ACT.Sin).then_inc(rotary, 1)
            act.wait_ge(sine_angles, 1)
            act.activation(sinT[64:96], mkT[64:96, 7], ACT.Sin).then_inc(rotary, 1)
            act.wait_ge(x_in, 16)
            load_tables(LN_EXP_TABLES)
            with act.Fori(0, L) as lay:
                steps[0] = 0
                row = bass.ds(lay, 1)
                act.dma_start(w_rout.rearrange("p c n -> p (c n)"), a["router_w"][row].rearrange("l p n -> p (l n)")).then_inc(M["params"], 16)
                act.dma_start(b_rout[:, :], a["router_b"][row].broadcast_to([P, NG + NE])).then_inc(M["params"], 16)

                nrow = mqT.rearrange("p a s -> p (a s)").rearrange("p (t c) -> p t c", t=T)
                for t in range(T):
                    sum_squares(h, nrow[:, t], t)
                for t in range(T):
                    first_rstd(0, t)
                act.wait_ge(M["par_ready"], 1)
                for n in range(2):
                    copy_out(f"xk{n}", kT[:, 2 * n:2 * n + 2].rearrange("p c s -> p (c s)"))
                act.activation(flat(dl), job("f")[:, :], ACT.Exp, scale=-1.0).then_inc(M["act_emptied"], 1)
                act.activation(flat(ql), job("q")[:, :], ACT.Exp, scale=-1.0).then_inc(M["sig_q"], 1)
                copy_out("i", ih.rearrange("p t s -> p (t s)"))
                act.wait_ge(M["fgate"], 1)
                act.activation(flat(dl), flat(dl), ACT.Ln).then_inc(M["logf"], 1)

                def exp_level(lv):
                    act.wait_ge(M["diff"], lv + 1)
                    if lv == 0:
                        act.activation(flat(ql), flat(dl), ACT.Exp).then_inc(M["act_step"], tick())
                        act.activation(flat(kl), flat(dl), ACT.Exp, scale=-1.0).then_inc(M["expdiff"], 1)
                    else:
                        act.activation(flat(dl), flat(dl), ACT.Exp).then_inc(M["expdiff"], 1)
                exp_level(0)
                act.activation(flat(gate), job("g")[:, :], ACT.Exp, scale=-1.0).then_inc(M["sig_g"], 1)
                copy_out("xk2", kT[:, 4:6].rearrange("p c s -> p (c s)"))
                exp_level(1)
                copy_out("b", flat(cb))
                exp_level(2)
                copy_out("c", flat(cu))
                exp_level(3)
                exp_level(4)
                copy_out("cq", flat(lat[:, 0:2]))
                act.wait_ge(M["qk_state"], 1)
                act.wait_ge(M["pe_job"], INDEX["lv4o"] + 1)
                act.activation(flat(ql), flat(bcum), ACT.Exp).then_inc(M["act_step"], tick())
                act.activation(flat(kl), flat(dl), ACT.Exp).then_inc(M["expdiff"], 1)
                o = job("kv")
                act.activation(lat[:, 2], o[:, 0:S], ACT.Copy).then_inc(M["act_step"], tick())
                act.activation(mkT[64:96, 0], o[64:96, S:2 * S], ACT.Copy).then_inc(M["act_emptied"], 1)
                settle()
                act.wait_ge(M["act_emptied"], emptied("kv"))
                act.activation(mqT.rearrange("p a s -> p (a s)")[:, 0:3 * S], flat(lat), ACT.Square).then_inc(M["lat_sq"], 1)
                copy_out("xk3", kT[:, 6:8].rearrange("p c s -> p (c s)"))
                o = job("latss")
                rl = mkT[:, 4:6]
                act.activation(rl[:, 0], o[:, 0:S], ACT.Ln, bias=tb("eps"), scale=1.0 / 256).then_inc(M["act_step"], tick())
                act.activation(rl[:, 1], o[:, S:2 * S], ACT.Ln, bias=tb("eps"), scale=1.0 / 128).then_inc(M["act_emptied"], 1)
                settle()
                act.wait_ge(M["act_emptied"], emptied("latss"))
                act.activation(flat(rl), flat(rl), ACT.Exp, scale=-0.5).then_inc(M["lat_rstd"], 1)
                copy_out("ktok", ktok.rearrange("p t c s -> p (t c s)"))
                act.wait_ge(M["conv_yb"], 1)
                act.activation(flat(cu), flat(cy), ACT.Square).then_inc(M["conv_sq"], 1)
                group_rstd("convss", flat(cb), 64, M["conv_rstd"])
                copy_out("o_in", flat(dl))

                def keep_latent_queries(n):
                    copy_out(f"mq{n}", mqT[0:QK, 2 * n:2 * n + 2].rearrange("p c s -> p (c s)"), lambda o: o[0:QK, :])
                keep_latent_queries(0)
                keep_latent_queries(1)
                act.wait_ge(M["o_sum"], 1)
                act.activation(flat(kl), flat(dl), ACT.Square).then_inc(M["hg_sq"], 1)
                keep_latent_queries(2)
                group_rstd("hgss", flat(ql), 64, M["hg_rstd"])
                keep_latent_queries(3)
                for n in range(4):
                    copy_out(f"mk{n}", mkT[0:NOPE, 2 * n:2 * n + 2].rearrange("p c s -> p (c s)"), lambda o: o[0:NOPE, :])
                for t in range(T):
                    copy_out(f"mv{t}", mV[:, t])

                def keep_values(n):
                    copy_out(f"xv{n}", vv[:, n % 2, 512 * (n // 2):512 * (n // 2) + 512])
                keep_values(0)
                for t, mp in enumerate((mp0, mp1)):
                    act.wait_ge(M["mla_neg"], t + 1)
                    for k in range(MH):
                        x = 8 * t + k
                        act.activation(mp[:, k], mp[:, k], ACT.Exp, bias=small[:, x:x + 1],
                                       accum_out=small[:, 16 + x:17 + x]).then_inc(M["mla_exp"], 1)
                keep_values(1)
                for n in range(2):
                    copy_out(f"mt{n}", mpt0[:, 4 * n:4 * n + 4].rearrange("p c s -> p (c s)"))
                keep_values(2)
                for n in range(4):
                    copy_out(f"mt{2 + n}", mpt1[:, n // 2, 4 * (n % 2):4 * (n % 2) + 4].rearrange("p c s -> p (c s)"))
                for n in range(2):
                    copy_out(f"mo{n}", mqT[:, 2 * n:2 * n + 2].rearrange("p c s -> p (c s)"))
                for n in range(2):
                    act.wait_ge(M["act_emptied"], emptied(f"mo{n}"))
                    act.activation(mqT[:, 4 + 2 * n:6 + 2 * n], mqT[:, 2 * n:2 * n + 2], ACT.Square).then_inc(M["mla_osq"], 1)
                for n in range(2):
                    group_rstd(f"mss{n}", mkT[:, 2 * n:2 * n + 2].rearrange("p c s -> p (c s)"), 64, M["mla_rstd"])

                keep_values(3)
                for t in range(T):
                    sum_squares(h, pT[:, t].rearrange("p h s -> p (h s)"), t, "out")
                    first_rstd(2, t)

                def keep_queries(t):
                    for n in range(2):
                        copy_out(f"xq{2 * t + n}", qT[:, 4 * n:4 * n + 4, t * P:t * P + P], lambda o: o[:, :].rearrange("p (c s) -> p c s", c=4))

                def exponentials(t):
                    for n in range(2 * t, 2 * t + 2):
                        act.wait_ge(M["x_max"], n + 1)
                        o = job(f"xs{n}")
                        for k in range(2):
                            x = 2 * n + k
                            i = act.activation(pr[:, n // 2, 2 * (n % 2) + k], o[:, k * S:(k + 1) * S], ACT.Exp, bias=xsm[:, x:x + 1],
                                               scale=XD ** -0.5, accum_out=xsm[:, 8 + x:9 + x])
                            i.then_inc(M["x_exp"], 1)
                        act.wait_ge(M["x_exp"], 2 * n + 2)
                        act.sem_inc(M["act_emptied"], 1)

                def keep_turned(t):
                    for kt in range(T):
                        copy_out(f"xt{2 * t + kt}", pT[:, kt, :, t * P:(t + 1) * P], lambda o: o[:, :].rearrange("p (h s) -> p h s", h=XH))

                keep_queries(0)
                exponentials(0)
                keep_queries(1)
                keep_turned(0)
                exponentials(1)
                keep_turned(1)

                for t in range(T):
                    junk = uT[:, 0:4].rearrange("p c s -> p (c s)") if t == 0 else xT.rearrange("p c k -> p (c k)")
                    sum_squares(h, junk, t, "xout")
                    first_rstd(4, t)
                act.wait_ge(M["r_exp"], 1)
                act.activation(rt[:, 100:108], rt[:, 100:108], ACT.Exp).then_inc(M["r_exp_e"], 1)
                act.wait_ge(M["r_exp"], 2)
                act.activation(rt[:, 112:114], rt[:, 112:114], ACT.Exp).then_inc(M["r_exp_e"], 1)
                load_tables(SILU_TABLES)

                def quads(step):
                    for g in range(QUADS_PER_STEP):
                        q = step * QUADS_PER_STEP + g
                        act.wait_ge(M["m_gather"], q * 4 + 3)
                        act.activation(cT.rearrange("p t s -> p (t s)"), bank[0][:, 0:S], ACT.Copy).then_inc(M["ct_ready"], 1)
                        act.wait_ge(M["m_up"], q * 4 + 4)
                        act.activation(sg[:, :], bank[2 + g % 2][:, 0:FE], ACT.Silu).then_inc(M["silu"], 1)
                        act.wait_ge(M["m_gather"], q * 4 + 4)
                        act.activation(hidT.rearrange("p c s -> p (c s)"), bank[1][:, 0:S], ACT.Copy).then_inc(M["hidT_ready"], 1)
                        act.wait_ge(M["m_down"], q * 2 + 1)
                        act.activation(yy[:, 0:512], bank[4][:, :], ACT.Copy).then_inc(M["ya_ready"], 1)
                quads(0)
                act.wait_ge(M["rounds"], 1)
                r = act.value_load(rounds_i[0:1, 0:1], min_val=1, max_val=8)
                with act.Fori(1, r * MOE_STEPS) as step:
                    quads(step)
                load_tables(LN_EXP_TABLES)
                act.sem_inc(M["arrived"], 1)
                act.wait_ge(released, lay + 1)
            act.dma_start(frow[:, :], a["final_norm"].rearrange("(l d) -> l d", l=1).broadcast_to([P, D])).then_inc(M["params"], 16)
            steps[0] = 0
            for t in range(T):
                sum_squares(h, hn[:, t].rearrange("p c k -> p (c k)"), t)
            for t in range(T):
                first_rstd(0, t)
            for t in range(T):
                for n in range(2):
                    half = slice(n * D // 2, (n + 1) * D // 2)
                    act.wait_ge(M["normed"], 2 * t + n + 1)
                    act.dma_start(out.rearrange("b (t p) d -> p (b t) d", p=P)[:, t, half], h[:, t, half]).then_inc(stored, 16)

        @block.vector
        def _(dve):
            steps = [0]

            def tick():
                steps[0] += 1
                return 1

            def settle():
                dve.wait_ge(M["dve_step"], steps[0])

            def st(i):
                i.then_inc(M["dve_step"], tick())

            def job(name):
                dve.wait_ge(M["pe_job"], INDEX[name] + 1)
                return bank[INDEX[name] % 8]

            def gone(i):
                i.then_inc(M["dve_emptied"], 1)

            flat = lambda x: x.rearrange("p c s -> p (c s)")

            def mean_square(k, t):
                dve.wait_ge(M["sumsq"], 2 * (k + t + 1))
                dve.tensor_scalar(ms[:, t:t + 1], ss[:, 2 * t:2 * t + 1], ss[:, 2 * t + 1:2 * t + 2], EPS, ALU.add, ALU.add).then_inc(M["meansq"], 1)

            def refine(k, t):
                col = slice(t, t + 1)
                dve.wait_ge(M["rstd0"], k + t + 1)
                st(dve.tensor_tensor(nt[:, col], rs0[:, col], rs0[:, col], ALU.mult))
                settle()
                st(dve.tensor_tensor(nt[:, col], nt[:, col], ms[:, col], ALU.mult))
                settle()
                st(dve.tensor_scalar(nt[:, col], nt[:, col], -0.5, 1.5, ALU.mult, ALU.add))
                settle()
                st(dve.tensor_tensor(rs[:, col], rs0[:, col], nt[:, col], ALU.mult))
                settle()

            def norm_tile(dst, k, t):
                refine(k, t)
                dve.tensor_scalar(dst.rearrange("p (c k) -> p c k", c=KC), h[:, t].rearrange("p (k c) -> p c k", c=KC),
                                  rs[:, t:t + 1], None, ALU.mult).then_inc(M["normed"], 1)

            def keep_transposes(prefix, gain, t):
                for n in range(2):
                    o = job(f"{prefix}_xt{2 * t + n}")
                    gone(dve.tensor_tensor(uT[:, 4 * n:4 * n + 4, t * P:t * P + P], o[:, :].rearrange("p (c s) -> p c s", c=4),
                                           gains[:, gain, 4 * n:4 * n + 4].unsqueeze(2).broadcast_to([P, 4, P]), ALU.mult))

            def add_bank(prefix, t, n):
                hx = h[:, t, 512 * n:512 * n + 512]
                gone(dve.tensor_tensor(hx, hx, job(f"{prefix}{2 * t + n}")[:, :], ALU.add))

            def norm_and_add(prefix, rows, k, next_prefix, gain):
                mean_square(k, 0)
                norm_tile(rows[:, 0], k, 0)
                add_bank(prefix, 1, 0)
                keep_transposes(next_prefix, gain, 0)
                add_bank(prefix, 1, 1)
                mean_square(k, 1)
                norm_tile(rows[:, 1], k, 1)

            next_layer = dve.alloc_register("next_layer")
            half_at = dve.alloc_register("half_at")
            dve.wait_ge(params_in, 16)
            dve.tensor_tensor(lb_tmp[:, 2], lb_raw[:, 0], lb_raw[:, 1], ALU.max).then_inc(setup_done, 1)
            dve.wait_ge(setup_done, 1)
            for l in range(L):
                i = dve.tensor_tensor(lb_tmp[:, l], lb_raw[:, l], lb_tmp[:, 2], ALU.subtract)
                i.then_inc(setup_done, 1)
            dve.wait_ge(setup_done, 3)
            dve.sem_inc(lb_x, 1)
            dve.wait_ge(lb_x, 2)
            dve.tensor_tensor(lb_tmp[:, 2], lb_tmp[:, 0], lb_tmp[:, 1], ALU.add).then_inc(setup_done, 1)
            dve.wait_ge(setup_done, 4)
            dve.reciprocal(lb_tmp[:, 3], lb_tmp[:, 2]).then_inc(setup_done, 1)
            dve.wait_ge(setup_done, 5)
            for l in range(L):
                dve.tensor_tensor(lb_tmp[:, l], lb_tmp[:, l], lb_tmp[:, 3], ALU.mult).then_inc(setup_done, 1)
            dve.wait_ge(setup_done, 7)
            dve.tensor_tensor(lb_tab[:, 0, 0], lb_tmp[:, 0], lb_tmp[:, 0], ALU.subtract).then_inc(setup_done, 1)
            dve.tensor_tensor(lb_tmp[:, 2], lb_tmp[:, 0], lb_tmp[:, 1], ALU.add).then_inc(setup_done, 1)
            dve.wait_ge(setup_done, 9)
            dve.tensor_tensor(lb_tab[:, 0, 1], lb_tmp[:, 2], lb_tmp[:, 0], ALU.subtract).then_inc(setup_done, 1)
            dve.memset(states[:, :, :, :], 0.0).then_inc(setup_done, 1)
            dve.wait_ge(setup_done, 11)
            dve.tensor_scalar(lb_tab[:, 1], lb_tab[:, 0], -1.0, 1.0, ALU.mult, ALU.add).then_inc(setup_done, 1)
            dve.wait_ge(setup_done, 12)

            dve.wait_ge(mem_sumsq, 2)
            dve.tensor_scalar(ms[:, :], ss[:, 0:T], 1.0 / D, EPS, ALU.mult, ALU.add).then_inc(mem_meansq, 1)
            dve.wait_ge(mem_rstd, 1)
            dve.tensor_tensor(nt[:, :], rs0[:, :], rs0[:, :], ALU.mult).then_inc(setup_done, 1)
            dve.wait_ge(setup_done, 13)
            dve.tensor_tensor(nt[:, :], nt[:, :], ms[:, :], ALU.mult).then_inc(setup_done, 1)
            dve.wait_ge(setup_done, 14)
            dve.tensor_scalar(nt[:, :], nt[:, :], -0.5, 1.5, ALU.mult, ALU.add).then_inc(setup_done, 1)
            dve.wait_ge(setup_done, 15)
            dve.tensor_tensor(rs[:, :], rs0[:, :], nt[:, :], ALU.mult).then_inc(setup_done, 1)
            dve.wait_ge(setup_done, 16)
            mrow = kT.rearrange("p c s -> p (c s)").rearrange("p (t d) -> p t d", t=T)
            nrow = mqT.rearrange("p a s -> p (a s)").rearrange("p (t c) -> p t c", t=T)
            for t in range(T):
                i = dve.tensor_scalar(nrow[:, t].rearrange("p (c k) -> p c k", c=KC),
                                      mrow[:, t].rearrange("p (k c) -> p c k", c=KC), rs[:, t:t + 1], None, ALU.mult)
                i.then_inc(setup_done, 1)
            dve.wait_ge(setup_done, 18)
            dve.sem_inc(mem_normed, 1)
            dve.wait_ge(tables_in, 16)
            dve.wait_ge(masks_in, 16)
            dve.tensor_copy(lvmask.rearrange("p l s -> p (l s)"), uT.rearrange("p c s -> p (c s)")[:, 0:LEVELS * P]).then_inc(setup_done, 1)
            dve.wait_ge(setup_done, 19)
            for n in range(4):
                dve.wait_ge(mem_kept, n + 1)
                first_gain = ptab[:, 0, PARAMS["gains"][0] + 2 * KC + 2 * n:PARAMS["gains"][0] + 2 * KC + 2 * n + 2]
                dve.tensor_tensor(mT[:, 2 * n:2 * n + 2], memN[:, 2 * n:2 * n + 2],
                                  first_gain.unsqueeze(2).broadcast_to([P, 2, S]), ALU.mult).then_inc(mem_gained, 1)
            done = [19]

            def step(i):
                done[0] += 1
                i.then_inc(setup_done, 1)
                dve.wait_ge(setup_done, done[0])
            dve.wait_ge(positions_in, 16)
            R = slice(64, 96)
            reduced_angles(dve, step, cosT[R], 0.25, sinT[R].bitcast(I32), mkT[R, 1], mkT[R, 2], mkT[R, 3], tb("invfreq")[R])
            dve.sem_inc(angles, 1)
            dve.wait_ge(mem_kept, 4)
            dve.wait_ge(x_in, 16)

            with dve.Fori(0, L) as lay:
                steps[0] = 0
                dve.tensor_copy(par[:, :], ptab[:, bass.ds(lay, 1)].rearrange("p l n -> p (l n)")).then_inc(M["par_ready"], 1)
                dve.wait_ge(M["par_ready"], 1)
                st(dve.tensor_copy(lb[:, :, :], lb_tab[:, :, bass.ds(lay, 1), :].rearrange("p w l c -> p w (l c)")))
                settle()
                nrow = mqT.rearrange("p a s -> p (a s)").rearrange("p (t c) -> p t c", t=T)
                for t in range(T):
                    mean_square(0, t)
                for t in range(T):
                    norm_tile(nrow[:, t], 0, t)
                for t in range(T):
                    keep_transposes("mix", 0, t)
                R = slice(64, 96)

                def inverse_of_one_more(x):
                    st(dve.tensor_scalar(x, x, 1.0, 3e38, ALU.add, ALU.min))
                    settle()
                    st(dve.reciprocal(x, x))
                    settle()
                st(dve.memset(sacc[:, :, :, :, :], 0.0))
                dve.wait_ge(M["act_emptied"], emptied("f"))
                inverse_of_one_more(flat(dl))
                for ct in range(2):
                    st(dve.tensor_scalar(dl[:, ct], dl[:, ct], lb[:, 1, ct:ct + 1], lb[:, 0, ct:ct + 1], ALU.mult, ALU.add))
                settle()
                st(dve.tensor_scalar(flat(dl), flat(dl), 1e-6, 1.0, ALU.max, ALU.min))
                settle()
                dve.tensor_scalar(flat(kh), flat(dl), -1.0, 1.0, ALU.mult, ALU.add).then_inc(M["fgate"], 1)
                dve.wait_ge(M["sig_q"], 1)
                inverse_of_one_more(flat(ql))
                gone(dve.tensor_tensor(flat(qh), flat(ql), job("q")[:, :], ALU.mult))
                dve.wait_ge(M["logf"], 1)
                for ct in range(2):
                    st(dve.tensor_tensor_scan(bcum[:, ct], tb("restart"), dl[:, ct], 0.0, ALU.mult, ALU.add))
                settle()

                def differences(lv):
                    blk = 4 << lv
                    b4 = flat(bcum).rearrange("p (n k) -> p n k", k=blk)
                    d4 = flat(dl).rearrange("p (n k) -> p n k", k=blk)
                    ref = (blk - 1) if lv == 0 else blk // 2 - 1
                    r4 = b4[:, :, ref:ref + 1].broadcast_to([P, 2 * S // blk, blk])
                    if lv == 0:
                        dve.tensor_tensor(d4, b4, r4, ALU.subtract).then_inc(M["diff"], 1)
                    else:
                        st(dve.tensor_tensor(d4, b4, r4, ALU.subtract))
                        settle()
                        dve.scalar_tensor_tensor(flat(dl), flat(dl), -1.0, flat(dl), ALU.mult, ALU.min).then_inc(M["diff"], 1)

                def scale_level(lv):
                    dve.wait_ge(M["expdiff"], lv + 1)
                    if lv:
                        dve.wait_ge(M["pe_job"], INDEX[f"lv{lv - 1}o"] + 1)
                    else:
                        dve.wait_ge(M["act_step"], 2)
                    st(dve.tensor_tensor(flat(ql), flat(qh), flat(dl if lv else ql), ALU.mult))
                    settle()
                    dve.tensor_tensor(flat(kl), flat(kh), flat(dl if lv else kl), ALU.mult).then_inc(M["levels_ready"], 1)

                def keep_level(lv):
                    for odd in range(2):
                        o = job(f"lv{lv}{'eo'[odd]}")
                        gone(dve.copy_predicated(sacc[:, odd].rearrange("p t c s -> p (t c) s"),
                                                 lvmask[:, lv:lv + 1].broadcast_to([P, 4, P]),
                                                 o[:, :].rearrange("p (n s) -> p n s", n=4)))

                differences(0)
                scale_level(0)
                for lv in range(1, LEVELS):
                    dve.wait_ge(M["levels_ready"], lv)
                    differences(lv)
                    if lv == 1:
                        dve.wait_ge(M["sig_g"], 1)
                        inverse_of_one_more(flat(gate))
                        gone(dve.tensor_tensor(flat(gate), flat(gate), job("g")[:, :], ALU.mult))
                        dve.wait_ge(M["dve_emptied"], emptied("g"))
                    scale_level(lv)
                    keep_level(lv - 1)
                    if lv == 3:
                        dve.wait_ge(M["act_emptied"], emptied("c"))
                        gone(dve.tensor_tensor(flat(cu), flat(cu), job("hc")[:, :], ALU.mult))
                b4 = flat(bcum).rearrange("p (n k) -> p n k", k=CHUNK)
                dve.wait_ge(M["levels_ready"], LEVELS)
                st(dve.tensor_tensor(flat(dl).rearrange("p (n k) -> p n k", k=CHUNK),
                                     b4[:, :, CHUNK - 1:CHUNK].broadcast_to([P, 2 * S // CHUNK, CHUNK]), b4, ALU.subtract))
                settle()
                dve.sem_inc(M["qk_state"], 1)
                keep_level(4)
                dve.wait_ge(M["dve_emptied"], emptied("lv4o"))
                dve.sem_inc(M["scores_done"], 1)
                dve.wait_ge(M["expdiff"], 6)
                st(dve.tensor_copy(small[:, 48:56].rearrange("p (c n) -> p c n", c=2), ql[:, :, CHUNK - 1::CHUNK]))
                settle()
                st(dve.tensor_tensor(flat(kl), flat(kh), flat(kl), ALU.mult))
                settle()
                dve.sem_inc(M["ktok_scaled"], 1)
                st(dve.tensor_tensor(flat(ql), flat(qh), flat(ql), ALU.mult))
                dve.wait_ge(M["dve_emptied"], emptied("hc"))
                for ct in range(2):
                    st(dve.tensor_scalar(cy[:, ct], cu[:, ct], w_conv[:, 2, ct:ct + 1], None, ALU.mult))
                settle()
                for k in (1, 2):
                    for ct in range(2):
                        st(dve.scalar_tensor_tensor(cy[:, ct, k:], cu[:, ct, 0:S - k], w_conv[:, 2 - k, ct:ct + 1], cy[:, ct, k:], ALU.mult, ALU.add))
                    settle()
                dve.wait_ge(M["act_emptied"], emptied("b"))
                dve.tensor_tensor(flat(cy), flat(cy), flat(cb), ALU.mult).then_inc(M["conv_yb"], 1)
                o = job("kvs")
                dve.wait_ge(rotary_ready, 1)
                dve.wait_ge(M["act_emptied"], emptied("kv"))
                st(dve.tensor_tensor(mkT[R, 0], mkT[R, 0], cosT[R], ALU.mult))
                settle()
                gone(dve.tensor_tensor(mkT[R, 1], o[R, 0:S], sinT[R], ALU.mult))
                dve.wait_ge(M["dve_emptied"], emptied("kvs"))
                st(dve.tensor_tensor(mkT[R, 2], mkT[R, 0], mkT[R, 1], ALU.add))
                dve.wait_ge(M["lat_rstd"], 1)
                for c in range(3):
                    i = dve.scalar_tensor_tensor(lat[:, c], lat[:, c], g_lat[:, c:c + 1], mkT[:, 4 if c < 2 else 5], ALU.mult, ALU.mult)
                    st(i)
                settle()
                dve.sem_inc(M["lat_ready"], 1)
                for k in (0, 1):
                    st(dve.tensor_copy(mkT[R, k], mkT[R, 2]))
                st(dve.tensor_copy(mkT[R, 3:8], mkT[R, 2:3].broadcast_to([ROPE, 5, S])))
                settle()
                dve.sem_inc(M["mla_k"], 1)
                o0, o1 = job("u0"), job("u1")

                def diag(x, pair, odd):
                    return x[64 * odd:64 * odd + 64, pair * P + 64 * odd:pair * P + 64 * odd + 64]

                for odd in range(2):
                    for pair in range(2):
                        lo = slice(64 * odd, 64 * odd + 64)
                        st(dve.tensor_copy(states[lo, 0, pair, lo], diag(o0, pair, odd)))
                for ch, (o, off) in ((1, (o1, 0)), (2, (o0, 2))):
                    settle()
                    for odd in range(2):
                        for pair in range(2):
                            lo = slice(64 * odd, 64 * odd + 64)
                            st(dve.scalar_tensor_tensor(states[lo, ch, pair, lo], states[lo, ch - 1, pair, lo],
                                                        small[lo, 48 + 4 * pair + ch:49 + 4 * pair + ch], diag(o, pair + off, odd), ALU.mult, ALU.add))
                settle()
                dve.sem_inc(M["dve_emptied"], 2)
                dve.sem_inc(M["state_ready"], 1)
                dve.wait_ge(M["pe_job"], INDEX["kvs"] + 1)
                dve.wait_ge(M["conv_rstd"], 1)
                for ct in range(2):
                    st(dve.scalar_tensor_tensor(uT[:, 2 + ct], cy[:, ct], g_conv[:, ct:ct + 1], cb[:, ct], ALU.mult, ALU.mult))
                settle()
                dve.sem_inc(M["mixed"], 1)
                dve.wait_ge(M["act_emptied"], emptied("o_in"))
                o = job("o_st")
                dv = dl[:, :, CHUNK:S]
                gone(dve.tensor_tensor(dv, dv, o[:, :].rearrange("p (c s) -> p c s", c=2)[:, :, CHUNK:S], ALU.add))
                dve.wait_ge(M["dve_emptied"], emptied("o_st"))
                dve.sem_inc(M["o_sum"], 1)
                st(dve.scalar_tensor_tensor(flat(gate), flat(gate), g_hgrn[:, 0:1], flat(dl), ALU.mult, ALU.mult))
                settle()
                dve.wait_ge(M["hg_rstd"], 1)
                st(dve.tensor_tensor(flat(uT[:, 0:2]), flat(gate), flat(ql), ALU.mult))
                settle()
                dve.sem_inc(M["mixed"], 1)
                for n in range(4):
                    dve.wait_ge(M["act_emptied"], emptied(f"mq{n}"))
                    o = job(f"mqs{n}")
                    q = mqT[R, 2 * n:2 * n + 2]
                    tmp = dl[R]
                    st(dve.tensor_tensor(q, q, cosT[R].unsqueeze(1).broadcast_to([ROPE, 2, S]), ALU.mult))
                    gone(dve.tensor_tensor(tmp, o[R, :].rearrange("p (c s) -> p c s", c=2), sinT[R].unsqueeze(1).broadcast_to([ROPE, 2, S]), ALU.mult))
                    settle()
                    dve.wait_ge(M["dve_emptied"], emptied(f"mqs{n}"))
                    st(dve.tensor_tensor(q, q, tmp, ALU.add))
                    settle()
                dve.sem_inc(M["mla_q"], 1)
                for t, mp in enumerate((mp0, mp1)):
                    keys = P * (t + 1)
                    per = 4 if t == 0 else 2
                    for n in range(2 if t == 0 else 4):
                        o = job(f"ms{n if t == 0 else 2 + n}")[:, :].rearrange("p (k s) -> p k s", k=per)
                        dst = mp[:, n * per:(n + 1) * per]
                        st(dve.tensor_scalar(dst[:, :, 0:keys - 64], o[:, :, 0:keys - 64], QK ** -0.5, None, ALU.mult))
                        dve.wait_ge(M["dve_step"], steps[0])
                        gone(dve.tensor_scalar(dst[:, :, keys - 64:keys], o[:, :, keys - 64:keys], QK ** -0.5, tb("chunkmask"), ALU.mult, ALU.add))
                    dve.wait_ge(M["dve_emptied"], emptied(f"ms{1 if t == 0 else 5}"))
                    st(dve.tensor_reduce(small[:, 8 * t:8 * t + 8], mp[:, :, :], AX.X, ALU.max))
                    settle()
                    dve.tensor_scalar(small[:, 8 * t:8 * t + 8], small[:, 8 * t:8 * t + 8], -1.0, None, ALU.mult).then_inc(M["mla_neg"], 1)
                for t, mp in enumerate((mp0, mp1)):
                    dve.wait_ge(M["mla_exp"], 8 * (t + 1))
                    st(dve.reciprocal(small[:, 32 + 8 * t:40 + 8 * t], small[:, 16 + 8 * t:24 + 8 * t]))
                    settle()
                    dve.tensor_tensor(mp[:, :, :], mp[:, :, :], small[:, 32 + 8 * t:40 + 8 * t].unsqueeze(2).broadcast_to([P, MH, P * (t + 1)]),
                                      ALU.mult).then_inc(M["mla_p"], 1)
                dve.wait_ge(M["mla_rstd"], 2)
                for ct in range(4):
                    st(dve.scalar_tensor_tensor(uT[:, 4 + ct], mqT[:, ct], g_out[:, ct:ct + 1], mkT[:, ct], ALU.mult, ALU.mult))
                settle()
                dve.sem_inc(M["mixed"], 1)
                for n in range(2):
                    add_bank("out", 0, n)
                norm_and_add("out", pr.rearrange("p t h s -> p t (h s)"), 2, "cross", 1)
                keep_transposes("cross", 1, 1)

                def negative_maxima(t):
                    for n in range(2 * t, 2 * t + 2):
                        o = job(f"xs{n}")
                        st(dve.tensor_reduce(xsm[:, 2 * n:2 * n + 2], o[:, :].rearrange("p (k s) -> p k s", k=2), AX.X, ALU.max))
                        settle()
                        dve.tensor_scalar(xsm[:, 2 * n:2 * n + 2], xsm[:, 2 * n:2 * n + 2], -XD ** -0.5, None, ALU.mult).then_inc(M["x_max"], 1)

                def probabilities(t):
                    dve.wait_ge(M["x_exp"], 4 * (t + 1))
                    st(dve.reciprocal(xsm[:, 16 + 4 * t:20 + 4 * t], xsm[:, 8 + 4 * t:12 + 4 * t]))
                    settle()
                    dve.tensor_tensor(pr[:, t], pr[:, t], xsm[:, 16 + 4 * t:20 + 4 * t].unsqueeze(2).broadcast_to([P, XH, S]), ALU.mult).then_inc(M["x_p"], 1)

                def keep_outputs(t):
                    for n in range(2):
                        gone(dve.tensor_copy(oT[:, 4 * n:4 * n + 4, t * P:t * P + P], job(f"xo{2 * t + n}")[:, :].rearrange("p (c s) -> p c s", c=4)))

                negative_maxima(0)
                probabilities(0)
                negative_maxima(1)
                keep_outputs(0)
                probabilities(1)
                add_bank("xout", 0, 0)
                keep_outputs(1)
                add_bank("xout", 0, 1)
                norm_and_add("xout", hn.rearrange("p t c k -> p t (c k)"), 4, "ffn", 3)

                dve.wait_ge(M["params"], 32)
                for t in range(T):
                    o = job(f"router{t}")
                    gone(dve.tensor_tensor(lg[:, t], o[:, 0:NG + NE], b_rout[:, :], ALU.add))
                    if t == 0:
                        keep_transposes("ffn", 3, 1)
                dve.wait_ge(M["dve_emptied"], emptied("router1"))

                def seg(x, *shape):
                    n = int(np.prod(shape))
                    v = rt[:, x:x + n]
                    return v if len(shape) == 1 else v.rearrange("p (a b) -> p a b", a=shape[0])

                low_numbers = tb("low_numbers")
                top_g, low, eq_g, penalty, exp_g = seg(80, T), seg(82, T), seg(84, T, NG), seg(92, T, NG), seg(100, T, NG)
                top1, top2, gap = seg(108, T), seg(110, T), seg(112, T)
                eq, own, oh1, oh2, rest = (seg(128 + 64 * k, T, NE) for k in range(5))

                def first_largest(x, top, n, equal):
                    for t in range(T):
                        st(dve.scalar_tensor_tensor(equal[:, t], x[:, t], top[:, t:t + 1], low_numbers[:, 0:n], ALU.is_equal, ALU.mult))
                    settle()
                    st(dve.tensor_reduce(low, equal, AX.X, ALU.min))
                    settle()

                def one_hot(dst, x, top):
                    st(dve.tensor_reduce(top, x, AX.X, ALU.max))
                    settle()
                    first_largest(x, top, NE, eq)
                    for t in range(T):
                        st(dve.tensor_scalar(dst[:, t], low_numbers, low[:, t:t + 1], None, ALU.is_equal))
                    settle()

                gl = lg[:, :, 0:NG]
                st(dve.tensor_reduce(top_g, gl, AX.X, ALU.max))
                settle()
                st(dve.tensor_tensor(exp_g, gl, top_g.unsqueeze(2).broadcast_to([P, T, NG]), ALU.subtract))
                first_largest(gl, top_g, NG, eq_g)
                dve.sem_inc(M["r_exp"], 1)
                for t in range(T):
                    st(dve.tensor_scalar(penalty[:, t], low_numbers[:, 0:NG], low[:, t:t + 1], -1e30, ALU.not_equal, ALU.mult))
                settle()
                for t in range(T):
                    st(dve.tensor_tensor(own[:, t].rearrange("p (g e) -> p g e", g=NG), lg[:, t, NG:].rearrange("p (g e) -> p g e", g=NG),
                                         penalty[:, t].unsqueeze(2).broadcast_to([P, NG, EG]), ALU.add))
                settle()
                one_hot(oh1, own, top1)
                st(dve.scalar_tensor_tensor(rest, oh1, -1e30, own, ALU.mult, ALU.add))
                settle()
                one_hot(oh2, rest, top2)
                st(dve.tensor_tensor(chosen[:, :, :], oh1, oh2, ALU.add))
                st(dve.tensor_tensor(gap, top2, top1, ALU.subtract))
                settle()
                dve.sem_inc(M["r_chosen"], 1)
                dve.sem_inc(M["r_exp"], 1)
                outside = own
                st(dve.tensor_scalar(outside, chosen[:, :, :], -1.0, 1e6, ALU.add, ALU.mult))
                settle()
                st(dve.tensor_scalar(outside, outside, float(SLOTS), None, ALU.subtract))
                settle()
                o = job("places")
                counts = eq
                st(dve.tensor_copy(counts.rearrange("p t e -> p (t e)"), o[:, 2 * NE:4 * NE]))
                st(dve.tensor_tensor(place[:, 0], o[:, 0:NE], outside[:, 0], ALU.add))
                settle()
                st(dve.tensor_tensor(outside[:, 1], counts[:, 0], outside[:, 1], ALU.add))
                settle()
                gone(dve.tensor_tensor(place[:, 1], o[:, NE:2 * NE], outside[:, 1], ALU.add))
                st(dve.tensor_tensor(rest[:, 0], counts[:, 0], counts[:, 1], ALU.add))
                dve.wait_ge(M["dve_emptied"], emptied("places"))
                settle()
                dve.sem_inc(M["added"], 1)
                ne = QUADS_PER_STEP * QUAD

                def slot_matrices(step, first):
                    e = bass.ds(first, ne) if not isinstance(step, int) else slice(0, ne)
                    for t in range(T):
                        dve.tensor_tensor(sel[:, t], place[:, t, e].unsqueeze(2).broadcast_to([P, ne, SLOTS]),
                                          tb("low_numbers")[:, NE - SLOTS:NE].unsqueeze(1).broadcast_to([P, ne, SLOTS]), ALU.is_equal).then_inc(M["sel_written"], 1)

                def weighted_slots(step, first):
                    e = bass.ds(first, ne) if not isinstance(step, int) else slice(0, ne)
                    dve.wait_ge(M["sel_written"], step * 2 + 2)
                    for t in range(T):
                        i = dve.tensor_tensor(comb[:, t], sel[:, t], combine[:, t, e].unsqueeze(2).broadcast_to([P, ne, SLOTS]), ALU.mult)
                        if t == T - 1:
                            i.then_inc(M["slots"], 1)
                    dve.tensor_scalar(place[:, :, e], place[:, :, e], float(SLOTS), None, ALU.subtract).then_inc(M["places_moved"], 1)

                def quads(step):
                    for g in range(QUADS_PER_STEP):
                        q = step * QUADS_PER_STEP + g
                        for half in range(2):
                            dve.wait_ge(M["m_gather"], q * 4 + (half + 1))
                            dve.tensor_tensor(xT[:, 4 * half:4 * half + 4], bank[half][:, :].rearrange("p (c s) -> p c s", c=4),
                                              gains[:, 3, 4 * half:4 * half + 4].unsqueeze(2).broadcast_to([P, 4, P]), ALU.mult).then_inc(M["xt_ready"], 1)
                        dve.wait_ge(M["silu"], q + 1)
                        dve.wait_ge(M["m_up"], q * 4 + 4)
                        dve.tensor_tensor(hid[:, :], sg[:, :], bank[2 + g % 2][:, FE:2 * FE], ALU.mult).then_inc(M["hid_ready"], 1)
                        dve.wait_ge(M["m_down"], q * 2 + 2)
                        dve.tensor_copy(yy[:, 512:1024], bank[5][:, :]).then_inc(M["yv_ready"], 1)
                        for t in range(T):
                            for n in range(2):
                                k = 2 * t + n
                                dve.wait_ge(M["m_scatter"], q * 4 + (k + 1))
                                dve.wait_ge(M["added"], q * 4 + (k + 1))
                                hx = h[:, t, 512 * n:512 * n + 512]
                                dve.tensor_tensor(hx, hx, bank[6 + n][:, :], ALU.add).then_inc(M["added"], 1)

                slot_matrices(0, 0)
                sum_g, both, product, w1, w2 = seg(114, T), seg(116, T), seg(118, T), seg(120, T), seg(122, T)
                dve.wait_ge(M["r_exp_e"], 1)
                st(dve.tensor_reduce(sum_g, exp_g, AX.X, ALU.add))
                dve.wait_ge(M["r_exp_e"], 2)
                st(dve.tensor_scalar(both, gap, 1.0, None, ALU.add))
                settle()
                st(dve.tensor_tensor(product, sum_g, both, ALU.mult))
                settle()
                st(dve.reciprocal(w1, product))
                settle()
                st(dve.tensor_tensor(w2, w1, gap, ALU.mult))
                settle()
                for t in range(T):
                    st(dve.tensor_scalar(oh2[:, t], oh2[:, t], w2[:, t:t + 1], None, ALU.mult))
                settle()
                for t in range(T):
                    st(dve.scalar_tensor_tensor(combine[:, t], oh1[:, t], w1[:, t:t + 1], oh2[:, t], ALU.mult, ALU.add))
                settle()
                weighted_slots(0, 0)
                st(dve.tensor_reduce(rounds_f[:, :], rest[:, 0], AX.X, ALU.max))
                settle()
                dve.wait_ge(M["dve_emptied"], emptied("places"))
                st(dve.tensor_tensor(rt[:, 0:8], rounds_f[:, 0:1].broadcast_to([P, 8]), tb("thresholds"), ALU.is_gt))
                settle()
                st(dve.tensor_reduce(rounds_f[:, :], rt[:, 0:8], AX.X, ALU.add))
                settle()
                dve.wait_ge(sp_took, lay + 1)
                dve.tensor_copy(rounds_i[:, :], rounds_f[:, :]).then_inc(M["rounds"], 1)
                dve.wait_ge(M["rounds"], 1)
                dve.sem_inc(sp_rounds, 1)
                quads(0)
                dve.reg_add(next_layer, lay, 1)
                dve.reg_mod(next_layer, next_layer, L)
                coming = dve.snap(next_layer, min_val=0, max_val=L - 1)
                mem_gain = ptab[:, bass.ds(coming, 1), PARAMS["gains"][0] + 2 * KC:PARAMS["gains"][0] + 3 * KC]
                dve.tensor_tensor(mT[:, :, :], memN[:, :, :], mem_gain.rearrange("p l c -> p (l c)").unsqueeze(2).broadcast_to([P, KC, S]),
                                  ALU.mult).then_inc(M["gained"], 1)
                dve.wait_ge(M["gained"], 1)
                r = dve.value_load(rounds_i[0:1, 0:1], min_val=1, max_val=8)
                with dve.Fori(1, r * MOE_STEPS) as step:
                    dve.reg_mod(half_at, step, MOE_STEPS)
                    first = dve.snap(half_at, min_val=0, max_val=MOE_STEPS - 1) * ne
                    dve.wait_ge(M["places_moved"], step)
                    dve.sem_inc(dve_saw, 1)
                    slot_matrices(step, first)
                    weighted_slots(step, first)
                    quads(step)
                    dve.wait_ge(M["added"], step * (4 * QUADS_PER_STEP) + (4 * QUADS_PER_STEP + 1))
                    dve.sem_inc(dve_saw, 1)
                dve.wait_ge(M["arrived"], 3)
                dve.sem_clear(per_layer_range)
                dve.sem_inc(released, 1)
            steps[0] = 0
            for t in range(T):
                mean_square(0, t)
            dve.wait_ge(M["params"], 16)
            for t in range(T):
                refine(0, t)
                for n in range(2):
                    half = slice(n * D // 2, (n + 1) * D // 2)
                    dve.scalar_tensor_tensor(h[:, t, half], h[:, t, half], rs[:, t:t + 1], frow[:, half], ALU.mult, ALU.mult).then_inc(M["normed"], 1)

        @block.gpsimd
        def _(pool):
            ring_at = pool.alloc_register("ring_at")
            pool.reg_mov(ring_at, 0)
            half = ROPE // 2
            pool.wait_ge(tables_in, 16)
            pool.wait_ge(positions_in, 16)
            R = slice(64, 96)
            done = [0]

            def step(i):
                done[0] += 1
                i.then_inc(rope_step, 1)
                pool.wait_ge(rope_step, done[0])
            reduced_angles(pool, step, mkT[R, 7], 0.0, sinT[R].bitcast(I32), mkT[R, 4], mkT[R, 5], mkT[R, 6], tb("invfreq")[R])
            pool.sem_inc(sine_angles, 1)
            pool.wait_ge(rotary, 2)
            pool.tensor_scalar(sinT[R], sinT[R], tb("sinsign")[R], None, ALU.mult).then_inc(rotary_ready, 1)
            pool.wait_ge(rotary_ready, 1)
            with pool.Fori(0, L) as lay:
                base = pool.snap(ring_at)
                for name in ("in_kv", "uq"):
                    n = UNIT_NUMBER[name]
                    slot = ring[n % RING]
                    pool.wait_ge(unit_in[n % RING], base + LOADED * (n // RING + 1))
                    pool.sem_inc(pool_saw, 1)
                    if name == "in_kv":
                        src = slot[:, 0:KC * 160].rearrange("p (c n) -> p c n", c=KC)[:, :, 128:160]
                        for k in range(2):
                            i = pool.tensor_copy(w_kps[:, :, k * half:(k + 1) * half], src[:, :, (1 - k) * half:(2 - k) * half])
                    else:
                        src = slot[:, 0:1536].rearrange("p (c h n) -> p c h n", c=2, h=MH)
                        for c in range(2):
                            for k in range(2):
                                i = pool.tensor_copy(w_uqs[:, c, :, k * half:(k + 1) * half], src[:, c, :, NOPE + (1 - k) * half:NOPE + (2 - k) * half])
                    i.then_inc(M["swapped"], 1)
                pool.wait_ge(M["rounds"], 1)
                r = pool.value_load(rounds_i[0:1, 0:1], min_val=1, max_val=8)
                pool.reg_add(ring_at, ring_at, LOADED * STRETCH // RING)
                with pool.Fori(1, r * MOE_STEPS):
                    pool.reg_add(ring_at, ring_at, LOADED * STEP_UNITS // RING)
                pool.sem_inc(M["arrived"], 1)
                pool.wait_ge(released, lay + 1)


def reduced_angles(engine, step, dst, quarter, positions, angle, turns, part_of, frequency):
    step(engine.tensor_copy(angle, positions))
    step(engine.tensor_scalar(angle, angle, frequency, None, ALU.mult))
    step(engine.tensor_scalar(turns, angle, 1.0 / (2 * np.pi), quarter, ALU.mult, ALU.add))
    step(engine.tensor_scalar(turns, turns, 12582912.0, None, ALU.add))
    step(engine.tensor_scalar(turns, turns, 12582912.0, None, ALU.subtract))
    src = angle
    for part in (6.28125, 0.0019340515136718750, 2 * np.pi - 6.28125 - 0.0019340515136718750):
        step(engine.tensor_scalar(part_of, turns, -float(part), None, ALU.mult))
        step(engine.tensor_tensor(dst, part_of, src, ALU.add))
        src = dst
    step(engine.tensor_scalar(dst, dst, float(np.pi / 2) if quarter else 0.0, 3.1415925, ALU.add, ALU.min))
    step(engine.tensor_scalar(dst, dst, -3.1415925, None, ALU.max))


def pack_params(a):
    def chunks(x, n):
        return x.reshape(L, n, P).transpose(2, 0, 1)
    parts = [a[n].reshape(L, P, KC).transpose(1, 0, 2) for n in ("norm_mix", "norm_cross", "norm_mem", "norm_ffn")]
    parts.append(np.concatenate([a["hgrn_norm"]] * (P // HD), axis=1).reshape(L, P, 1).transpose(1, 0, 2))
    parts += [chunks(a["conv_norm"], 2), chunks(a["mla_q_norm"], 2), chunks(a["mla_kv_norm"], 1), chunks(a["mla_out_norm"], 4)]
    parts.append(a["conv_w"].reshape(L, 3, 2, P).transpose(3, 0, 1, 2).reshape(P, L, 6))
    parts.append(chunks(a["hgrn_lower_bounds"], 2))
    return np.concatenate(parts, axis=2)


def pack_router(a):
    w = np.concatenate([a["router_group_w"], a["router_expert_w"].transpose(0, 2, 1, 3).reshape(L, D, NE)], axis=2)
    b = np.concatenate([a["router_group_b"], a["router_expert_b"].reshape(L, NE)], axis=1)
    return w.reshape(L, P, KC * (NG + NE)), b


_INS = ["x", "mem", "positions", "w_in", "mla_w_uq", "mla_w_ukv", "w_out", "xa_wq", "xa_wk", "xa_wv", "xa_wo",
        "expert_w_gate", "expert_w_up", "expert_w_down", "final_norm"]


def kernel(**inputs):
    import numpy as _np
    import concourse.bacc as _bacc
    from concourse import mybir as _mybir
    from concourse.bass_utils import run_bass_kernel_spmd as _run

    nc = _bacc.Bacc("TRN2", target_bir_lowering=False, num_devices=1)
    arrays, aps = {}, {}
    tables, level_masks = shape_tables()
    given = {n: inputs[n] for n in _INS}
    small = {n: _np.asarray(x) for n, x in inputs.items() if n not in _INS}
    given["params"] = pack_params(small)
    given["router_w"], given["router_b"] = pack_router(small)
    given["tables"], given["level_masks"] = tables, level_masks
    for name, x in given.items():
        x = _np.ascontiguousarray(x)
        arrays[f"in_{name}"] = x
        aps[name] = nc.dram_tensor(f"in_{name}", x.shape, _mybir.dt.from_np(x.dtype), kind="ExternalInput").ap()
    out = nc.dram_tensor("out_rows", (1, S, D), _mybir.dt.float32, kind="ExternalOutput").ap()
    hybrid_trunk(nc, aps.pop("tables"), aps.pop("level_masks"), aps, out)
    r = _run(nc, [arrays], core_ids=[0])
    return r.results[0]["out_rows"]
```
